# Optimizing a Trainium2 kernel written in Bass

```python
import jax, jax.numpy as jnp
from jax import lax
import numpy as np
import math

D_MODEL = 1024
BATCH = 1
SEQ = 256
DEPTH = 2

HG_HEADS = 4
HG_KDIM = 128
HG_VDIM = 128
HG_CHUNK = 64
ATT_GROUPS = ((128, 1), (512, 4), (2048, 16))
N_GROUPS = 3
ATT_HEADS = 4
ATT_DIM = 128
ROPE_THETA = 500000.0
ROPE_DIM = ATT_DIM // 4
D_FF = 4 * D_MODEL
EPS = 1e-6

HG_QK_W = HG_HEADS * HG_KDIM
HG_V_W = HG_HEADS * HG_VDIM
ATT_W = ATT_HEADS * ATT_DIM
ATT_QKV_W = 3 * N_GROUPS * ATT_W
SPLITS = (HG_QK_W, HG_QK_W, HG_V_W, HG_V_W, ATT_QKV_W, D_MODEL, D_MODEL)
N_IN = HG_QK_W + HG_QK_W + HG_V_W + HG_V_W + ATT_QKV_W + D_MODEL + D_MODEL


def rms_norm(x, g):
    xf = x.astype(jnp.float32)
    y = xf * lax.rsqrt(jnp.mean(xf * xf, axis=-1, keepdims=True) + EPS)
    return (y * g.astype(jnp.float32)).astype(x.dtype)

def partial_rope(t, cos, sin):
    tf = t.astype(jnp.float32)
    c = cos[:, None, :]
    s = sin[:, None, :]
    half = ROPE_DIM // 2
    r1 = tf[..., :half]
    r2 = tf[..., half:ROPE_DIM]
    out = jnp.concatenate([r1 * c - r2 * s, r2 * c + r1 * s, tf[..., ROPE_DIM:]], axis=-1)
    return out.astype(t.dtype)

def hgrn2_chunked(q, log_f, k, v):
    B, S, H, K = q.shape
    V = v.shape[-1]
    C = HG_CHUNK
    nc = S // C

    def chunks(t):
        return t.reshape(B, nc, C, H, t.shape[-1]).swapaxes(0, 1)

    causal = jnp.tril(jnp.ones((C, C), dtype=bool))[None, :, :, None, None]

    def step(state, xs):
        qc, gc, kc, vc = xs
        b = jnp.cumsum(gc, axis=1)
        rel = jnp.where(causal, b[:, :, None] - b[:, None, :], -jnp.inf)
        attn = jnp.einsum('bthk,btshk,bshk->bhts', qc, jnp.exp(rel), kc)
        o = (jnp.einsum('bhts,bshv->bthv', attn, vc)
             + jnp.einsum('bthk,bhkv->bthv', qc * jnp.exp(b), state))
        b_last = b[:, -1]
        k_dec = kc * jnp.exp(b_last[:, None] - b)
        state = state * jnp.exp(b_last)[..., None] + jnp.einsum('bshk,bshv->bhkv', k_dec, vc)
        return state, o

    state0 = jnp.zeros((B, H, K, V), jnp.float32)
    _, o = lax.scan(step, state0, (chunks(q), chunks(log_f), chunks(k), chunks(v)))
    return o.swapaxes(0, 1).reshape(B, S, H, V)

def dilated_window_attention(q, k, v, window, dilation):
    B, S, H, Dh = q.shape
    L = window // dilation
    period = dilation * L
    Sp = -(-S // period) * period
    M = Sp // dilation
    nb = M // L
    pad = Sp - S

    def to_blocks(t):
        t = jnp.pad(t, ((0, 0), (0, pad), (0, 0), (0, 0)))
        t = t.reshape(B, M, dilation, H, Dh)
        t = t.transpose(0, 2, 3, 1, 4)
        return t.reshape(B, dilation, H, nb, L, Dh)

    def with_prev(t):
        prev = jnp.pad(t, ((0, 0), (0, 0), (0, 0), (1, 0), (0, 0), (0, 0)))[:, :, :, :-1]
        return jnp.concatenate([prev, t], axis=4)

    qb = to_blocks(q).astype(jnp.float32)
    kw = with_prev(to_blocks(k)).astype(jnp.float32)
    vw = with_prev(to_blocks(v)).astype(jnp.float32)

    scores = jnp.einsum('bzhnqd,bzhnkd->bzhnqk', qb, kw) * (Dh ** -0.5)
    i = jnp.arange(L)[:, None]
    j = jnp.arange(2 * L)[None, :]
    delta = L + i - j
    band = (delta >= 0) & (delta <= L)
    n = jnp.arange(nb)[:, None, None]
    mask = band[None] & ((n > 0) | (j[None] >= L))
    scores = jnp.where(mask, scores, -jnp.inf)
    m = jnp.max(scores, axis=-1, keepdims=True)
    p = jnp.exp(scores - m)
    den = jnp.sum(p, axis=-1, keepdims=True)
    o = jnp.einsum('bzhnqk,bzhnkd->bzhnqd', p, vw) / den
    lse = (m + jnp.log(den))[..., 0]

    o = o.reshape(B, dilation, H, M, Dh).transpose(0, 3, 1, 2, 4).reshape(B, Sp, H, Dh)[:, :S]
    lse = lse.reshape(B, dilation, H, M).transpose(0, 3, 1, 2).reshape(B, Sp, H)[:, :S]
    return o, lse

def first_inputs(seed: int = 0) -> dict:
    key = jax.random.key(seed)
    ks = jax.random.split(key, 13)
    f32 = jnp.float32
    nrm = lambda k, shape, scale: jax.random.normal(k, shape, f32) * scale
    return {
        "x": nrm(ks[0], (BATCH, SEQ, D_MODEL), 1.0),
        "norm1_g": 1.0 + nrm(ks[1], (DEPTH, D_MODEL), 0.02),
        "w_in": nrm(ks[2], (DEPTH, D_MODEL, N_IN), D_MODEL ** -0.5),
        "hg_lower_bounds": nrm(ks[3], (DEPTH, HG_QK_W), 1.0),
        "hg_norm_g": 1.0 + nrm(ks[4], (DEPTH, HG_V_W), 0.02),
        "w_branch_a": nrm(ks[5], (DEPTH, HG_V_W, D_MODEL), HG_V_W ** -0.5),
        "w_branch_b": nrm(ks[6], (DEPTH, ATT_W, D_MODEL), ATT_W ** -0.5),
        "w_out": nrm(ks[7], (DEPTH, D_MODEL, D_MODEL), D_MODEL ** -0.5),
        "norm2_g": 1.0 + nrm(ks[8], (DEPTH, D_MODEL), 0.02),
        "w_up": nrm(ks[9], (DEPTH, D_MODEL, D_FF), D_MODEL ** -0.5),
        "w_down": nrm(ks[10], (DEPTH, D_FF, D_MODEL), D_FF ** -0.5),
        "final_norm_g": 1.0 + nrm(ks[11], (D_MODEL,), 0.02),
    }

def first_block(x, norm1_g, w_in, hg_lower_bounds, hg_norm_g, w_branch_a, w_branch_b,
              w_out, norm2_g, w_up, w_down, final_norm_g):
    B, S, _ = x.shape
    f32 = jnp.float32
    split_idx = [int(c) for c in np.cumsum(SPLITS)[:-1]]

    pos = jnp.arange(S, dtype=f32)
    inv_freq = ROPE_THETA ** (-jnp.arange(0, ROPE_DIM, 2, dtype=f32) / ROPE_DIM)
    ang = pos[:, None] * inv_freq[None, :]
    cos, sin = jnp.cos(ang), jnp.sin(ang)

    lb_all = jnp.cumsum(jax.nn.softmax(hg_lower_bounds.astype(f32), axis=0), axis=0)
    lb_all = lb_all - lb_all[0:1]

    for l in range(DEPTH):
        h = rms_norm(x, norm1_g[l])
        z = h @ w_in[l]
        zq, zf, zi, zg, zatt, za, zb = jnp.split(z, split_idx, axis=-1)

        q_hg = jax.nn.silu(zq.astype(f32)).reshape(B, S, HG_HEADS, HG_KDIM)
        lb = lb_all[l]
        log_f = jnp.logaddexp(jnp.log(lb), jnp.log1p(-lb) + jax.nn.log_sigmoid(zf.astype(f32)))
        log_f = log_f.reshape(B, S, HG_HEADS, HG_KDIM)
        k_hg = -jnp.expm1(log_f)
        v_hg = zi.astype(f32).reshape(B, S, HG_HEADS, HG_VDIM)
        o_hg = hgrn2_chunked(q_hg, log_f, k_hg, v_hg)
        o_hg = rms_norm(o_hg, hg_norm_g[l].reshape(HG_HEADS, HG_VDIM))
        o_hg = o_hg * jax.nn.sigmoid(zg.astype(f32)).reshape(B, S, HG_HEADS, HG_VDIM)
        o_hg = o_hg.reshape(B, S, HG_V_W).astype(x.dtype)

        qkv = zatt.reshape(B, S, 3, N_GROUPS, ATT_HEADS, ATT_DIM)
        outs, lses = [], []
        for g, (window, dilation) in enumerate(ATT_GROUPS):
            qg = partial_rope(qkv[:, :, 0, g], cos, sin)
            kg = partial_rope(qkv[:, :, 1, g], cos, sin)
            vg = qkv[:, :, 2, g]
            o_g, lse_g = dilated_window_attention(qg, kg, vg, window, dilation)
            outs.append(o_g)
            lses.append(lse_g)
        w_grp = jax.nn.softmax(jnp.stack(lses, axis=0), axis=0)
        o_att = jnp.sum(w_grp[..., None] * jnp.stack(outs, axis=0), axis=0)
        o_att = o_att.reshape(B, S, ATT_W).astype(x.dtype)

        y = (jax.nn.sigmoid(za) * (o_hg @ w_branch_a[l])
             + jax.nn.sigmoid(zb) * (o_att @ w_branch_b[l]))
        x = x + y @ w_out[l]

        h2 = rms_norm(x, norm2_g[l])
        x = x + jnp.square(jax.nn.relu(h2 @ w_up[l])) @ w_down[l]

    return rms_norm(x, final_norm_g)


PLE_DIM = 256
HEAD_DIM = 64
DIFF_HEADS = 4
DIFF_QK = 2 * HEAD_DIM
DIFF_V = 2 * HEAD_DIM
FOX_HEADS = 4
FOX_DIM = HEAD_DIM
RET_HEADS = 4
RET_DIM = HEAD_DIM
WA = DIFF_HEADS * DIFF_V
WB = FOX_HEADS * FOX_DIM
WC = RET_HEADS * RET_DIM
MIX_WIDTH = WA + WB + WC
IN_SIZES = (DIFF_HEADS * DIFF_QK, DIFF_HEADS * DIFF_QK, WA, WB, WB, WB, FOX_HEADS, WC, WC, WC, WC)
IN_COLS = sum(IN_SIZES)
Q_BLOCK = 128
RET_CHUNK = 128
RET_THETA = 10000.0
D_FF_DENSE = 2816
N_EXPERTS = 8
TOP_K = 2
D_FF_EXPERT = 3584
N_DENSE = (DEPTH + 1) // 2
N_MOE = DEPTH // 2
NEG_INF = -1e30


def rmsnorm(x, g):
    xf = x.astype(jnp.float32)
    y = xf * lax.rsqrt(jnp.mean(xf * xf, axis=-1, keepdims=True) + EPS)
    return (y * g.astype(jnp.float32)).astype(x.dtype)

def head_groupnorm(x):
    xf = x.astype(jnp.float32)
    mu = jnp.mean(xf, axis=-1, keepdims=True)
    var = jnp.mean(jnp.square(xf - mu), axis=-1, keepdims=True)
    return ((xf - mu) * lax.rsqrt(var + EPS)).astype(x.dtype)

def split_heads(t, n_heads):
    B, S, _ = t.shape
    return t.reshape(B, S, n_heads, -1).transpose(0, 2, 1, 3)

def merge_heads(t):
    B, H, S, D = t.shape
    return t.transpose(0, 2, 1, 3).reshape(B, S, H * D)

def rotary(x):
    S, D = x.shape[2], x.shape[3]
    half = D // 2
    inv = RET_THETA ** (-jnp.arange(half, dtype=jnp.float32) / half)
    ang = jnp.arange(S, dtype=jnp.float32)[:, None] * inv[None, :]
    cos, sin = jnp.cos(ang).astype(x.dtype), jnp.sin(ang).astype(x.dtype)
    x1, x2 = x[..., :half], x[..., half:]
    return jnp.concatenate([x1 * cos - x2 * sin, x1 * sin + x2 * cos], axis=-1)

def causal_block_attention(q, k, v, scale, cum_logf=None):
    B, H, S, Dk = q.shape
    nb = S // Q_BLOCK
    q_blocks = q.reshape(B, H, nb, Q_BLOCK, Dk).transpose(2, 0, 1, 3, 4)
    k_pos = jnp.arange(S)
    xs = [jnp.arange(nb), q_blocks]
    if cum_logf is not None:
        xs.append(cum_logf.reshape(B, H, nb, Q_BLOCK).transpose(2, 0, 1, 3))

    def one_block(blk):
        i, q_i = blk[0], blk[1]
        s = jnp.einsum('bhqd,bhkd->bhqk', q_i, k).astype(jnp.float32) * scale
        if cum_logf is not None:
            s = s + blk[2][..., :, None] - cum_logf[:, :, None, :]
        q_pos = i * Q_BLOCK + jnp.arange(Q_BLOCK)
        s = jnp.where(k_pos[None, :] <= q_pos[:, None], s, NEG_INF)
        w = jax.nn.softmax(s, axis=-1).astype(v.dtype)
        return jnp.einsum('bhqk,bhkv->bhqv', w, v)

    o = lax.map(one_block, tuple(xs))
    return o.transpose(1, 2, 0, 3, 4).reshape(B, H, S, v.shape[-1])

def retention_chunkwise(q, k, v):
    B, H, S, Dk = q.shape
    Dv = v.shape[-1]
    nc = S // RET_CHUNK
    log_g = jnp.log1p(-jnp.exp2(-5.0 - jnp.arange(H, dtype=jnp.float32)))
    j = jnp.arange(RET_CHUNK, dtype=jnp.float32)
    diff = j[:, None] - j[None, :]
    inner = jnp.exp(jnp.where(diff[None] >= 0, diff[None] * log_g[:, None, None], -jnp.inf))
    q_dec = jnp.exp((j + 1.0)[None, :] * log_g[:, None])
    k_dec = jnp.exp((RET_CHUNK - 1.0 - j)[None, :] * log_g[:, None])
    c_dec = jnp.exp(RET_CHUNK * log_g)

    def to_chunks(t):
        return t.astype(jnp.float32).reshape(B, H, nc, RET_CHUNK, -1).transpose(2, 0, 1, 3, 4)

    def step(state, qkv):
        qc, kc, vc = qkv
        a = jnp.einsum('bhqd,bhkd->bhqk', qc, kc) * inner
        o = (jnp.einsum('bhqk,bhkv->bhqv', a, vc)
             + jnp.einsum('bhqd,bhdv->bhqv', qc * q_dec[:, :, None], state))
        state = state * c_dec[:, None, None] + jnp.einsum('bhkd,bhkv->bhdv', kc * k_dec[:, :, None], vc)
        return state, o

    state0 = jnp.zeros((B, H, Dk, Dv), jnp.float32)
    _, o = lax.scan(step, state0, (to_chunks(q), to_chunks(k), to_chunks(v)))
    return o.transpose(1, 2, 0, 3, 4).reshape(B, H, S, Dv).astype(v.dtype)

def hybrid_mixer(xn, w_in, b_forget, lq1, lk1, lq2, lk2, subln_g, ret_gn_g, w_out, layer_idx):
    B, S, _ = xn.shape
    proj = xn @ w_in
    qa, ka, va, qb, kb, vb, fb, qc, kc, vc, gc = jnp.split(proj, list(np.cumsum(IN_SIZES)[:-1]), axis=-1)

    qa = split_heads(qa, 2 * DIFF_HEADS)
    ka = split_heads(ka, 2 * DIFF_HEADS)
    va = jnp.repeat(split_heads(va, DIFF_HEADS), 2, axis=1)
    o = causal_block_attention(qa, ka, va, HEAD_DIM ** -0.5)
    o = o.reshape(B, DIFF_HEADS, 2, S, DIFF_V)
    lam_init = 0.8 - 0.6 * math.exp(-0.3 * layer_idx)
    lam = (jnp.exp(jnp.sum(lq1.astype(jnp.float32) * lk1.astype(jnp.float32)))
           - jnp.exp(jnp.sum(lq2.astype(jnp.float32) * lk2.astype(jnp.float32))) + lam_init)
    o_a = o[:, :, 0] - lam.astype(o.dtype) * o[:, :, 1]
    o_a = merge_heads(rmsnorm(o_a, subln_g) * (1.0 - lam_init))

    log_f = jax.nn.log_sigmoid((fb + b_forget).astype(jnp.float32))
    cum = jnp.cumsum(log_f, axis=1).transpose(0, 2, 1)
    o_b = causal_block_attention(split_heads(qb, FOX_HEADS), split_heads(kb, FOX_HEADS),
                                 split_heads(vb, FOX_HEADS), FOX_DIM ** -0.5, cum)
    o_b = merge_heads(o_b)

    qr = rotary(split_heads(qc, RET_HEADS))
    kr = rotary(split_heads(kc, RET_HEADS)) * (RET_DIM ** -0.5)
    o_c = retention_chunkwise(qr, kr, split_heads(vc, RET_HEADS))
    o_c = merge_heads(head_groupnorm(o_c)) * ret_gn_g
    o_c = jax.nn.silu(gc) * o_c

    return jnp.concatenate([o_a, o_b, o_c], axis=-1) @ w_out

def swiglu(x, wg, wu, wd):
    return (jax.nn.silu(x @ wg) * (x @ wu)) @ wd

def moe_swiglu(xn, router, wg, wu, wd):
    B, S, D = xn.shape
    t = xn.reshape(B * S, D)
    logits = (t @ router).astype(jnp.float32)
    top_val, top_idx = lax.top_k(logits, TOP_K)
    gates = jax.nn.softmax(top_val, axis=-1)
    combine = jnp.sum(jax.nn.one_hot(top_idx, N_EXPERTS, dtype=jnp.float32) * gates[..., None], axis=1)
    out = jnp.zeros_like(t)
    for e in range(N_EXPERTS):
        out = out + combine[:, e:e + 1].astype(t.dtype) * swiglu(t, wg[e], wu[e], wd[e])
    return out.reshape(B, S, D)

def second_inputs(seed: int = 0) -> dict:
    key = jax.random.key(seed)
    ks = jax.random.split(key, 26)
    f32 = jnp.float32

    def nrm(k, shape, scale):
        return jax.random.normal(k, shape, f32) * scale

    def gain(k, shape):
        return 1.0 + 0.05 * jax.random.normal(k, shape, f32)

    return {
        "x": nrm(ks[0], (BATCH, SEQ, D_MODEL), 1.0),
        "p": nrm(ks[1], (DEPTH, BATCH, SEQ, PLE_DIM), 1.0),
        "norm_mix": gain(ks[2], (DEPTH, D_MODEL)),
        "w_in": nrm(ks[3], (DEPTH, D_MODEL, IN_COLS), D_MODEL ** -0.5),
        "b_forget": 3.0 + 0.5 * jax.random.normal(ks[4], (DEPTH, FOX_HEADS), f32),
        "lambda_q1": nrm(ks[5], (DEPTH, HEAD_DIM), 0.1),
        "lambda_k1": nrm(ks[6], (DEPTH, HEAD_DIM), 0.1),
        "lambda_q2": nrm(ks[7], (DEPTH, HEAD_DIM), 0.1),
        "lambda_k2": nrm(ks[8], (DEPTH, HEAD_DIM), 0.1),
        "diff_subln": gain(ks[9], (DEPTH, DIFF_V)),
        "ret_gn": gain(ks[10], (DEPTH, WC)),
        "w_out": nrm(ks[11], (DEPTH, MIX_WIDTH, D_MODEL), MIX_WIDTH ** -0.5),
        "norm_ffn": gain(ks[12], (DEPTH, D_MODEL)),
        "dense_w_gate": nrm(ks[13], (N_DENSE, D_MODEL, D_FF_DENSE), D_MODEL ** -0.5),
        "dense_w_up": nrm(ks[14], (N_DENSE, D_MODEL, D_FF_DENSE), D_MODEL ** -0.5),
        "dense_w_down": nrm(ks[15], (N_DENSE, D_FF_DENSE, D_MODEL), D_FF_DENSE ** -0.5),
        "router": nrm(ks[16], (N_MOE, D_MODEL, N_EXPERTS), D_MODEL ** -0.5),
        "moe_w_gate": nrm(ks[17], (N_MOE, N_EXPERTS, D_MODEL, D_FF_EXPERT), D_MODEL ** -0.5),
        "moe_w_up": nrm(ks[18], (N_MOE, N_EXPERTS, D_MODEL, D_FF_EXPERT), D_MODEL ** -0.5),
        "moe_w_down": nrm(ks[19], (N_MOE, N_EXPERTS, D_FF_EXPERT, D_MODEL), D_FF_EXPERT ** -0.5),
        "ple_norm": gain(ks[20], (DEPTH, D_MODEL)),
        "ple_gate": nrm(ks[21], (DEPTH, D_MODEL, D_MODEL), D_MODEL ** -0.5),
        "ple_proj": nrm(ks[22], (DEPTH, PLE_DIM, D_MODEL), PLE_DIM ** -0.5),
        "final_norm": gain(ks[23], (D_MODEL,)),
    }

def second_block(x, p, norm_mix, w_in, b_forget, lambda_q1, lambda_k1, lambda_q2, lambda_k2,
              diff_subln, ret_gn, w_out, norm_ffn, dense_w_gate, dense_w_up, dense_w_down,
              router, moe_w_gate, moe_w_up, moe_w_down, ple_norm, ple_gate, ple_proj, final_norm):
    h = x
    for i in range(DEPTH):
        xn = rmsnorm(h, norm_mix[i])
        h = h + hybrid_mixer(xn, w_in[i], b_forget[i], lambda_q1[i], lambda_k1[i], lambda_q2[i],
                             lambda_k2[i], diff_subln[i], ret_gn[i], w_out[i], i)
        xn = rmsnorm(h, norm_ffn[i])
        j = i // 2
        if i % 2 == 0:
            h = h + swiglu(xn, dense_w_gate[j], dense_w_up[j], dense_w_down[j])
        else:
            h = h + moe_swiglu(xn, router[j], moe_w_gate[j], moe_w_up[j], moe_w_down[j])
        gate = jax.nn.sigmoid(rmsnorm(h, ple_norm[i]) @ ple_gate[i])
        h = h + gate * (p[i] @ ple_proj[i])
    return rmsnorm(h, final_norm)


def setup_inputs(seed=0):
    out = dict(first_inputs(seed))
    for name, value in second_inputs(seed + 1).items():
        if name != "x":
            out[name + "_2"] = value
    return out


def reference(
    x, norm1_g, w_in, hg_lower_bounds, hg_norm_g, w_branch_a, w_branch_b, w_out, norm2_g, w_up,
    w_down, final_norm_g, p_2, norm_mix_2, w_in_2, b_forget_2, lambda_q1_2, lambda_k1_2,
    lambda_q2_2, lambda_k2_2, diff_subln_2, ret_gn_2, w_out_2, norm_ffn_2, dense_w_gate_2,
    dense_w_up_2, dense_w_down_2, router_2, moe_w_gate_2, moe_w_up_2, moe_w_down_2, ple_norm_2,
    ple_gate_2, ple_proj_2, final_norm_2,
):
    x = first_block(
        x, norm1_g, w_in, hg_lower_bounds, hg_norm_g, w_branch_a, w_branch_b, w_out, norm2_g,
        w_up, w_down, final_norm_g,
    )
    return second_block(
        x, p_2, norm_mix_2, w_in_2, b_forget_2, lambda_q1_2, lambda_k1_2, lambda_q2_2,
        lambda_k2_2, diff_subln_2, ret_gn_2, w_out_2, norm_ffn_2, dense_w_gate_2, dense_w_up_2,
        dense_w_down_2, router_2, moe_w_gate_2, moe_w_up_2, moe_w_down_2, ple_norm_2,
        ple_gate_2, ple_proj_2, final_norm_2,
    )


_drawn_inputs = setup_inputs


def setup_inputs(seed=0):
    import zlib

    import numpy as np

    out = dict(_drawn_inputs(seed))
    spreads = {}
    factors = {'ple_norm_2': 3.126, 'norm1_g': 3.14, 'hg_norm_g': 2.84, 'lambda_q2_2': 4.423}
    for name, (base, spread) in spreads.items():
        noise = np.random.default_rng([zlib.crc32(name.encode()), seed]).standard_normal(out[name].shape)
        drawn = base * np.exp(spread * noise) if base else spread * noise
        out[name] = __import__('jax').numpy.asarray(drawn.astype(out[name].dtype))
    for name, factor in factors.items():
        out[name] = (out[name] * factor).astype(out[name].dtype)
    return out
```

```python
import numpy as np
import concourse.bass as bass
from concourse import mybir
from contextlib import ExitStack

F32 = mybir.dt.float32
F32R = mybir.dt.float32r
BF16 = mybir.dt.bfloat16
I8 = mybir.dt.int8
U32 = mybir.dt.uint32
ALU = mybir.AluOpType
ACT = mybir.ActivationFunctionType
AX = mybir.AxisListType

P = 128
T = 2
D = 1024
EPS = 1e-6
RAW = 5
WR = 3
LAM_INIT = [0.8 - 0.6 * float(np.exp(-0.3 * i)) for i in range(2)]
FF2, FE, NE = 2816, 3584, 8
A0 = 2048
LEVELS = [0, 1, 2, 4, 8, 16, 32, 64]


class Eng:

    def __init__(self, e, sem):
        self.e, self.sem, self.n, self.seen = e, sem, 0, {}

    def at(self, *toks):
        for tok in toks:
            if tok is None:
                continue
            key, sem, val = tok
            if self.seen.get(key, 0) < val:
                self.seen[key] = val
                self.e.wait_ge(sem, val)
        return self.e

    def i(self, ins):
        ins.then_inc(self.sem, 1)
        self.n += 1
        return (self.sem.name, self.sem, self.n)

    @property
    def last(self):
        return (self.sem.name, self.sem, self.n) if self.n else None


def plan(dr):
    out = []

    def rows(w, kp, c0, n):
        return w[kp * 512:kp * 512 + 512, c0:c0 + n].rearrange("(k p) n -> p k n", p=P)

    def up(key, w, c0, n, K=D):
        for kp in range(K // 512):
            out.append(((key, kp), rows(w, kp, c0, n), 4, n))

    def down(key, w, r0, K):
        for kp in range(K // 256):
            out.append(((key, kp), w[r0 + kp * 256:r0 + kp * 256 + 256, :].rearrange("(k p) n -> p k n", p=P), 2, D))

    def mlp(key, gate, upw, dn, F):
        ng = -(-F // 512)
        for n in range(ng + 1):
            w = min(512, F - n * 512)
            if n < ng:
                if gate is not None:
                    up((key, "g", n), gate, n * 512, w)
                up((key, "u", n), upw, n * 512, w)
            if n:
                down((key, "d", n - 1), dn, (n - 1) * 512, min(512, F - (n - 1) * 512))

    for l in range(2):
        for g in range(17):
            up(("in1", l, g), dr["w_in"][l], g * 512, 512)
        for br in ("a", "b"):
            for n in range(2):
                up(("br" + br, l, n), dr["w_branch_" + br][l], n * 512, 512, 512)
        for n in range(2):
            up(("out1", l, n), dr["w_out"][l], n * 512, 512)
        mlp(("m1", l), None, dr["w_up"][l], dr["w_down"][l], 4096)
    for l in range(2):
        for name, c0, n in (("qa", 0, 512), ("ka", 512, 512), ("va", 1024, 512), ("vf", 2048, 260),
                            ("qkb", 1536, 512), ("qkc", 2308, 512), ("vgc", 2820, 512)):
            up(("in2", l, name), dr["w_in_2"][l], c0, n)
        for n in range(2):
            up(("out2", l, n), dr["w_out_2"][l], n * 512, 512)
        if l == 0:
            mlp(("m2", 0), dr["dense_w_gate_2"][0], dr["dense_w_up_2"][0], dr["dense_w_down_2"][0], FF2)
        else:
            for e in range(NE):
                mlp(("moe", e), dr["moe_w_gate_2"][0, e], dr["moe_w_up_2"][0, e], dr["moe_w_down_2"][0, e], FE)
        down(("pp", l), dr["ple_proj_2"][l], 0, 256)
        for n in range(2):
            up(("pg", l, n), dr["ple_gate_2"][l], n * 512, 512)
    return out


def program(nc, dr, cf, cb, ci, out):
    ctx = ExitStack()
    with ctx:
        def sb(name, shape, dt=F32):
            return ctx.enter_context(nc.sbuf_tensor(name, shape, dt))

        def sem(name):
            return ctx.enter_context(nc.semaphore(name))

        PS = ctx.enter_context(nc.psum_tensor("PS", [P, 8, 512], F32))
        raw = sb("raw", [P, RAW, 2048])
        WH = sb("WH", [P, WR, 2048], F32R)
        WL = sb("WL", [P, WR, 2048], F32R)
        XTH = sb("XTH", [P, 8, 256], F32R)
        XTL = sb("XTL", [P, 8, 256], F32R)
        HTH = sb("HTH", [P, 4, 256], F32R)
        HTL = sb("HTL", [P, 4, 256], F32R)
        RTH = sb("RTH", [P, 8, 8], F32R)
        RTL = sb("RTL", [P, 8, 8], F32R)
        X = sb("X", [P, T, D])
        XN = sb("XN", [P, T, D])
        AR = sb("AR", [P, 16384])
        CF = sb("CF", [P, cf.shape[1]])
        CB = sb("CB", [P, cb.shape[1]], BF16)
        CI = sb("CI", [P, ci.shape[1]], I8)
        G = sb("G", [P, 128])
        GR = sb("GR", [P, 128])
        sm = sb("sm", [P, 256])
        RT = sb("RT", [P, 64])
        LQ = sb("LQ", [P, 2, 4, 64])
        BF = sb("BF", [P, 2, 4])
        idx = sb("idx", [P, 2, 8], U32)

        PE = Eng(nc.tensor, sem("s_pe"))
        V = Eng(nc.vector, sem("s_v"))
        S = Eng(nc.scalar, sem("s_s"))
        GP = Eng(nc.gpsimd, sem("s_g"))
        SP = Eng(nc.sync, sem("s_sp"))

        ident = CF[:, 0:128]
        tri = CF[:, 128:256]
        ones = CF[:, 256:384]
        ropeA = CF[:, 384:448].rearrange("p (t d) -> p t d", t=2)
        ropeB = CF[:, 448:512].rearrange("p (t d) -> p t d", t=2)
        rotA = CF[:, 512:640].rearrange("p (t d) -> p t d", t=2)
        rotB = CF[:, 640:768].rearrange("p (t d) -> p t d", t=2)
        iota8 = CF[:, 768:776]
        RD = CF[:, 776:776 + 1024].rearrange("p (h t) -> p h t", h=4)
        mask1 = [CB[:, 0:384].rearrange("p (g k) -> p g k", g=3), CB[:, 384:1152].rearrange("p (g k) -> p g k", g=3)]
        mask2 = [CB[:, 0:128], CB[:, 1152:1408]]
        hmask = [CI[:, i * 128:(i + 1) * 128] for i in range(8)]

        def small(name, pairs):
            s = sem(name)
            for a, b in pairs:
                nc.sync.dma_start(a, b).then_inc(s, 16)
            return (name, s, 16 * len(pairs))

        ld_x = small("ld_x", [(X[:, :, :], dr["x"][0].rearrange("(t p) d -> p t d", p=P))])
        rows, pairs = {}, []

        def grow(key, ap, n):
            k = sum(v[1] for v in rows.values())
            rows[key] = (k, n)
            pairs.append((GR[k:k + n, :], ap.rearrange("(c p) -> c p", p=P)))

        for l in range(2):
            grow(("n1", l), dr["norm1_g"][l], 8)
            grow(("n2", l), dr["norm2_g"][l], 8)
            grow(("nm", l), dr["norm_mix_2"][l], 8)
            grow(("nf", l), dr["norm_ffn_2"][l], 8)
            grow(("pn", l), dr["ple_norm_2"][l], 8)
            grow(("hb", l), dr["hg_lower_bounds"][l], 4)
            grow(("hn", l), dr["hg_norm_g"][l], 4)
            grow(("sub", l), dr["diff_subln_2"][l], 1)
            grow(("rg", l), dr["ret_gn_2"][l], 2)
        NG = sum(v[1] for v in rows.values())
        ld_c = small("ld_c", [(CF[:, :], cf), (AR[:, 1024:2432], cb), (AR[:, 0:1024], ci)])
        ld_g = small("ld_g", pairs)

        PIECES = plan(dr)
        dsem = [sem(f"ld_w{i}") for i in range(RAW)]
        raw_free = [[] for _ in range(RAW)]
        loaded, split_tok, pe_done = [], [], []

        def load():
            i = len(loaded)
            if i >= len(PIECES):
                return
            _, src, nb, n = PIECES[i]
            s = i % RAW
            SP.at(*raw_free[s])
            nc.sync.dma_start(raw[:, s, 0:nb * n].rearrange("p (k n) -> p k n", k=nb), src).then_inc(dsem[s], 16)
            loaded.append((f"ld_w{s}", dsem[s], 16 * (i // RAW + 1)))

        def split():
            i = len(split_tok)
            if i >= len(PIECES):
                return
            _, _, nb, n = PIECES[i]
            s, w, m = i % RAW, i % WR, nb * n
            free = pe_done[i - WR] if i >= WR else None
            a = S.i(S.at(loaded[i], free).copy(WH[:, w, 0:m], raw[:, s, 0:m]))
            b = V.i(V.at(loaded[i], a, free).tensor_tensor(WL[:, w, 0:m], raw[:, s, 0:m],
                                                           WH[:, w, 0:m].bitcast(F32), ALU.subtract))
            split_tok.append(b)
            raw_free[s] = [a, b]
            load()

        for _ in range(RAW):
            load()

        bg = []

        def tick():
            for g in list(bg):
                try:
                    next(g)
                except StopIteration:
                    bg.remove(g)

        def drain():
            while bg:
                tick()

        def take(key):
            i = len(pe_done)
            assert PIECES[i][0] == key, (PIECES[i][0], key)
            while len(split_tok) < min(i + WR, len(PIECES)):
                split()
            PE.at(split_tok[i])
            _, _, nb, n = PIECES[i]
            w = i % WR
            return [f[:, w, 0:nb * n].rearrange("p (k n) -> p k n", k=nb) for f in (WH, WL)]

        bank_free = [[] for _ in range(8)]

        def mm3(o, lh, ll, rh, rl, start, stop):
            nc.tensor.matmul(o, lh, rh, start=start, stop=False, skip_group_check=True)
            nc.tensor.matmul(o, lh, rl, start=False, stop=False, skip_group_check=True)
            return nc.tensor.matmul(o, ll, rh, start=False, stop=stop, skip_group_check=True)

        def up(key, n, ready, K=D, k0=0, banks=(4, 5), mid=None):
            nk = K // 512
            toks = [None, None]
            PE.at(*ready)
            for kp in range(nk):
                wh, wl = take((key, kp))
                for t in range(T):
                    if kp == 0:
                        PE.at(*bank_free[banks[t]])
                    for k in range(4):
                        kk = k0 + kp * 4 + k
                        last = mm3(PS[:, banks[t], 0:n], XTH[:, kk, t * P:t * P + P], XTL[:, kk, t * P:t * P + P],
                                   wh[:, k, :], wl[:, k, :], kp == 0 and k == 0, kp == nk - 1 and k == 3)
                    if kp == nk - 1 or t == 1:
                        toks[t] = PE.i(last)
                pe_done.append(PE.last)
                if kp < nk - 1:
                    if mid is not None:
                        mid()
                    tick()
            return toks

        def down(key, K, lh, ll, ready, first, final):
            PE.at(*ready)
            if first:
                PE.at(*bank_free[0], *bank_free[1], *bank_free[2], *bank_free[3])
            nk = K // 256
            for kp in range(nk):
                wh, wl = take((key, kp))
                for t in range(T):
                    for j in range(2):
                        for k in range(2):
                            kk = kp * 2 + k
                            last = mm3(PS[:, 2 * t + j, :], lh[:, kk, t * P:t * P + P], ll[:, kk, t * P:t * P + P],
                                       wh[:, k, j * 512:j * 512 + 512], wl[:, k, j * 512:j * 512 + 512],
                                       first and kk == 0, final and kk == 2 * nk - 1)
                pe_done.append(PE.i(last))
                tick()
            return PE.last

        PE.at(ld_c, ld_g)
        t0 = PE.i(nc.tensor.transpose(PS[:, 7, 0:NG], GR[0:NG, :], ident[0:NG, 0:NG]))
        g_all = V.i(V.at(t0).tensor_copy(G[:, 0:NG], PS[:, 7, 0:NG]))
        bank_free[7] = [g_all]
        S.at(ld_c)
        V.i(V.at(ld_c).tensor_copy(CB[:, :], AR[:, 1024:2432]))
        ci_tok = V.i(V.at(ld_c).tensor_copy(CI[:, :], AR[:, 0:1024]))

        def gc(key, c=0, n=1):
            return G[:, rows[key][0] + c:rows[key][0] + c + n]

        LB = sm[:, 0:4]
        OMB = sm[:, 4:8]
        lt = sm[:, 8:32]
        a = V.i(V.at(g_all).tensor_tensor(lt[:, 0:4], gc(("hb", 0), 0, 4), gc(("hb", 1), 0, 4), ALU.max))
        a = V.i(V.at(a).tensor_tensor(lt[:, 4:8], gc(("hb", 0), 0, 4), lt[:, 0:4], ALU.subtract))
        a = V.i(V.at(a).tensor_tensor(lt[:, 8:12], gc(("hb", 1), 0, 4), lt[:, 0:4], ALU.subtract))
        a = S.i(S.at(a).activation(lt[:, 12:20], lt[:, 4:12], ACT.Exp))
        a = V.i(V.at(a).tensor_tensor(lt[:, 20:24], lt[:, 12:16], lt[:, 16:20], ALU.add))
        a = V.i(V.at(a).reciprocal(lt[:, 20:24], lt[:, 20:24]))
        a = V.i(V.at(a).tensor_tensor(LB, lt[:, 16:20], lt[:, 20:24], ALU.mult))
        lb_tok = V.i(V.at(a).tensor_scalar(OMB, LB, -1.0, 1.0, ALU.mult, ALU.add))

        ss = sm[:, 32:34]
        rs = sm[:, 34:36]

        def rstd(xready, xn_free):
            a = None
            for t in range(T):
                a = S.i(S.at(*xready, *xn_free, V.last).activation(XN[:, t, :], X[:, t, :], ACT.Square,
                                                                   accum_out=ss[:, t:t + 1]))
            a = V.i(V.at(a).tensor_scalar(rs, ss, 1.0 / D, EPS, ALU.mult, ALU.add))
            a = S.i(S.at(a).activation(rs, rs, ACT.Sqrt))
            return V.i(V.at(a).reciprocal(rs, rs))

        def to_xt(src, ready, gains, c0=0, nch=8, dst=None):
            dh, dl = dst if dst is not None else (XTH, XTL)
            wr = []
            pe_last = PE.last
            for r in range(nch // 2):
                b = 4 + r % 4
                PE.at(*ready, *bank_free[b])
                for c in range(2):
                    for t in range(T):
                        cc = 2 * r + c
                        last = nc.tensor.transpose(PS[:, b, c * 256 + t * P:c * 256 + t * P + P],
                                                   src[:, t, cc * P:cc * P + P], ident)
                tp = PE.i(last)
                for c in range(2):
                    cc = 2 * r + c
                    pv = PS[:, b, c * 256:c * 256 + 256]
                    if gains[cc] is None:
                        a = S.i(S.at(tp, pe_last).copy(dh[:, c0 + cc, :], pv))
                    else:
                        a = S.i(S.at(tp, pe_last, g_all).activation(dh[:, c0 + cc, :], pv, ACT.Copy, scale=gains[cc]))
                for c in range(2):
                    cc = 2 * r + c
                    pv = PS[:, b, c * 256:c * 256 + 256]
                    dhf = dh[:, c0 + cc, :].bitcast(F32)
                    if gains[cc] is None:
                        v = V.i(V.at(a, tp, pe_last).tensor_tensor(dl[:, c0 + cc, :], pv, dhf, ALU.subtract))
                    else:
                        v = V.i(V.at(a, tp, pe_last).scalar_tensor_tensor(
                            out=dl[:, c0 + cc, :], in0=pv, scalar=gains[cc], in1=dhf, op0=ALU.mult, op1=ALU.subtract))
                wr += [a, v]
                bank_free[b] = [a, v]
            return [wr[-2], wr[-1], tp]

        def norm_t(key, xready, xn_free):
            r = rstd(xready, xn_free)
            for t in range(T):
                a = V.i(V.at(r).tensor_scalar(XN[:, t, :], X[:, t, :], rs[:, t:t + 1], None, ALU.mult))
            return to_xt(XN, [a], [gc(key, c) for c in range(8)])

        def block_norm(gain_dram, name, dst, xready, xn_free):
            gb = AR[:, 0:1024]
            s = sem(name)
            SP.at(*xready, PE.last, V.last, S.last)
            nc.sync.dma_start(gb, gain_dram.partition_broadcast(P)).then_inc(s, 16)
            r = rstd(xready, xn_free)
            for t in range(T):
                a = V.i(V.at(r, (name, s, 16)).scalar_tensor_tensor(
                    out=dst[:, t, :], in0=X[:, t, :], scalar=rs[:, t:t + 1], in1=gb, op0=ALU.mult, op1=ALU.mult))
            return a

        HM = AR[:, 15360:16384].rearrange("p (t n) -> p t n", t=2)

        def mlp(key, gated, F, ready, comb=None, first=True, final=True):
            ng = -(-F // 512)
            hm_tok = ht_tok = None
            tr_last = [None]
            for n in range(ng + 1):
                w = min(512, F - n * 512)
                state = {}

                def turn(n=n):
                    wp = min(512, F - (n - 1) * 512)
                    toks = []
                    pd = PE.last
                    for r in range(wp // 256):
                        b = 6 + r
                        PE.at(*hm_tok, *bank_free[b])
                        for c in range(2):
                            for t in range(T):
                                last = nc.tensor.transpose(PS[:, b, c * 256 + t * P:c * 256 + t * P + P],
                                                           HM[:, t, (2 * r + c) * P:(2 * r + c) * P + P], ident)
                        tp = PE.i(last)
                        pv = PS[:, b, :].rearrange("p (c m) -> p c m", c=2)
                        a = S.i(S.at(tp, pd).copy(HTH[:, 2 * r:2 * r + 2, :], pv))
                        v = V.i(V.at(a, tp, pd).tensor_tensor(HTL[:, 2 * r:2 * r + 2, :], pv,
                                                              HTH[:, 2 * r:2 * r + 2, :].bitcast(F32), ALU.subtract))
                        bank_free[b] = [a, v]
                        toks += [a, v]
                    state["ht"] = toks
                    tr_last[0] = PE.last

                if n < ng:
                    if gated:
                        tg = up((key, "g", n), w, ready, mid=turn if n else None)
                        sil = []
                        for t in range(T):
                            a = S.i(S.at(tg[t], tr_last[0], V.last if n == 0 else None).activation(
                                HM[:, t, 0:w], PS[:, 4 + t, 0:w], ACT.Silu))
                            bank_free[4 + t] = [a]
                            sil.append(a)
                        tick()
                        tu = up((key, "u", n), w, ready)
                        new = []
                        for t in range(T):
                            if comb is None:
                                v = V.i(V.at(tu[t], sil[t]).tensor_tensor(HM[:, t, 0:w], PS[:, 4 + t, 0:w],
                                                                          HM[:, t, 0:w], ALU.mult))
                            else:
                                v = V.i(V.at(tu[t], sil[t]).scalar_tensor_tensor(
                                    out=HM[:, t, 0:w], in0=PS[:, 4 + t, 0:w], scalar=comb[t], in1=HM[:, t, 0:w],
                                    op0=ALU.mult, op1=ALU.mult))
                            bank_free[4 + t] = [v]
                            new.append(v)
                    else:
                        tu = up((key, "u", n), w, ready, mid=turn if n else None)
                        new = []
                        for t in range(T):
                            a = S.i(S.at(tu[t], tr_last[0], V.last if n == 0 else None).activation(
                                HM[:, t, 0:w], PS[:, 4 + t, 0:w], ACT.Relu))
                            v = V.i(V.at(a).scalar_tensor_tensor(out=HM[:, t, 0:w], in0=PS[:, 4 + t, 0:w], scalar=0.0,
                                                                 in1=HM[:, t, 0:w], op0=ALU.max, op1=ALU.mult))
                            bank_free[4 + t] = [v]
                            new.append(v)
                    hm_next = new
                    tick()
                else:
                    turn()
                if n:
                    d = down((key, "d", n - 1), min(512, F - (n - 1) * 512), HTH, HTL, state["ht"],
                             first and n == 1, final and n == ng)
                hm_tok = hm_next
            return d

        def add_x(tok):
            r = []
            for t in range(T):
                for j in range(2):
                    v = V.i(V.at(tok).tensor_tensor(X[:, t, j * 512:j * 512 + 512], PS[:, 2 * t + j, :],
                                                    X[:, t, j * 512:j * 512 + 512], ALU.add))
                    bank_free[2 * t + j] = [v]
            return v

        def out_proj(key, ready):
            for n in range(2):
                tk = up((key[0], key[1], n), 512, ready)
                for t in range(T):
                    v = V.i(V.at(tk[t]).tensor_tensor(X[:, t, n * 512:n * 512 + 512], PS[:, 4 + t, :],
                                                      X[:, t, n * 512:n * 512 + 512], ALU.add))
                    bank_free[4 + t] = [v]
                tick()
            return v

        QT = AR[:, 0:3072].rearrange("p (g h m) -> p g h m", g=3, h=4)
        KT = AR[:, 3072:6144].rearrange("p (g h m) -> p g h m", g=3, h=4)
        VV = AR[:, 6144:9216].rearrange("p (t g n) -> p t g n", t=2, g=3)
        GG = AR[:, 9216:10240].rearrange("p (t n) -> p t n", t=2)
        VH = AR[:, 6144:7168].rearrange("p (t n) -> p t n", t=2)
        SG = AR[:, 7168:8192]
        TOT = AR[:, 8192:9216]
        HQ = AR[:, 10240:11264]
        HK = AR[:, 11264:12288]
        ATT = AR[:, 12288:13312].rearrange("p (a m) -> p a m", a=8)
        ATX = AR[:, 13312:13824].rearrange("p (h m) -> p h m", h=4)
        TT = AR[:, 13824:14336]
        ZT = AR[:, 14336:15360].rearrange("p (t n) -> p t n", t=2)
        RP = AR[:, 15360:15872].rearrange("p (t x) -> p t x", t=2)
        ZB = AR[:, 10240:12288].rearrange("p (t n) -> p t n", t=2)
        SC = AR[:, 12288:13824].rearrange("p (b n) -> p b n", b=2)
        PT = AR[:, 13824:15360].rearrange("p (b n) -> p b n", b=2)
        OA = AR[:, 15360:16384].rearrange("p (t n) -> p t n", t=2)

        def turn_heads(src, ready, np_=P, nh=4, wd=P):
            toks = []
            for b in range(nh // 2):
                PE.at(*ready, *bank_free[6 + b])
                for c in range(2):
                    for t in range(T):
                        last = nc.tensor.transpose(PS[0:wd, 6 + b, c * 256 + t * P:c * 256 + t * P + P],
                                                   src(t, 2 * b + c), ident)
                toks.append(PE.i(last))
            return toks

        def hgrn(l, st):
            free = st["at_free"]
            z = V.i(V.at(*free).memset(AR[:, 12288:13312], 0.0))
            q4 = HQ.rearrange("p (a m) -> p a m", m=P)
            k4 = HK.rearrange("p (a m) -> p a m", m=P)
            ready = st["qk"]
            tot_tok = st["f"]
            tot = TOT
            ntot = 1024
            alt = TT
            for li, m in enumerate(LEVELS):
                pt = []
                for b in range(2):
                    PE.at(*ready, *bank_free[b])
                    for a_ in range(4):
                        last = nc.tensor.matmul(PS[:, b, a_ * P:a_ * P + P], k4[:, 4 * b + a_, :], q4[:, 4 * b + a_, :],
                                                start=True, stop=True)
                    pt.append(PE.i(last))
                yield
                for b in range(2):
                    v = V.i(V.at(pt[b], z, V.last).copy_predicated(
                        ATT[:, 4 * b:4 * b + 4, :], hmask[li].unsqueeze(1).to_broadcast([P, 4, P]),
                        PS[:, b, :].rearrange("p (a m) -> p a m", a=4)))
                    bank_free[b] = [v]
                if m == 0:
                    v = V.i(V.at(*pt, tot_tok).tensor_tensor(HQ, HQ, TOT, ALU.mult))
                    ready = [v]
                else:
                    nb = 1024 // (2 * m)
                    q3 = HQ.rearrange("p (b w m) -> p b w m", w=2, m=m)
                    k3 = HK.rearrange("p (b w m) -> p b w m", w=2, m=m)
                    t3 = tot[:, 0:2 * nb].rearrange("p (b w) -> p b w", w=2)
                    v1 = V.i(V.at(*pt, tot_tok).tensor_tensor(
                        q3[:, :, 1, :], q3[:, :, 1, :], t3[:, :, 0:1].to_broadcast([P, nb, m]), ALU.mult))
                    v2 = V.i(V.at(*pt, tot_tok).tensor_tensor(
                        k3[:, :, 0, :], k3[:, :, 0, :], t3[:, :, 1:2].to_broadcast([P, nb, m]), ALU.mult))
                    nt = alt[:, 0:nb]
                    tot_tok = V.i(V.at(tot_tok, v2).tensor_tensor(nt, t3[:, :, 0], t3[:, :, 1], ALU.mult))
                    tot, alt = alt, (TOT if alt is TT else TT)
                    ready = [v1, v2]
            q3 = HQ.rearrange("p (h t m) -> p h t m", h=4, t=2)
            k3 = HK.rearrange("p (h t m) -> p h t m", h=4, t=2)
            PE.at(*ready, *bank_free[0])
            for h in range(4):
                last = nc.tensor.matmul(PS[:, 0, h * P:h * P + P], k3[:, h, 0, :], q3[:, h, 1, :], start=True, stop=True)
            tk = PE.i(last)
            yield
            ax = V.i(V.at(tk).tensor_copy(AR[:, 13312:13824], PS[:, 0, :]))
            bank_free[0] = [ax]
            yield
            pv = []
            for t in range(T):
                PE.at(ax, V.last, st["v"], *bank_free[2 + t])
                for h in range(4):
                    o = PS[:, 2 + t, h * P:h * P + P]
                    last = nc.tensor.matmul(o, ATT[:, 2 * h + t, :], VH[:, t, h * P:h * P + P],
                                            start=True, stop=(t == 0))
                    if t == 1:
                        last = nc.tensor.matmul(o, ATX[:, h, :], VH[:, 0, h * P:h * P + P], start=False, stop=True)
                pv.append(PE.i(last))
            yield
            for t in range(T):
                sq = SG[:, 0:512]
                a = S.i(S.at(pv[t], V.last).activation(sq, PS[:, 2 + t, :], ACT.Square))
                r4 = sm[:, 40:44]
                v = V.i(V.at(a, V.last).tensor_reduce(r4, sq.rearrange("p (h m) -> p h m", h=4), AX.X, ALU.add))
                v = V.i(V.at(v).tensor_scalar(r4, r4, 1.0 / P, EPS, ALU.mult, ALU.add))
                a = S.i(S.at(v).activation(r4, r4, ACT.Sqrt))
                v = V.i(V.at(a).reciprocal(r4, r4))
                g3 = GG[:, t, :].rearrange("p (h m) -> p h m", h=4)
                v = V.i(V.at(v, st["g"]).tensor_tensor(g3, g3, r4.unsqueeze(2).to_broadcast([P, 4, P]), ALU.mult))
                v = V.i(V.at(v).tensor_tensor(GG[:, t, :], PS[:, 2 + t, :], GG[:, t, :], ALU.mult))
                bank_free[2 + t] = [v, a]
                yield
            st["done"] = [v, a, pv[1]]

        def softmax_tasks(tasks):
            n = len(tasks)
            st = [dict() for _ in tasks]

            def sA(i):
                q = tasks[i]
                PE.at(*q["ready"], *bank_free[0], *bank_free[1])
                for o, lh, rh in q["scores"]:
                    last = nc.tensor.matmul(o, lh, rh, start=True, stop=True)
                st[i]["s"] = PE.i(last)

            def sB(i):
                q, b = tasks[i], i % 2
                prev = st[i - 2]["tr"] if i >= 2 else None
                s2 = SC[:, b, 0:q["n"]]
                V.at(st[i]["s"], prev, st[i - 2]["e"] if i >= 2 else None, *q["scfree"])
                for dst, ps, mk in q["mask"](s2):
                    v = V.i(nc.vector.scalar_tensor_tensor(out=dst, in0=ps, scalar=q["scale"], in1=mk,
                                                           op0=ALU.mult, op1=ALU.add))
                bank_free[0] = bank_free[1] = [v]
                ns = q["nsub"]
                mx = sm[:, 48 + 4 * b:48 + 4 * b + ns]
                v = V.i(V.at(v).tensor_reduce(mx, s2.rearrange("p (a k) -> p a k", a=ns), AX.X, ALU.max))
                v = V.i(V.at(v).tensor_scalar(mx, mx, -1.0, None, ALU.mult))
                w = q["n"] // ns
                for a_ in range(ns):
                    e = S.i(S.at(v, q["denfree"]).activation(s2[:, a_ * w:a_ * w + w], s2[:, a_ * w:a_ * w + w], ACT.Exp,
                                               bias=mx[:, a_:a_ + 1], accum_out=q["den"][:, a_:a_ + 1]))
                st[i]["e"] = e

            def sC(i):
                q, b = tasks[i], i % 2
                nch = q["n"] // P
                PE.at(st[i]["e"])
                st[i]["ev"] = []
                for bb in range(-(-nch // 4)):
                    PE.at(*bank_free[6 + bb])
                    m = min(4, nch - 4 * bb)
                    for c in range(m):
                        last = nc.tensor.transpose(PS[:, 6 + bb, c * P:c * P + P],
                                                   SC[:, b, (4 * bb + c) * P:(4 * bb + c) * P + P], ident)
                    tp = PE.i(last)
                    old = st[i - 2]["pv"] if i >= 2 else None
                    dst = PT[:, b, bb * 512:bb * 512 + m * P]
                    if bb == 0:
                        ev = S.i(S.at(tp, old, *q["scfree"]).copy(dst, PS[:, 6, 0:m * P]))
                    else:
                        ev = V.i(V.at(tp, old, *q["scfree"]).tensor_copy(dst, PS[:, 7, 0:m * P]))
                    bank_free[6 + bb] = [ev]
                    st[i]["ev"].append(ev)
                st[i]["tr"] = PE.last

            def sE(i):
                q, b = tasks[i], i % 2
                PE.at(*st[i]["ev"], *bank_free[q["obank"]] if q["ofirst"] else [])
                PE.at(*st[i]["ev"])
                for o, chunks in q["pv"]:
                    for j, (c, v) in enumerate(chunks):
                        last = nc.tensor.matmul(o, PT[:, b, c * P:c * P + P], v, start=(j == 0), stop=(j == len(chunks) - 1))
                st[i]["pv"] = PE.i(last)
                if q["after"] is not None:
                    q["after"](st[i]["pv"], st[i]["e"])

            for k in range(n + 2):
                if 0 <= k - 2 < n:
                    sE(k - 2)
                if 0 <= k - 1 < n:
                    sC(k - 1)
                if k < n:
                    sA(k)
                    sB(k)
                yield

        xr = [ld_x]
        xn_free = []
        ar_free = [ci_tok]
        for l in range(2):
            xt = norm_t(("n1", l), xr, xn_free)
            st = {}
            ztr = [None]
            hg_tmp = []

            def qk1(which, g, tk):
                cp = []
                for t in range(T):
                    a = S.i(S.at(tk[t], ztr[0], V.last if which == 0 and g == 0 else None).copy(ZT[:, t, :], PS[:, 4 + t, :]))
                    bank_free[4 + t] = [a]
                cp.append(a)
                r4 = ZT[:, :, :].rearrange("p t (h d) -> p t h d", h=4)
                p1 = RP[:, :, 0:128].rearrange("p t (h d) -> p t h d", h=4)
                p2 = RP[:, :, 128:256].rearrange("p t (h d) -> p t h d", h=4)
                V.at(a, V.last)
                v = None
                for t in range(T):
                    A = ropeA[:, t, :].unsqueeze(1).to_broadcast([P, 4, 32])
                    B = ropeB[:, t, :].unsqueeze(1).to_broadcast([P, 4, 32])
                    V.i(nc.vector.tensor_tensor(p1[:, t], r4[:, t, :, 0:32], A, ALU.mult))
                    V.i(nc.vector.tensor_tensor(p2[:, t, :, 0:16], r4[:, t, :, 16:32], B[:, :, 0:16], ALU.mult))
                    v = V.i(nc.vector.tensor_tensor(p2[:, t, :, 16:32], r4[:, t, :, 0:16], B[:, :, 16:32], ALU.mult))
                for t in range(T):
                    v = V.i(V.at(v).tensor_tensor(r4[:, t, :, 0:32], p1[:, t], p2[:, t], ALU.add))
                yield
                dst = QT if which == 0 else KT
                tt = turn_heads(lambda t, h: ZT[:, t, h * P:h * P + P], [v, a])
                ztr[0] = tt[-1]
                a = S.i(S.at(tt[0]).copy(dst[:, g, 0:2, :], PS[:, 6, :].rearrange("p (h m) -> p h m", h=2)))
                v = V.i(V.at(tt[1]).tensor_copy(dst[:, g, 2:4, :], PS[:, 7, :].rearrange("p (h m) -> p h m", h=2)))
                bank_free[6], bank_free[7] = [a], [v]
                st[("qk", which, g)] = [a, v]
                yield

            def hq(which, tk):
                for t in range(T):
                    a = S.i(S.at(tk[t], ztr[0], *ar_free).copy(ZT[:, t, :], PS[:, 4 + t, :]))
                    bank_free[4 + t] = [a]
                yield
                tt = turn_heads(lambda t, h: ZT[:, t, h * P:h * P + P], [a])
                ztr[0] = tt[-1]
                for b in range(2):
                    sl = slice(b * 512, b * 512 + 512)
                    if which == 0:
                        a = S.i(S.at(tt[b], V.last).activation(SG[:, sl], PS[:, 6 + b, :], ACT.Sigmoid))
                        v = V.i(V.at(a).tensor_tensor(HQ[:, sl], PS[:, 6 + b, :], SG[:, sl], ALU.mult))
                        st["q"] = v
                    else:
                        a = S.i(S.at(tt[b]).activation(TOT[:, sl], PS[:, 6 + b, :], ACT.Sigmoid))
                        a = S.i(S.at(tt[b]).activation(HK[:, sl], PS[:, 6 + b, :], ACT.Sigmoid, scale=-1.0))
                        v = a
                        if l == 1:
                            for h in range(2 * b, 2 * b + 2):
                                hs = slice(h * 256, h * 256 + 256)
                                V.i(V.at(a, lb_tok).tensor_scalar(TOT[:, hs], TOT[:, hs], OMB[:, h:h + 1], LB[:, h:h + 1],
                                                                  ALU.mult, ALU.add))
                                v = V.i(V.at(a, lb_tok).tensor_scalar(HK[:, hs], HK[:, hs], OMB[:, h:h + 1], None, ALU.mult))
                        st["f"] = v
                    bank_free[6 + b] = [a, v if which == 0 else a]
                st["qk"] = [st["q"], st.get("f")]
                if which == 1:
                    st["at_free"] = ar_free
                    bg.append(hgrn(l, st))
                yield

            def plain(dst, tk, fn, wait=()):
                for t in range(T):
                    if fn is None:
                        a = S.i(S.at(tk[t], *wait).copy(dst(t), PS[:, 4 + t, :]))
                    else:
                        a = S.i(S.at(tk[t], *wait).activation(dst(t), PS[:, 4 + t, :], fn))
                    bank_free[4 + t] = [a]
                return a

            for g in range(17):
                if g == 10:
                    while "done" not in st:
                        tick()
                tk = up(("in1", l, g), 512, xt)
                if g < 2:
                    bg.append(hq(g, tk))
                elif g == 2:
                    st["v"] = plain(lambda t: VH[:, t, :], tk, None, ar_free)
                elif g == 3:
                    st["g"] = plain(lambda t: GG[:, t, :], tk, ACT.Sigmoid, ar_free)
                elif g < 10:
                    bg.append(qk1((g - 4) // 3, (g - 4) % 3, tk))
                elif g < 13:
                    st["vv"] = plain(lambda t: VV[:, t, g - 10, :], tk, None, st["done"])
                else:
                    if g == 13:
                        while bg:
                            tick()
                    dst = XN if g < 15 else ZB
                    o = (g - 13) % 2 * 512
                    st[("z", g)] = plain(lambda t: dst[:, t, o:o + 512], tk, None, st["done"] + [xt[2], ztr[0]])
                if g == 12:
                    while bg:
                        tick()
                    tasks = []
                    rd = [st["vv"]] + [x for w in range(2) for gg in range(3) for x in st[("qk", w, gg)]]
                    for t in range(T):
                        nk = (t + 1) * P
                        for h in range(4):
                            den = sm[:, 64 + 4 * t + h:65 + 4 * t + h]
                            sc, mk = [], []
                            for gg in range(3):
                                if t == 0:
                                    o = PS[:, 0, gg * P:gg * P + P]
                                else:
                                    o = PS[:, gg // 2, (gg % 2) * 256:(gg % 2) * 256 + 256]
                                sc.append((o, QT[:, gg, h, t * P:t * P + P], KT[:, gg, h, 0:nk]))

                            def mask(s2, t=t, nk=nk):
                                if t == 0:
                                    return [(s2, PS[:, 0, 0:384], CB[:, 0:384])]
                                return [(s2[:, 0:512], PS[:, 0, :], CB[:, 384:896]),
                                        (s2[:, 512:768], PS[:, 1, 0:256], CB[:, 896:1152])]

                            chunks = [(gg * (t + 1) + kc, VV[:, kc, gg, h * P:h * P + P])
                                      for gg in range(3) for kc in range(t + 1)]

                            def after(pv, e, t=t, h=h):
                                if h < 3:
                                    return
                                rden = sm[:, 72 + 4 * t:76 + 4 * t]
                                v = V.i(V.at(e, V.last).reciprocal(rden, sm[:, 64 + 4 * t:68 + 4 * t]))
                                v = V.i(V.at(v, pv, *st["done"]).tensor_tensor(
                                    OA[:, t, :].rearrange("p (h m) -> p h m", h=4),
                                    PS[:, 2 + t, :].rearrange("p (h m) -> p h m", h=4),
                                    rden.unsqueeze(2).to_broadcast([P, 4, P]), ALU.mult))
                                bank_free[2 + t] = [v]
                                st["oa"] = v

                            tasks.append(dict(ready=rd, scores=sc, n=3 * nk, nsub=1, scale=float(P) ** -0.5, mask=mask,
                                              scfree=st["done"] + [ztr[0]], den=den, denfree=V.last, obank=2 + t, ofirst=h == 0,
                                              pv=[(PS[:, 2 + t, h * P:h * P + P], chunks)], after=after))
                    bg.append(softmax_tasks(tasks))
                else:
                    tick()
            drain()
            xg = to_xt(GG, st["done"], [gc(("hn", l), c) for c in range(4)], 0, 4)
            xo = to_xt(OA, [st["oa"]], [None] * 4, 4, 4)
            sa = sb_ = None
            for t in range(T):
                sa = S.i(S.at(*[st[("z", g)] for g in range(13, 17)]).activation(XN[:, t, :], XN[:, t, :], ACT.Sigmoid))
                sb_ = S.i(S.at().activation(ZB[:, t, :], ZB[:, t, :], ACT.Sigmoid))
            for n in range(2):
                tk = up(("bra", l, n), 512, xg, K=512, k0=0)
                for t in range(T):
                    o = XN[:, t, n * 512:n * 512 + 512]
                    v = V.i(V.at(tk[t], sa, sb_).tensor_tensor(o, PS[:, 4 + t, :], o, ALU.mult))
                    bank_free[4 + t] = [v]
            for n in range(2):
                tk = up(("brb", l, n), 512, xo, K=512, k0=4)
                for t in range(T):
                    o = XN[:, t, n * 512:n * 512 + 512]
                    z = ZB[:, t, n * 512:n * 512 + 512]
                    v = V.i(V.at(tk[t]).tensor_tensor(z, PS[:, 4 + t, :], z, ALU.mult))
                    bank_free[4 + t] = [v]
                    v = V.i(V.at(v).tensor_tensor(o, o, z, ALU.add))
            xy = to_xt(XN, [v], [None] * 8)
            v = out_proj(("out1", l), xy)
            xt = norm_t(("n2", l), [v], [xy[2]])
            d = mlp(("m1", l), False, 4096, xt)
            v = add_x(d)
            xr = [v]
            xn_free = [xt[2]]
            ar_free = [PE.last, v, S.last]

        v = block_norm(dr["final_norm_g"], "ld_f1", X, xr, xn_free)
        xr = [v]

        s_m = sem("ld_m")
        nld = 0
        for l in range(2):
            for j, nm in enumerate(("lambda_q1_2", "lambda_k1_2", "lambda_q2_2", "lambda_k2_2")):
                nc.sync.dma_start(LQ[:, l, j, :], dr[nm][l].partition_broadcast(P)).then_inc(s_m, 16)
                nld += 16
            nc.sync.dma_start(BF[:, l, :], dr["b_forget_2"][l].partition_broadcast(P)).then_inc(s_m, 16)
            nld += 16
        nc.sync.dma_start(RT[:, :].rearrange("p (c e) -> p c e", c=8),
                          dr["router_2"][0].rearrange("(c p) e -> p c e", p=P)).then_inc(s_m, 16)
        ld_m = ("ld_m", s_m, nld + 16)
        NLAM = sm[:, 80:82]
        lp = sm[:, 84:88]
        for l in range(2):
            for j in range(2):
                v = V.i(V.at(ld_m).tensor_tensor(LQ[:, l, 2 * j, :], LQ[:, l, 2 * j, :], LQ[:, l, 2 * j + 1, :], ALU.mult))
                v = V.i(V.at(v).tensor_reduce(lp[:, 2 * l + j:2 * l + j + 1], LQ[:, l, 2 * j, :], AX.X, ALU.add))
        a = S.i(S.at(v).activation(lp, lp, ACT.Exp))
        for l in range(2):
            v = V.i(V.at(a).tensor_scalar(NLAM[:, l:l + 1], lp[:, 2 * l + 1:2 * l + 2], lp[:, 2 * l:2 * l + 1], -LAM_INIT[l],
                                          ALU.subtract, ALU.add))
            v = V.i(V.at(g_all, PE.last).tensor_scalar(gc(("sub", l)), gc(("sub", l)), 1.0 - LAM_INIT[l], None, ALU.mult))
        lam_tok = v
        ra = S.i(S.at(ld_m).copy(RTH[:, :, :], RT[:, :].rearrange("p (c e) -> p c e", c=8)))
        rt_tok = V.i(V.at(ra).tensor_tensor(RTL[:, :, :], RT[:, :].rearrange("p (c e) -> p c e", c=8),
                                            RTH[:, :, :].bitcast(F32), ALU.subtract))
        ar_free = [v, S.last, PE.last]

        def a2(o, n, **k):
            return AR[:, o:o + n]

        QAT = a2(0, 1024).rearrange("p (c m) -> p c m", c=4)
        KAT = a2(1024, 1024).rearrange("p (c m) -> p c m", c=4)
        VA = a2(2048, 1024).rearrange("p (t n) -> p t n", t=2)
        QB = a2(3072, 528).rearrange("p (t h d) -> p t h d", t=2, h=4)
        KB = a2(3600, 528).rearrange("p (t h d) -> p t h d", t=2, h=4)
        QBT = a2(4128, 1024).rearrange("p (h m) -> p h m", h=4)
        KBT = a2(5152, 1024).rearrange("p (h m) -> p h m", h=4)
        VB = a2(6176, 512).rearrange("p (t n) -> p t n", t=2)
        QKC = a2(6688, 1024).rearrange("p (c m) -> p c m", c=4)
        VC = a2(7712, 512).rearrange("p (t n) -> p t n", t=2)
        GC = a2(8224, 512).rearrange("p (t n) -> p t n", t=2)
        RA = a2(8736, 1536).rearrange("p (h n) -> p h n", h=4)
        SQ = a2(10272, 512)
        LF = sm[:, 88:136]
        MIX = XN

        for l in range(2):
            xt = norm_t(("nm", l), xr, [PE.last])
            xtp = xt[2]
            st = {}
            ztr = [None]

            def qk_a(dst, tk, name, rot=False):
                for t in range(T):
                    a = S.i(S.at(tk[t], ztr[0], *ar_free).copy(ZT[:, t, :], PS[:, 4 + t, :]))
                    bank_free[4 + t] = [a]
                v = None
                if rot:
                    for t in range(T):
                        r4 = ZT[:, t, :].rearrange("p (h d) -> p h d", h=8)
                        p1 = OA[:, 0, :].rearrange("p (h d) -> p h d", h=8)
                        p2 = OA[:, 1, :].rearrange("p (h d) -> p h d", h=8)
                        A = rotA[:, t, :].unsqueeze(1).to_broadcast([P, 8, 64])
                        B = rotB[:, t, :].unsqueeze(1).to_broadcast([P, 8, 64])
                        V.i(V.at(a, V.last).tensor_tensor(p1, r4, A, ALU.mult))
                        V.i(nc.vector.tensor_tensor(p2[:, :, 0:32], r4[:, :, 32:64], B[:, :, 0:32], ALU.mult))
                        v = V.i(nc.vector.tensor_tensor(p2[:, :, 32:64], r4[:, :, 0:32], B[:, :, 32:64], ALU.mult))
                        v = V.i(V.at(v).tensor_tensor(r4, p1, p2, ALU.add))
                yield
                tt = turn_heads(lambda t, h: ZT[:, t, h * P:h * P + P], [v, a])
                ztr[0] = tt[-1]
                a = S.i(S.at(tt[0]).copy(dst[:, 0:2, :], PS[:, 6, :].rearrange("p (h m) -> p h m", h=2)))
                v = V.i(V.at(tt[1], *ar_free).tensor_copy(dst[:, 2:4, :], PS[:, 7, :].rearrange("p (h m) -> p h m", h=2)))
                bank_free[6], bank_free[7] = [a], [v]
                st[name] = [a, v]
                yield

            def fox_gate(tk):
                a = None
                for t in range(T):
                    a = S.i(S.at(tk[t], *ar_free).copy(VB[:, t, :], PS[:, 4 + t, 0:256]))
                    v = V.i(V.at(a, ld_m, V.last).tensor_tensor(LF[:, 4 * t:4 * t + 4], PS[:, 4 + t, 256:260], BF[:, l, :], ALU.add))
                    bank_free[4 + t] = [a, v]
                st["vb"] = a
                x, y, z = LF[:, 0:8], LF[:, 8:16], LF[:, 16:24]
                v = V.i(V.at(v).tensor_scalar(y, x, -1.0, None, ALU.mult))
                v = V.i(V.at(v).tensor_tensor(z, x, y, ALU.max))
                v = V.i(V.at(v).tensor_scalar(y, y, 0.0, None, ALU.max))
                a = S.i(S.at(v).activation(z, z, ACT.Exp, scale=-1.0))
                a = S.i(S.at(a).activation(z, z, ACT.Ln, bias=1.0))
                v = V.i(V.at(a).tensor_tensor(y, y, z, ALU.add))
                v = V.i(V.at(v).tensor_scalar(y, y, -1.0, None, ALU.mult))
                st["lf"] = v
                yield
                PE.at(v, *bank_free[7])
                nc.tensor.matmul(PS[:, 7, 0:4], tri, y[:, 0:4], start=True, stop=True)
                nc.tensor.matmul(PS[:, 7, 8:12], ones, y[:, 0:4], start=True, stop=False)
                c = PE.i(nc.tensor.matmul(PS[:, 7, 8:12], tri, y[:, 4:8], start=False, stop=True))
                for t in range(T):
                    cu = PS[:, 7, 8 * t:8 * t + 4].unsqueeze(2)
                    V.i(V.at(c, *ar_free).tensor_scalar(QB[:, t, :, 64:65], cu, 8.0, None, ALU.mult))
                    V.i(nc.vector.tensor_scalar(KB[:, t, :, 65:66], cu, -8.0, None, ALU.mult))
                    V.i(nc.vector.memset(QB[:, t, :, 65:66], 1.0))
                    v = V.i(nc.vector.memset(KB[:, t, :, 64:65], 1.0))
                bank_free[7] = [v]
                st["cum"] = v
                yield

            def qk_b(tk):
                for t in range(T):
                    a = S.i(S.at(tk[t], *ar_free).copy(QB[:, t, :, 0:64], PS[:, 4 + t, 0:256].rearrange("p (h d) -> p h d", h=4)))
                    a = S.i(nc.scalar.copy(KB[:, t, :, 0:64], PS[:, 4 + t, 256:512].rearrange("p (h d) -> p h d", h=4)))
                    bank_free[4 + t] = [a]
                yield
                r = []
                for src, dst in ((QB, QBT), (KB, KBT)):
                    tt = turn_heads(lambda t, h: src[:, t, h, :], [a, st["cum"]], wd=66)
                    a2_ = S.i(S.at(tt[0], *ar_free).copy(dst[0:66, 0:2, :], PS[0:66, 6, :].rearrange("p (h m) -> p h m", h=2)))
                    v2_ = V.i(V.at(tt[1], *ar_free).tensor_copy(dst[0:66, 2:4, :], PS[0:66, 7, :].rearrange("p (h m) -> p h m", h=2)))
                    bank_free[6], bank_free[7] = [a2_], [v2_]
                    r += [a2_, v2_]
                    yield
                st["qkb"] = r

            def soft2(kind, start_free):
                tasks = []
                for t in range(T):
                    nk = (t + 1) * P
                    for pr in range(4 if kind == "diff" else 2):
                        b = len(tasks) % 2
                        den = sm[:, 140 + 2 * b:142 + 2 * b]
                        rd2 = sm[:, 144 + 2 * b:146 + 2 * b]
                        sc, pv = [], []
                        ob = 2 + b
                        for j in range(2):
                            o = PS[:, j, 0:nk] if kind == "diff" else PS[:, 0, j * nk:j * nk + nk]
                            if kind == "diff":
                                r = slice(64 * j, 64 * j + 64)
                                sc.append((o, QAT[r, pr, t * P:t * P + P], KAT[r, pr, 0:nk]))
                                ch = [(j * (t + 1) + kc, VA[:, kc, pr * P:pr * P + P]) for kc in range(t + 1)]
                                pv.append((PS[:, ob, j * P:j * P + P], ch))
                            else:
                                h = 2 * pr + j
                                sc.append((o, QBT[0:66, h, t * P:t * P + P], KBT[0:66, h, 0:nk]))
                                ch = [(j * (t + 1) + kc, VB[:, kc, h * 64:h * 64 + 64]) for kc in range(t + 1)]
                                pv.append((PS[:, ob, j * 64:j * 64 + 64], ch))

                        def mask(s2, nk=nk, t=t):
                            if kind == "diff":
                                return [(s2[:, j * nk:j * nk + nk], PS[:, j, 0:nk], mask2[t]) for j in range(2)]
                            m = mask2[t].unsqueeze(1).to_broadcast([P, 2, nk])
                            return [(s2.rearrange("p (a k) -> p a k", a=2),
                                     PS[:, 0, 0:2 * nk].rearrange("p (a k) -> p a k", a=2), m)]

                        def after(pvt, e, t=t, pr=pr, ob=ob, den=den, rd2=rd2):
                            v = V.i(V.at(e, V.last).reciprocal(rd2, den))
                            if kind == "diff":
                                v = V.i(V.at(v, lam_tok).tensor_tensor(rd2[:, 1:2], rd2[:, 1:2], NLAM[:, l:l + 1], ALU.mult))
                                dst = MIX[:, t, pr * P:pr * P + P]
                                v = V.i(V.at(v, pvt, xtp).tensor_scalar(dst, PS[:, ob, 0:P], rd2[:, 0:1], None, ALU.mult))
                                v = V.i(V.at(v).scalar_tensor_tensor(out=dst, in0=PS[:, ob, P:2 * P], scalar=rd2[:, 1:2],
                                                                     in1=dst, op0=ALU.mult, op1=ALU.add))
                            else:
                                dst = MIX[:, t, 512 + pr * P:512 + pr * P + P].rearrange("p (a d) -> p a d", a=2)
                                v = V.i(V.at(v, pvt, xtp).tensor_tensor(
                                    dst, PS[:, ob, 0:P].rearrange("p (a d) -> p a d", a=2),
                                    rd2.unsqueeze(2).to_broadcast([P, 2, 64]), ALU.mult))
                            bank_free[ob] = [v]
                            st[kind] = v

                        rdy = st["qa"] + st["ka"] + [st["va"]] if kind == "diff" else st["qkb"] + [st["vb"]]
                        tasks.append(dict(ready=rdy, scores=sc, n=2 * nk, nsub=2, scale=0.125, mask=mask,
                                          scfree=start_free, den=den, denfree=V.last, obank=ob, ofirst=True, pv=pv, after=after))
                return softmax_tasks(tasks)

            def diff_norm():
                for t in range(T):
                    m = MIX[:, t, 0:512]
                    a = S.i(S.at(st["diff"], V.last).activation(SQ, m, ACT.Square))
                    r4 = sm[:, 40:44]
                    v = V.i(V.at(a).tensor_reduce(r4, SQ.rearrange("p (h m) -> p h m", h=4), AX.X, ALU.add))
                    v = V.i(V.at(v).tensor_scalar(r4, r4, 1.0 / P, EPS, ALU.mult, ALU.add))
                    a = S.i(S.at(v).activation(r4, r4, ACT.Sqrt))
                    v = V.i(V.at(a).reciprocal(r4, r4))
                    m3 = m.rearrange("p (h m) -> p h m", h=4)
                    v = V.i(V.at(v).tensor_tensor(m3, m3, r4.unsqueeze(2).to_broadcast([P, 4, P]), ALU.mult))
                    yield
                st["dn"] = v

            def retention():
                for h in range(4):
                    b = h % 2
                    r = slice(64 * (h % 2), 64 * (h % 2) + 64)
                    c = h // 2
                    PE.at(*st["qkc"], *bank_free[b])
                    nc.tensor.matmul(PS[:, b, 0:256], QKC[r, 2 + c, 0:128], QKC[r, c, 0:256], start=True, stop=True)
                    tk = PE.i(nc.tensor.matmul(PS[:, b, 256:384], QKC[r, 2 + c, 128:256], QKC[r, c, 128:256], start=True, stop=True))
                    V.i(V.at(tk, *ar_free).tensor_tensor(RA[:, h, 0:256], PS[:, b, 0:256], RD[:, h, :], ALU.mult))
                    v = V.i(nc.vector.tensor_tensor(RA[:, h, 256:384], PS[:, b, 256:384], RD[:, h, 0:128], ALU.mult))
                    bank_free[b] = [v]
                yield
                pv = []
                for t in range(T):
                    PE.at(v, st["vgc"], *bank_free[2 + t])
                    for h in range(4):
                        o = PS[:, 2 + t, h * 64:h * 64 + 64]
                        last = nc.tensor.matmul(o, RA[:, h, t * P:t * P + P], VC[:, 0, h * 64:h * 64 + 64], start=True, stop=t == 0)
                        if t:
                            last = nc.tensor.matmul(o, RA[:, h, 256:384], VC[:, 1, h * 64:h * 64 + 64], start=False, stop=True)
                    pv.append(PE.i(last))
                yield
                for t in range(T):
                    o3 = PS[:, 2 + t, 0:256].rearrange("p (h d) -> p h d", h=4)
                    m3 = MIX[:, t, 768:1024].rearrange("p (h d) -> p h d", h=4)
                    r4 = sm[:, 148:152]
                    v = V.i(V.at(pv[t], V.last).tensor_reduce(r4, o3, AX.X, ALU.add))
                    v = V.i(V.at(v).tensor_scalar(r4, r4, 1.0 / 64, None, ALU.mult))
                    v = V.i(V.at(v, xtp).tensor_tensor(m3, o3, r4.unsqueeze(2).to_broadcast([P, 4, 64]), ALU.subtract))
                    bank_free[2 + t] = [v]
                    q3 = SQ[:, 0:256].rearrange("p (h d) -> p h d", h=4)
                    a = S.i(S.at(v).activation(q3, m3, ACT.Square))
                    v = V.i(V.at(a, V.last).tensor_reduce(r4, q3, AX.X, ALU.add))
                    v = V.i(V.at(v).tensor_scalar(r4, r4, 1.0 / 64, EPS, ALU.mult, ALU.add))
                    a = S.i(S.at(v).activation(r4, r4, ACT.Sqrt))
                    v = V.i(V.at(a).reciprocal(r4, r4))
                    v = V.i(V.at(v).tensor_tensor(m3, m3, r4.unsqueeze(2).to_broadcast([P, 4, 64]), ALU.mult))
                    v = V.i(V.at(v, st["vgc"]).tensor_tensor(MIX[:, t, 768:1024], MIX[:, t, 768:1024], GC[:, t, :], ALU.mult))
                    yield
                st["ret"] = v

            def chain(*gens):
                for g in gens:
                    yield from g()

            tk = up(("in2", l, "qa"), 512, xt)
            bg.append(qk_a(QAT, tk, "qa"))
            tick()
            tk = up(("in2", l, "ka"), 512, xt)
            bg.append(qk_a(KAT, tk, "ka"))
            tick()
            tk = up(("in2", l, "va"), 512, xt)
            for t in range(T):
                a = S.i(S.at(tk[t], *ar_free).copy(VA[:, t, :], PS[:, 4 + t, :]))
                bank_free[4 + t] = [a]
            st["va"] = a
            drain()
            tk = up(("in2", l, "vf"), 260, xt)
            bg.append(fox_gate(tk))
            drain()
            tk = up(("in2", l, "qkb"), 512, xt)
            bg.append(qk_b(tk))
            drain()
            tk = up(("in2", l, "qkc"), 512, xt)
            bg.append(qk_a(QKC, tk, "qkc", rot=True))
            drain()

            def seq():
                yield from soft2("diff", [ztr[0], V.last, S.last])
                yield from soft2("fox", [PE.last, V.last, S.last])
                yield from diff_norm()

            bg.append(seq())
            tick()
            tk = up(("in2", l, "vgc"), 512, xt)
            for t in range(T):
                a = S.i(S.at(tk[t], *ar_free).copy(VC[:, t, :], PS[:, 4 + t, 0:256]))
                a = S.i(nc.scalar.activation(GC[:, t, :], PS[:, 4 + t, 256:512], ACT.Silu))
                bank_free[4 + t] = [a]
            st["vgc"] = a
            drain()
            bg.append(retention())
            drain()
            gains = [gc(("sub", l))] * 4 + [None] * 2 + [gc(("rg", l), 0), gc(("rg", l), 1)]
            xy = to_xt(MIX, [st["dn"], st["fox"], st["ret"]], gains)
            v = out_proj(("out2", l), xy)
            xt = norm_t(("nf", l), [v], [xy[2]])
            if l == 0:
                d = mlp(("m2", 0), True, FF2, xt)
            else:
                combs = []
                for t in range(T):
                    PE.at(rt_tok, *xt, *bank_free[7])
                    for k in range(8):
                        last = mm3(PS[:, 7, 8 * t:8 * t + 8], XTH[:, k, t * P:t * P + P], XTL[:, k, t * P:t * P + P],
                                   RTH[:, k, :], RTL[:, k, :], k == 0, k == 7)
                    tk = PE.i(last)
                    lg, mx, gt = sm[:, 152:160], sm[:, 160:168], sm[:, 168:176]
                    f8, oh = sm[:, 176:184], sm[:, 184:192]
                    cm = sm[:, 192 + 8 * t:200 + 8 * t]
                    v = V.i(V.at(tk, V.last).tensor_copy(lg, PS[:, 7, 8 * t:8 * t + 8]))
                    bank_free[7] = [v]
                    v = V.i(V.at(v).max(mx, lg))
                    v = V.i(V.at(v).max_index(idx[:, t, :], mx, lg))
                    v = V.i(V.at(v).tensor_copy(f8, idx[:, t, :]))
                    v = V.i(V.at(v).tensor_tensor(gt[:, 0:1], mx[:, 1:2], mx[:, 0:1], ALU.subtract))
                    a = S.i(S.at(v).activation(gt[:, 1:2], gt[:, 0:1], ACT.Exp))
                    v = V.i(V.at(a).tensor_scalar(gt[:, 2:3], gt[:, 1:2], 1.0, None, ALU.add))
                    v = V.i(V.at(v).reciprocal(gt[:, 2:3], gt[:, 2:3]))
                    v = V.i(V.at(v).tensor_tensor(gt[:, 3:4], gt[:, 1:2], gt[:, 2:3], ALU.mult))
                    v = V.i(V.at(v).tensor_scalar(cm, iota8, f8[:, 0:1], gt[:, 2:3], ALU.is_equal, ALU.mult))
                    v = V.i(V.at(v).tensor_scalar(oh, iota8, f8[:, 1:2], gt[:, 3:4], ALU.is_equal, ALU.mult))
                    v = V.i(V.at(v).tensor_tensor(cm, cm, oh, ALU.add))
                    combs.append(cm)
                V.at(v)
                for e in range(NE):
                    d = mlp(("moe", e), True, FE, xt, comb=[c[:, e:e + 1] for c in combs],
                            first=e == 0, final=e == NE - 1)
            v = add_x(d)
            xt = norm_t(("pn", l), [v], [xt[2]])
            PP = AR[:, 0:512].rearrange("p (t n) -> p t n", t=2)
            SGT = AR[:, 2048:4096].rearrange("p (t n) -> p t n", t=2)
            s_p = sem(f"ld_p{l}")
            SP.at(PE.last, V.last, S.last)
            nc.sync.dma_start(PP, dr["p_2"][l, 0].rearrange("(t p) n -> p t n", p=P)).then_inc(s_p, 16)
            pt = to_xt(PP, [(f"ld_p{l}", s_p, 16)], [None] * 2, 0, 2, dst=(HTH, HTL))
            d = down(("pp", l), 256, HTH, HTL, pt, True, True)
            for n in range(2):
                tk = up(("pg", l, n), 512, xt)
                for t in range(T):
                    sg = SGT[:, t, n * 512:n * 512 + 512]
                    xo = X[:, t, n * 512:n * 512 + 512]
                    a = S.i(S.at(tk[t], pt[0], V.last).activation(sg, PS[:, 4 + t, :], ACT.Sigmoid))
                    bank_free[4 + t] = [a]
                    v = V.i(V.at(a, d).tensor_tensor(sg, PS[:, 2 * t + n, :], sg, ALU.mult))
                    bank_free[2 * t + n] = [v]
                    v = V.i(V.at(v).tensor_tensor(xo, xo, sg, ALU.add))
            xr = [v]
            ar_free = [PE.last, v, S.last]

        v = block_norm(dr["final_norm_2"], "ld_f2", XN, xr, [PE.last])
        s_o = sem("s_out")
        SP.at(v)
        nc.sync.dma_start(out[0].rearrange("(t p) d -> p t d", p=P), XN[:, :, :]).then_inc(s_o, 16)
        nc.sync.wait_ge(s_o, 16)


def constants():
    i = np.arange(128)
    cf = np.zeros((128, 776 + 1024), np.float32)
    cf[:, 0:128] = np.eye(128)
    cf[:, 128:256] = i[:, None] <= i[None, :]
    cf[:, 256:384] = 1.0
    pos = np.arange(256, dtype=np.float32)
    f1 = (np.float32(500000.0) ** (-np.arange(0, 32, 2, dtype=np.float32) / np.float32(32))).astype(np.float32)
    a1 = (pos[:, None] * f1[None, :]).astype(np.float32).astype(np.float64)
    f2 = (np.float32(10000.0) ** (-np.arange(32, dtype=np.float32) / np.float32(32))).astype(np.float32)
    a2 = (pos[:, None] * f2[None, :]).astype(np.float32).astype(np.float64)
    for o, w, ang in ((384, 32, a1), (512, 64, a2)):
        A = np.concatenate([np.cos(ang), np.cos(ang)], 1).astype(np.float32).reshape(2, 128, w)
        B = np.concatenate([-np.sin(ang), np.sin(ang)], 1).astype(np.float32).reshape(2, 128, w)
        cf[:, o:o + 2 * w] = A.transpose(1, 0, 2).reshape(128, 2 * w)
        cf[:, o + 2 * w:o + 4 * w] = B.transpose(1, 0, 2).reshape(128, 2 * w)
    cf[:, 768:776] = np.arange(8)
    lg = np.log1p(-np.exp2(-5.0 - np.arange(4)))
    d = np.arange(256)[None, :] - i[:, None]
    for h in range(4):
        cf[:, 776 + 256 * h:776 + 256 * h + 256] = np.where(d >= 0, np.exp(np.maximum(d, 0) * lg[h]), 0.0) * 0.125
    neg = -1e30
    cb = np.zeros((128, 1408), np.float32)
    for t in range(2):
        q = t * 128 + i[:, None]
        k = np.arange((t + 1) * 128)[None, :]
        for g, (w, dil) in enumerate(((128, 1), (512, 4), (2048, 16))):
            ok = (k <= q) & (q - k <= w) & ((q - k) % dil == 0)
            o = g * 128 if t == 0 else 384 + g * 256
            cb[:, o:o + (t + 1) * 128] = np.where(ok, 0.0, neg)
    cb[:, 1152:1408] = np.where(np.arange(256)[None, :] <= 128 + i[:, None], 0.0, neg)
    ci = np.zeros((128, 1024), np.float32)
    s, t = i[:, None], i[None, :]
    for li, m in enumerate(LEVELS):
        if m == 0:
            ok = s == t
        else:
            ok = (s // (2 * m) == t // (2 * m)) & ((s // m) % 2 == 0) & ((t // m) % 2 == 1)
        ci[:, li * 128:li * 128 + 128] = ok
    return cf, cb, ci


_INS = ["x", "norm1_g", "w_in", "hg_lower_bounds", "hg_norm_g", "w_branch_a", "w_branch_b", "w_out", "norm2_g", "w_up",
        "w_down", "final_norm_g", "p_2", "norm_mix_2", "w_in_2", "b_forget_2", "lambda_q1_2", "lambda_k1_2",
        "lambda_q2_2", "lambda_k2_2", "diff_subln_2", "ret_gn_2", "w_out_2", "norm_ffn_2", "dense_w_gate_2",
        "dense_w_up_2", "dense_w_down_2", "router_2", "moe_w_gate_2", "moe_w_up_2", "moe_w_down_2", "ple_norm_2",
        "ple_gate_2", "ple_proj_2", "final_norm_2"]


def kernel(**inputs):
    from concourse import bacc as _bacc
    from concourse.bass_utils import run_bass_kernel_spmd as _run

    nc = _bacc.Bacc("TRN2", target_bir_lowering=False, num_devices=1)
    arrays, dr = {}, {}
    for name in _INS:
        a = np.ascontiguousarray(inputs[name])
        arrays[f"in_{name}"] = a
        dr[name] = nc.dram_tensor(f"in_{name}", a.shape, mybir.dt.from_np(a.dtype), kind="ExternalInput").ap()
    cs = []
    for name, a in zip(("cf", "cb", "ci"), constants()):
        arrays[f"const_{name}"] = a
        cs.append(nc.dram_tensor(f"const_{name}", a.shape, mybir.dt.from_np(a.dtype), kind="ExternalInput").ap())
    o = nc.dram_tensor("out_0", (1, 256, 1024), F32, kind="ExternalOutput").ap()
    program(nc, dr, cs[0], cs[1], cs[2], o)
    r = _run(nc, [arrays], core_ids=[0])
    return r.results[0]["out_0"]
```

```python
import numpy as np
import concourse.bass as bass
from concourse import mybir
from contextlib import ExitStack

F32 = mybir.dt.float32
F32R = mybir.dt.float32r
BF16 = mybir.dt.bfloat16
I8 = mybir.dt.int8
U32 = mybir.dt.uint32
ALU = mybir.AluOpType
ACT = mybir.ActivationFunctionType
AX = mybir.AxisListType

P = 128
T = 2
D = 1024
EPS = 1e-6
RAW = 5
WR = 3
LAM_INIT = [0.8 - 0.6 * float(np.exp(-0.3 * i)) for i in range(2)]
FF2, FE, NE = 2816, 3584, 8
A0 = 2048
LEVELS = [0, 1, 2, 4, 8, 16, 32, 64]


class Eng:

    def __init__(self, e, sem):
        self.e, self.sem, self.n, self.seen = e, sem, 0, {}

    def at(self, *toks):
        for tok in toks:
            if tok is None:
                continue
            key, sem, val = tok
            if self.seen.get(key, 0) < val:
                self.seen[key] = val
                self.e.wait_ge(sem, val)
        return self.e

    def i(self, ins):
        ins.then_inc(self.sem, 1)
        self.n += 1
        return (self.sem.name, self.sem, self.n)

    @property
    def last(self):
        return (self.sem.name, self.sem, self.n) if self.n else None


def plan(dr):
    out = []

    def rows(w, kp, c0, n):
        return w[kp * 512:kp * 512 + 512, c0:c0 + n].rearrange("(k p) n -> p k n", p=P)

    def up(key, w, c0, n, K=D):
        for kp in range(K // 512):
            out.append(((key, kp), rows(w, kp, c0, n), 4, n))

    def down(key, w, r0, K):
        for kp in range(K // 256):
            out.append(((key, kp), w[r0 + kp * 256:r0 + kp * 256 + 256, :].rearrange("(k p) n -> p k n", p=P), 2, D))

    def mlp(key, gate, upw, dn, F):
        ng = -(-F // 512)
        for n in range(ng + 1):
            w = min(512, F - n * 512)
            if n < ng:
                if gate is not None:
                    up((key, "g", n), gate, n * 512, w)
                up((key, "u", n), upw, n * 512, w)
            if n:
                down((key, "d", n - 1), dn, (n - 1) * 512, min(512, F - (n - 1) * 512))

    for l in range(2):
        for g in range(17):
            up(("in1", l, g), dr["w_in"][l], g * 512, 512)
        for br in ("a", "b"):
            for n in range(2):
                up(("br" + br, l, n), dr["w_branch_" + br][l], n * 512, 512, 512)
        for n in range(2):
            up(("out1", l, n), dr["w_out"][l], n * 512, 512)
        mlp(("m1", l), None, dr["w_up"][l], dr["w_down"][l], 4096)
    for l in range(2):
        for name, c0, n in (("qa", 0, 512), ("ka", 512, 512), ("va", 1024, 512), ("vf", 2048, 260),
                            ("qkb", 1536, 512), ("qkc", 2308, 512), ("vgc", 2820, 512)):
            up(("in2", l, name), dr["w_in_2"][l], c0, n)
        for n in range(2):
            up(("out2", l, n), dr["w_out_2"][l], n * 512, 512)
        if l == 0:
            mlp(("m2", 0), dr["dense_w_gate_2"][0], dr["dense_w_up_2"][0], dr["dense_w_down_2"][0], FF2)
        else:
            gr = [(e, n) for e in range(NE) for n in range(FE // 512)]
            for i in range(len(gr) + 1):
                if i < len(gr):
                    e, n = gr[i]
                    up(("moe", "g", e, n), dr["moe_w_gate_2"][0, e], n * 512, 512)
                    up(("moe", "u", e, n), dr["moe_w_up_2"][0, e], n * 512, 512)
                if i:
                    e, n = gr[i - 1]
                    down(("moe", "d", e, n), dr["moe_w_down_2"][0, e], n * 512, 512)
        down(("pp", l), dr["ple_proj_2"][l], 0, 256)
        for n in range(2):
            up(("pg", l, n), dr["ple_gate_2"][l], n * 512, 512)
    return out


def program(nc, dr, cf, cb, ci, out):
    ctx = ExitStack()
    with ctx:
        def sb(name, shape, dt=F32):
            return ctx.enter_context(nc.sbuf_tensor(name, shape, dt))

        def sem(name):
            return ctx.enter_context(nc.semaphore(name))

        PS = ctx.enter_context(nc.psum_tensor("PS", [P, 8, 512], F32))
        raw = sb("raw", [P, RAW, 2048])
        WH = sb("WH", [P, WR, 2048], F32R)
        WL = sb("WL", [P, WR, 2048], F32R)
        XTH = sb("XTH", [P, 8, 256], F32R)
        XTL = sb("XTL", [P, 8, 256], F32R)
        HTH = sb("HTH", [P, 4, 256], F32R)
        HTL = sb("HTL", [P, 4, 256], F32R)
        RTH = sb("RTH", [P, 8, 8], F32R)
        RTL = sb("RTL", [P, 8, 8], F32R)
        X = sb("X", [P, T, D])
        XN = sb("XN", [P, T, D])
        AR = sb("AR", [P, 16384])
        CF = sb("CF", [P, cf.shape[1]])
        CB = sb("CB", [P, cb.shape[1]], BF16)
        CI = sb("CI", [P, ci.shape[1]], I8)
        G = sb("G", [P, 128])
        GR = sb("GR", [P, 128])
        sm = sb("sm", [P, 256])
        RT = sb("RT", [P, 64])
        LQ = AR[:, 8192:8704].rearrange("p (l j d) -> p l j d", l=2, j=4)
        BF = sb("BF", [P, 2, 4])
        sm2 = sb("sm2", [P, 64])
        CNT = sb("CNT", [P, 1], mybir.dt.int32)
        idx = sb("idx", [P, 2, 8], U32)

        PE = Eng(nc.tensor, sem("s_pe"))
        V = Eng(nc.vector, sem("s_v"))
        S = Eng(nc.scalar, sem("s_s"))
        GP = Eng(nc.gpsimd, sem("s_g"))
        SP = Eng(nc.sync, sem("s_sp"))

        ident = CF[:, 0:128]
        tri = CF[:, 128:256]
        ones = CF[:, 256:384]
        ropeA = CF[:, 384:448].rearrange("p (t d) -> p t d", t=2)
        ropeB = CF[:, 448:512].rearrange("p (t d) -> p t d", t=2)
        rotA = CF[:, 512:640].rearrange("p (t d) -> p t d", t=2)
        rotB = CF[:, 640:768].rearrange("p (t d) -> p t d", t=2)
        iota = CF[:, 1800:1928]
        RD = CF[:, 776:776 + 1024].rearrange("p (h t) -> p h t", h=4)
        mask1 = [CB[:, 0:384].rearrange("p (g k) -> p g k", g=3), CB[:, 384:1152].rearrange("p (g k) -> p g k", g=3)]
        mask2 = [CB[:, 0:128], CB[:, 1152:1408]]
        hmask = [CI[:, i * 128:(i + 1) * 128] for i in range(8)]

        def small(name, pairs):
            s = sem(name)
            for a, b in pairs:
                nc.sync.dma_start(a, b).then_inc(s, 16)
            return (name, s, 16 * len(pairs))

        ld_x = small("ld_x", [(X[:, :, :], dr["x"][0].rearrange("(t p) d -> p t d", p=P))])
        rows, pairs = {}, []

        def grow(key, ap, n):
            k = sum(v[1] for v in rows.values())
            rows[key] = (k, n)
            pairs.append((GR[k:k + n, :], ap.rearrange("(c p) -> c p", p=P)))

        for l in range(2):
            grow(("n1", l), dr["norm1_g"][l], 8)
            grow(("n2", l), dr["norm2_g"][l], 8)
            grow(("nm", l), dr["norm_mix_2"][l], 8)
            grow(("nf", l), dr["norm_ffn_2"][l], 8)
            grow(("pn", l), dr["ple_norm_2"][l], 8)
            grow(("hb", l), dr["hg_lower_bounds"][l], 4)
            grow(("hn", l), dr["hg_norm_g"][l], 4)
            grow(("sub", l), dr["diff_subln_2"][l], 1)
            grow(("rg", l), dr["ret_gn_2"][l], 2)
        NG = sum(v[1] for v in rows.values())
        ld_c = small("ld_c", [(CF[:, :], cf), (AR[:, 1024:2432], cb), (AR[:, 0:1024], ci)])
        ld_g = small("ld_g", pairs)

        PIECES = plan(dr)
        dsem = [sem(f"ld_w{i}") for i in range(RAW)]
        raw_free = [[] for _ in range(RAW)]
        loaded, split_tok, pe_done = [], [], []

        def load():
            i = len(loaded)
            if i >= len(PIECES):
                return
            _, src, nb, n = PIECES[i]
            s = i % RAW
            SP.at(*raw_free[s])
            nc.sync.dma_start(raw[:, s, 0:nb * n].rearrange("p (k n) -> p k n", k=nb), src).then_inc(dsem[s], 16)
            loaded.append((f"ld_w{s}", dsem[s], 16 * (i // RAW + 1)))

        def split():
            i = len(split_tok)
            if i >= len(PIECES):
                return
            _, _, nb, n = PIECES[i]
            s, w, m = i % RAW, i % WR, nb * n
            free = pe_done[i - WR] if i >= WR else None
            a = S.i(S.at(loaded[i], free).copy(WH[:, w, 0:m], raw[:, s, 0:m]))
            b = V.i(V.at(loaded[i], a, free).tensor_tensor(WL[:, w, 0:m], raw[:, s, 0:m],
                                                           WH[:, w, 0:m].bitcast(F32), ALU.subtract))
            split_tok.append(b)
            raw_free[s] = [a, b]
            load()

        for _ in range(RAW):
            load()

        bg = []

        def tick():
            for g in list(bg):
                try:
                    next(g)
                except StopIteration:
                    bg.remove(g)

        def drain():
            while bg:
                tick()

        def take(key):
            i = len(pe_done)
            assert PIECES[i][0] == key, (PIECES[i][0], key)
            while len(split_tok) < min(i + WR, len(PIECES)):
                split()
            PE.at(split_tok[i])
            _, _, nb, n = PIECES[i]
            w = i % WR
            return [f[:, w, 0:nb * n].rearrange("p (k n) -> p k n", k=nb) for f in (WH, WL)]

        bank_free = [[] for _ in range(8)]

        def mm3(o, lh, ll, rh, rl, start, stop):
            nc.tensor.matmul(o, lh, rh, start=start, stop=False, skip_group_check=True)
            nc.tensor.matmul(o, lh, rl, start=False, stop=False, skip_group_check=True)
            return nc.tensor.matmul(o, ll, rh, start=False, stop=stop, skip_group_check=True)

        def up(key, n, ready, K=D, k0=0, banks=(4, 5), mid=None):
            nk = K // 512
            toks = [None, None]
            PE.at(*ready)
            for kp in range(nk):
                wh, wl = take((key, kp))
                for t in range(T):
                    if kp == 0:
                        PE.at(*bank_free[banks[t]])
                    for k in range(4):
                        kk = k0 + kp * 4 + k
                        last = mm3(PS[:, banks[t], 0:n], XTH[:, kk, t * P:t * P + P], XTL[:, kk, t * P:t * P + P],
                                   wh[:, k, :], wl[:, k, :], kp == 0 and k == 0, kp == nk - 1 and k == 3)
                    if kp == nk - 1 or t == 1:
                        toks[t] = PE.i(last)
                pe_done.append(PE.last)
                if kp < nk - 1:
                    if mid is not None:
                        mid()
                    tick()
            return toks

        def down(key, K, lh, ll, ready, first, final):
            PE.at(*ready)
            if first:
                PE.at(*bank_free[0], *bank_free[1], *bank_free[2], *bank_free[3])
            nk = K // 256
            for kp in range(nk):
                wh, wl = take((key, kp))
                for t in range(T):
                    for j in range(2):
                        for k in range(2):
                            kk = kp * 2 + k
                            last = mm3(PS[:, 2 * t + j, :], lh[:, kk, t * P:t * P + P], ll[:, kk, t * P:t * P + P],
                                       wh[:, k, j * 512:j * 512 + 512], wl[:, k, j * 512:j * 512 + 512],
                                       first and kk == 0, final and kk == 2 * nk - 1)
                pe_done.append(PE.i(last))
                tick()
            return PE.last

        PE.at(ld_c, ld_g)
        t0 = PE.i(nc.tensor.transpose(PS[:, 7, 0:NG], GR[0:NG, :], ident[0:NG, 0:NG]))
        g_all = V.i(V.at(t0).tensor_copy(G[:, 0:NG], PS[:, 7, 0:NG]))
        bank_free[7] = [g_all]
        S.at(ld_c)
        V.i(V.at(ld_c).tensor_copy(CB[:, :], AR[:, 1024:2432]))
        ci_tok = V.i(V.at(ld_c).tensor_copy(CI[:, :], AR[:, 0:1024]))

        def gc(key, c=0, n=1):
            return G[:, rows[key][0] + c:rows[key][0] + c + n]

        LB = sm[:, 0:4]
        OMB = sm[:, 4:8]
        lt = sm[:, 8:32]
        a = V.i(V.at(g_all).tensor_tensor(lt[:, 0:4], gc(("hb", 0), 0, 4), gc(("hb", 1), 0, 4), ALU.max))
        a = V.i(V.at(a).tensor_tensor(lt[:, 4:8], gc(("hb", 0), 0, 4), lt[:, 0:4], ALU.subtract))
        a = V.i(V.at(a).tensor_tensor(lt[:, 8:12], gc(("hb", 1), 0, 4), lt[:, 0:4], ALU.subtract))
        a = S.i(S.at(a).activation(lt[:, 12:20], lt[:, 4:12], ACT.Exp))
        a = V.i(V.at(a).tensor_tensor(lt[:, 20:24], lt[:, 12:16], lt[:, 16:20], ALU.add))
        a = V.i(V.at(a).reciprocal(lt[:, 20:24], lt[:, 20:24]))
        a = V.i(V.at(a).tensor_tensor(LB, lt[:, 16:20], lt[:, 20:24], ALU.mult))
        lb_tok = V.i(V.at(a).tensor_scalar(OMB, LB, -1.0, 1.0, ALU.mult, ALU.add))

        ss = sm[:, 32:34]
        rs = sm[:, 34:36]

        def rstd(xready, xn_free):
            a = None
            for t in range(T):
                a = S.i(S.at(*xready, *xn_free, V.last).activation(XN[:, t, :], X[:, t, :], ACT.Square,
                                                                   accum_out=ss[:, t:t + 1]))
            a = V.i(V.at(a).tensor_scalar(rs, ss, 1.0 / D, EPS, ALU.mult, ALU.add))
            a = S.i(S.at(a).activation(rs, rs, ACT.Sqrt))
            return V.i(V.at(a).reciprocal(rs, rs))

        def to_xt(src, ready, gains, c0=0, nch=8, dst=None):
            dh, dl = dst if dst is not None else (XTH, XTL)
            wr = []
            pe_last = PE.last
            for r in range(nch // 2):
                b = 4 + r % 4
                PE.at(*ready, *bank_free[b])
                for c in range(2):
                    for t in range(T):
                        cc = 2 * r + c
                        last = nc.tensor.transpose(PS[:, b, c * 256 + t * P:c * 256 + t * P + P],
                                                   src[:, t, cc * P:cc * P + P], ident)
                tp = PE.i(last)
                for c in range(2):
                    cc = 2 * r + c
                    pv = PS[:, b, c * 256:c * 256 + 256]
                    if gains[cc] is None:
                        a = S.i(S.at(tp, pe_last).copy(dh[:, c0 + cc, :], pv))
                    else:
                        a = S.i(S.at(tp, pe_last, g_all).activation(dh[:, c0 + cc, :], pv, ACT.Copy, scale=gains[cc]))
                for c in range(2):
                    cc = 2 * r + c
                    pv = PS[:, b, c * 256:c * 256 + 256]
                    dhf = dh[:, c0 + cc, :].bitcast(F32)
                    if gains[cc] is None:
                        v = V.i(V.at(a, tp, pe_last).tensor_tensor(dl[:, c0 + cc, :], pv, dhf, ALU.subtract))
                    else:
                        v = V.i(V.at(a, tp, pe_last).scalar_tensor_tensor(
                            out=dl[:, c0 + cc, :], in0=pv, scalar=gains[cc], in1=dhf, op0=ALU.mult, op1=ALU.subtract))
                wr += [a, v]
                bank_free[b] = [a, v]
            return [wr[-2], wr[-1], tp]

        def norm_t(key, xready, xn_free):
            r = rstd(xready, xn_free)
            for t in range(T):
                a = V.i(V.at(r).tensor_scalar(XN[:, t, :], X[:, t, :], rs[:, t:t + 1], None, ALU.mult))
            return to_xt(XN, [a], [gc(key, c) for c in range(8)])

        def block_norm(gain_dram, name, dst, xready, xn_free):
            gb = AR[:, 0:1024]
            s = sem(name)
            SP.at(*xready, PE.last, V.last, S.last)
            nc.sync.dma_start(gb, gain_dram.partition_broadcast(P)).then_inc(s, 16)
            r = rstd(xready, xn_free)
            for t in range(T):
                a = V.i(V.at(r, (name, s, 16)).scalar_tensor_tensor(
                    out=dst[:, t, :], in0=X[:, t, :], scalar=rs[:, t:t + 1], in1=gb, op0=ALU.mult, op1=ALU.mult))
            return a

        HM = AR[:, 15360:16384].rearrange("p (t n) -> p t n", t=2)

        def mlp(key, gated, F, ready, comb=None, first=True, final=True):
            ng = -(-F // 512)
            hm_tok = ht_tok = None
            tr_last = [None]
            for n in range(ng + 1):
                w = min(512, F - n * 512)
                state = {}

                def turn(n=n):
                    wp = min(512, F - (n - 1) * 512)
                    toks = []
                    pd = PE.last
                    for r in range(wp // 256):
                        b = 6 + r
                        PE.at(*hm_tok, *bank_free[b])
                        for c in range(2):
                            for t in range(T):
                                last = nc.tensor.transpose(PS[:, b, c * 256 + t * P:c * 256 + t * P + P],
                                                           HM[:, t, (2 * r + c) * P:(2 * r + c) * P + P], ident)
                        tp = PE.i(last)
                        pv = PS[:, b, :].rearrange("p (c m) -> p c m", c=2)
                        a = S.i(S.at(tp, pd).copy(HTH[:, 2 * r:2 * r + 2, :], pv))
                        v = V.i(V.at(a, tp, pd).tensor_tensor(HTL[:, 2 * r:2 * r + 2, :], pv,
                                                              HTH[:, 2 * r:2 * r + 2, :].bitcast(F32), ALU.subtract))
                        bank_free[b] = [a, v]
                        toks += [a, v]
                    state["ht"] = toks
                    tr_last[0] = PE.last

                if n < ng:
                    if gated:
                        tg = up((key, "g", n), w, ready, mid=turn if n else None)
                        sil = []
                        for t in range(T):
                            a = S.i(S.at(tg[t], tr_last[0], V.last if n == 0 else None).activation(
                                HM[:, t, 0:w], PS[:, 4 + t, 0:w], ACT.Silu))
                            bank_free[4 + t] = [a]
                            sil.append(a)
                        tick()
                        tu = up((key, "u", n), w, ready)
                        new = []
                        for t in range(T):
                            if comb is None:
                                v = V.i(V.at(tu[t], sil[t]).tensor_tensor(HM[:, t, 0:w], PS[:, 4 + t, 0:w],
                                                                          HM[:, t, 0:w], ALU.mult))
                            else:
                                v = V.i(V.at(tu[t], sil[t]).scalar_tensor_tensor(
                                    out=HM[:, t, 0:w], in0=PS[:, 4 + t, 0:w], scalar=comb[t], in1=HM[:, t, 0:w],
                                    op0=ALU.mult, op1=ALU.mult))
                            bank_free[4 + t] = [v]
                            new.append(v)
                    else:
                        tu = up((key, "u", n), w, ready, mid=turn if n else None)
                        new = []
                        for t in range(T):
                            a = S.i(S.at(tu[t], tr_last[0], V.last if n == 0 else None).activation(
                                HM[:, t, 0:w], PS[:, 4 + t, 0:w], ACT.Relu))
                            v = V.i(V.at(a).scalar_tensor_tensor(out=HM[:, t, 0:w], in0=PS[:, 4 + t, 0:w], scalar=0.0,
                                                                 in1=HM[:, t, 0:w], op0=ALU.max, op1=ALU.mult))
                            bank_free[4 + t] = [v]
                            new.append(v)
                    hm_next = new
                    tick()
                else:
                    turn()
                if n:
                    d = down((key, "d", n - 1), min(512, F - (n - 1) * 512), HTH, HTL, state["ht"],
                             first and n == 1, final and n == ng)
                hm_tok = hm_next
            return d

        def add_x(tok):
            r = []
            for t in range(T):
                for j in range(2):
                    v = V.i(V.at(tok).tensor_tensor(X[:, t, j * 512:j * 512 + 512], PS[:, 2 * t + j, :],
                                                    X[:, t, j * 512:j * 512 + 512], ALU.add))
                    bank_free[2 * t + j] = [v]
            return v

        def out_proj(key, ready):
            for n in range(2):
                tk = up((key[0], key[1], n), 512, ready)
                for t in range(T):
                    v = V.i(V.at(tk[t]).tensor_tensor(X[:, t, n * 512:n * 512 + 512], PS[:, 4 + t, :],
                                                      X[:, t, n * 512:n * 512 + 512], ALU.add))
                    bank_free[4 + t] = [v]
                tick()
            return v


        SEL = sm2[:, 0:16]
        SLOT = sm2[:, 16:32]
        SLOT2 = sm2[:, 32:48]
        COMB = sm2[:, 48:64]

        def moe(xt):
            for t in range(T):
                PE.at(rt_tok, *xt, *bank_free[7])
                for k in range(8):
                    last = mm3(PS[:, 7, 8 * t:8 * t + 8], XTH[:, k, t * P:t * P + P], XTL[:, k, t * P:t * P + P],
                               RTH[:, k, :], RTL[:, k, :], k == 0, k == 7)
                tk = PE.i(last)
                lg, mx, gt = sm[:, 152:160], sm[:, 160:168], sm[:, 168:176]
                f8, oh = sm[:, 176:184], sm[:, 184:192]
                cm, sel = COMB[:, 8 * t:8 * t + 8], SEL[:, 8 * t:8 * t + 8]
                v = V.i(V.at(tk, V.last).tensor_copy(lg, PS[:, 7, 8 * t:8 * t + 8]))
                bank_free[7] = [v]
                v = V.i(V.at(v).max(mx, lg))
                v = V.i(V.at(v).max_index(idx[:, t, :], mx, lg))
                v = V.i(V.at(v).tensor_copy(f8, idx[:, t, :]))
                v = V.i(V.at(v).tensor_tensor(gt[:, 0:1], mx[:, 1:2], mx[:, 0:1], ALU.subtract))
                a = S.i(S.at(v).activation(gt[:, 1:2], gt[:, 0:1], ACT.Exp))
                v = V.i(V.at(a).tensor_scalar(gt[:, 2:3], gt[:, 1:2], 1.0, None, ALU.add))
                v = V.i(V.at(v).reciprocal(gt[:, 2:3], gt[:, 2:3]))
                v = V.i(V.at(v).tensor_tensor(gt[:, 3:4], gt[:, 1:2], gt[:, 2:3], ALU.mult))
                V.i(V.at(v).tensor_scalar(sel, iota[:, 0:8], f8[:, 0:1], None, ALU.is_equal))
                v = V.i(V.at(v).tensor_scalar(oh, iota[:, 0:8], f8[:, 1:2], None, ALU.is_equal))
                V.i(V.at(v).tensor_scalar(cm, sel, gt[:, 2:3], None, ALU.mult))
                v = V.i(V.at(v).tensor_tensor(sel, sel, oh, ALU.add))
                v = V.i(V.at(v).scalar_tensor_tensor(out=cm, in0=oh, scalar=gt[:, 3:4], in1=cm, op0=ALU.mult, op1=ALU.add))
            PE.at(v)
            nc.tensor.matmul(PS[:, 7, 0:8], tri, SEL[:, 0:8], start=True, stop=True)
            nc.tensor.matmul(PS[:, 7, 8:16], ones, SEL[:, 0:8], start=True, stop=False)
            nc.tensor.matmul(PS[:, 7, 8:16], tri, SEL[:, 8:16], start=False, stop=True)
            nc.tensor.matmul(PS[:, 7, 16:24], ones, SEL[:, 0:8], start=True, stop=False)
            tk = PE.i(nc.tensor.matmul(PS[:, 7, 16:24], ones, SEL[:, 8:16], start=False, stop=True))
            v = V.i(V.at(tk).tensor_tensor(SLOT, PS[:, 7, 0:16], SEL, ALU.mult))
            v = V.i(V.at(v).tensor_scalar(SLOT, SLOT, -1.0, None, ALU.add))
            V.i(V.at(v).tensor_scalar(SLOT2, SLOT, -128.0, None, ALU.add))
            v = V.i(V.at(v).tensor_reduce(sm[:, 184:185], PS[:, 7, 16:24], AX.X, ALU.max))
            bank_free[7] = [v]
            cnt_tok = slot_tok = V.i(V.at(v).tensor_copy(CNT[:, :], sm[:, 184:185]))
            nfg = [gc(("nf", 1), c) for c in range(8)]

            GPM = AR[:, 0:512].rearrange("p (b t j) -> p b t j", b=2, t=2)
            PCM = AR[:, 512:1024].rearrange("p (b t j) -> p b t j", b=2, t=2)
            PTM = AR[:, 1024:1536].rearrange("p (b m) -> p b m", b=2)
            YE = AR[:, 1536:2560]
            HX = AR[:, 15360:16384].rearrange("p (b n) -> p b n", b=2)
            xg, ptm, up_last, sc_last = {}, {}, {}, {}

            def select(g, pc, slot, e, wait):
                for t in range(T):
                    k = 8 * t + e
                    V.i(V.at(*wait).tensor_scalar(g[:, t, :], iota, slot[:, k:k + 1], None, ALU.is_equal))
                    v = V.i(nc.vector.tensor_scalar(pc[:, t, :], iota, slot[:, k:k + 1], COMB[:, k:k + 1],
                                                    ALU.is_equal, ALU.mult))
                return v

            def prep(e):
                b = e % 2
                sl = slice(b * P, b * P + P)
                v = select(GPM[:, b], PCM[:, b], SLOT, e, [slot_tok, *ar_free, up_last.get(e - 2)])
                yield
                wr = []
                for half, bank in enumerate((7, 3)):
                    PE.at(v, *bank_free[bank])
                    for c in range(4):
                        cc = 4 * half + c
                        for t in range(T):
                            last = nc.tensor.matmul(PS[:, bank, c * P:c * P + P], XN[:, t, cc * P:cc * P + P],
                                                    GPM[:, b, t, :], start=t == 0, stop=t == 1)
                    tk = PE.i(last)
                    for c in range(4):
                        cc = 4 * half + c
                        a = S.i(S.at(tk, up_last.get(e - 2)).activation(XTH[:, cc, sl], PS[:, bank, c * P:c * P + P], ACT.Copy,
                                                     scale=nfg[cc]))
                    for c in range(4):
                        cc = 4 * half + c
                        w = V.i(V.at(a, tk, up_last.get(e - 2)).scalar_tensor_tensor(
                            out=XTL[:, cc, sl], in0=PS[:, bank, c * P:c * P + P], scalar=nfg[cc],
                            in1=XTH[:, cc, sl].bitcast(F32), op0=ALU.mult, op1=ALU.subtract))
                    bank_free[bank] = [w]
                    wr += [a, w]
                xg[e] = wr
                yield
                PE.at(v, *bank_free[7])
                for t in range(T):
                    last = nc.tensor.transpose(PS[:, 7, t * P:t * P + P], PCM[:, b, t, :], ident)
                tk = PE.i(last)
                w = V.i(V.at(tk, sc_last.get(e - 2)).tensor_copy(PTM[:, b, :], PS[:, 7, 0:256]))
                bank_free[7] = [w]
                ptm[e] = w
                yield

            def up1(key, e, bank, mid=None):
                sl = slice((e % 2) * P, (e % 2) * P + P)
                PE.at(*xg[e])
                for kp in range(2):
                    wh, wl = take((key, kp))
                    if kp == 0:
                        PE.at(*bank_free[bank])
                    for k in range(4):
                        last = mm3(PS[:, bank, :], XTH[:, 4 * kp + k, sl], XTL[:, 4 * kp + k, sl], wh[:, k, :], wl[:, k, :],
                                   kp + k == 0, kp == 1 and k == 3)
                    pe_done.append(PE.i(last))
                    if kp == 0 and mid is not None:
                        mid()
                    tick()
                return PE.last

            def put_back(e, d):
                a = S.i(S.at(d, sc_last.get(e - 1)).copy(YE[:, 0:512], PS[:, 0, :]))
                v = V.i(V.at(d, sc_last.get(e - 1)).tensor_copy(YE[:, 512:1024], PS[:, 1, :]))
                bank_free[0], bank_free[1] = [a], [v]
                yield
                for t in range(T):
                    for j in range(2):
                        PE.at(a, v, ptm[e], *bank_free[2 + j])
                        tk = PE.i(nc.tensor.matmul(PS[:, 2 + j, :], PTM[:, e % 2, t * P:t * P + P],
                                                   YE[:, j * 512:j * 512 + 512], start=True, stop=True))
                        xo = X[:, t, j * 512:j * 512 + 512]
                        w = V.i(V.at(tk).tensor_tensor(xo, PS[:, 2 + j, :], xo, ALU.add))
                        bank_free[2 + j] = [w]
                sc_last[e] = tk
                yield

            for _ in prep(0):
                pass
            gr = [(e, n) for e in range(NE) for n in range(FE // 512)]
            hm = {}
            ht = {}

            def turn(i):
                pd = PE.last
                PE.at(hm[i], *bank_free[6])
                for c in range(4):
                    last = nc.tensor.transpose(PS[:, 6, c * P:c * P + P], HX[:, i % 2, c * P:c * P + P], ident)
                tp = PE.i(last)
                pv = PS[:, 6, :].rearrange("p (c m) -> p c m", c=4)
                a = S.i(S.at(tp, pd).copy(HTH[:, :, 0:P], pv))
                w = V.i(V.at(a, tp, pd).tensor_tensor(HTL[:, :, 0:P], pv, HTH[:, :, 0:P].bitcast(F32), ALU.subtract))
                bank_free[6] = [a, w]
                ht[i] = [a, w, tp]

            for i in range(len(gr) + 1):
                if i < len(gr):
                    e, n = gr[i]
                    if n == 0 and e not in xg:
                        drain()
                    tg = up1(("moe", "g", e, n), e, 4, mid=(lambda i=i: turn(i - 1)) if i else None)
                    hx = HX[:, i % 2, :]
                    old = ht[i - 2][2] if i >= 2 else None
                    a = S.i(S.at(tg, old, *ar_free).activation(hx, PS[:, 4, :], ACT.Silu))
                    bank_free[4] = [a]
                    tu = up1(("moe", "u", e, n), e, 5)
                    w = V.i(V.at(tu, a).tensor_tensor(hx, PS[:, 5, :], hx, ALU.mult))
                    bank_free[5] = [w]
                    hm[i] = w
                    if n == FE // 512 - 1:
                        up_last[e] = PE.last
                    if n == 2 and e + 1 < NE:
                        bg.append(prep(e + 1))
                else:
                    turn(i - 1)
                if i:
                    e, n = gr[i - 1]
                    PE.at(*ht[i - 1])
                    if n == 0:
                        PE.at(*bank_free[0], *bank_free[1])
                    for kp in range(2):
                        wh, wl = take((("moe", "d", e, n), kp))
                        for j in range(2):
                            for k in range(2):
                                kk = kp * 2 + k
                                js = slice(j * 512, j * 512 + 512)
                                last = mm3(PS[:, j, :], HTH[:, kk, 0:P], HTL[:, kk, 0:P], wh[:, k, js], wl[:, k, js],
                                           n == 0 and kk == 0, n == FE // 512 - 1 and kk == 3)
                        pe_done.append(PE.i(last))
                        tick()
                    if n == FE // 512 - 1:
                        bg.append(put_back(e, PE.last))
            drain()

            engs = (PE, V, S, SP)
            for E in (PE, S, SP):
                E.at(cnt_tok)
            V.at(cnt_tok)
            over = nc.values_load(CNT[0:1, 0:1], engines=[mybir.EngineType.PE, mybir.EngineType.DVE,
                                                          mybir.EngineType.Activation, mybir.EngineType.SP],
                                  min_val=0, max_val=256)
            before = [(E, E.n, dict(E.seen)) for E in engs]
            WB = AR[:, 8192:12288].rearrange("p (b n) -> p b n", b=2)
            XG2 = AR[:, 12288:13312].rearrange("p (c j) -> p c j", c=8)
            H2 = AR[:, 13312:13824]
            HT2 = AR[:, 14336:14848].rearrange("p (c j) -> p c j", c=4)
            G2 = AR[:, 7168:7424].rearrange("p (t j) -> p t j", t=2)
            PC2 = AR[:, 7424:7680].rearrange("p (t j) -> p t j", t=2)
            PT2 = AR[:, 7680:7936]
            osem = [sem("ld_o0"), sem("ld_o1")]
            with nc.If(over > 128):
                nload = [0]
                buf_free = [PE.last, PE.last]

                def fetch(src, kb, n):
                    i = nload[0]
                    nload[0] += 1
                    b = i % 2
                    SP.at(buf_free[b], V.last if i < 2 else None)
                    nc.sync.dma_start(WB[:, b, 0:kb * n].rearrange("p (k n) -> p k n", k=kb),
                                      src.rearrange("(k p) n -> p k n", p=P)).then_inc(osem[b], 16)
                    PE.at((f"ld_o{b}", osem[b], 16 * (i // 2 + 1)))
                    return WB[:, b, 0:kb * n].rearrange("p (k n) -> p k n", k=kb), b

                for e in range(NE):
                    v = select(G2, PC2, SLOT2, e, [slot_tok, PE.last])
                    for half in range(2):
                        PE.at(v, V.last)
                        for c in range(4):
                            cc = 4 * half + c
                            for t in range(T):
                                last = nc.tensor.matmul(PS[:, half, c * P:c * P + P], XN[:, t, cc * P:cc * P + P],
                                                        G2[:, t, :], start=t == 0, stop=t == 1)
                        tk = PE.i(last)
                        for c in range(4):
                            cc = 4 * half + c
                            w = V.i(V.at(tk).tensor_scalar(XG2[:, cc, :], PS[:, half, c * P:c * P + P], nfg[cc], None,
                                                           ALU.mult))
                    PE.at(w)
                    for t in range(T):
                        last = nc.tensor.transpose(PS[:, 2, t * P:t * P + P], PC2[:, t, :], ident)
                    tk = PE.i(last)
                    v = V.i(V.at(tk).tensor_copy(PT2, PS[:, 2, 0:256]))
                    for n in range(FE // 512):
                        cs = slice(n * 512, n * 512 + 512)
                        for which, w_ in enumerate((dr["moe_w_gate_2"], dr["moe_w_up_2"])):
                            PE.at(V.last, S.last)
                            for kp in range(2):
                                wb, b = fetch(w_[0, e, kp * 512:kp * 512 + 512, cs], 4, 512)
                                for k in range(4):
                                    last = nc.tensor.matmul(PS[:, 4 + which, :], XG2[:, 4 * kp + k, :], wb[:, k, :],
                                                            start=kp + k == 0, stop=kp == 1 and k == 3)
                                buf_free[b] = PE.i(last)
                        tk = PE.last
                        a = S.i(S.at(tk).activation(H2, PS[:, 4, :], ACT.Silu))
                        v = V.i(V.at(tk, a).tensor_tensor(H2, PS[:, 5, :], H2, ALU.mult))
                        PE.at(v)
                        for c in range(4):
                            last = nc.tensor.transpose(PS[:, 6, c * P:c * P + P], H2[:, c * P:c * P + P], ident)
                        tk = PE.i(last)
                        v = V.i(V.at(tk).tensor_copy(HT2, PS[:, 6, :].rearrange("p (c j) -> p c j", c=4)))
                        PE.at(v)
                        for kp in range(2):
                            wb, b = fetch(dr["moe_w_down_2"][0, e, n * 512 + kp * 256:n * 512 + kp * 256 + 256, :], 2, D)
                            for j in range(2):
                                for k in range(2):
                                    last = nc.tensor.matmul(PS[:, j, :], HT2[:, 2 * kp + k, :], wb[:, k, j * 512:j * 512 + 512],
                                                            start=n == 0 and kp + k == 0,
                                                            stop=n == FE // 512 - 1 and kp + k == 2,
                                                            skip_group_check=True)
                            buf_free[b] = PE.i(last)
                    for j in range(2):
                        v = V.i(V.at(PE.last).tensor_copy(YE[:, j * 512:j * 512 + 512], PS[:, j, :]))
                    for t in range(T):
                        for j in range(2):
                            PE.at(V.last)
                            tk = PE.i(nc.tensor.matmul(PS[:, 2 + j, :], PT2[:, t * P:t * P + P], YE[:, j * 512:j * 512 + 512],
                                                       start=True, stop=True))
                            xo = X[:, t, j * 512:j * 512 + 512]
                            V.i(V.at(tk).tensor_tensor(xo, PS[:, 2 + j, :], xo, ALU.add))
            with nc.Else():
                for E, n0, _ in before:
                    if E.n > n0:
                        E.e.wait_ge(E.sem, n0)
                        E.e.sem_inc(E.sem, E.n - n0)
            nc.end_ifs()
            for E, _, seen in before:
                E.seen = seen
            for b in range(8):
                bank_free[b] = [V.last, PE.last, S.last]
            return V.last

        QT = AR[:, 0:3072].rearrange("p (g h m) -> p g h m", g=3, h=4)
        KT = AR[:, 3072:6144].rearrange("p (g h m) -> p g h m", g=3, h=4)
        VV = AR[:, 6144:9216].rearrange("p (t g n) -> p t g n", t=2, g=3)
        GG = AR[:, 9216:10240].rearrange("p (t n) -> p t n", t=2)
        VH = AR[:, 6144:7168].rearrange("p (t n) -> p t n", t=2)
        SG = AR[:, 7168:8192]
        TOT = AR[:, 8192:9216]
        HQ = AR[:, 10240:11264]
        HK = AR[:, 11264:12288]
        ATT = AR[:, 12288:13312].rearrange("p (a m) -> p a m", a=8)
        ATX = AR[:, 13312:13824].rearrange("p (h m) -> p h m", h=4)
        TT = AR[:, 13824:14336]
        ZT = AR[:, 14336:15360].rearrange("p (t n) -> p t n", t=2)
        RP = AR[:, 15360:15872].rearrange("p (t x) -> p t x", t=2)
        ZB = AR[:, 10240:12288].rearrange("p (t n) -> p t n", t=2)
        SC = AR[:, 12288:13824].rearrange("p (b n) -> p b n", b=2)
        PT = AR[:, 13824:15360].rearrange("p (b n) -> p b n", b=2)
        OA = AR[:, 15360:16384].rearrange("p (t n) -> p t n", t=2)

        def turn_heads(src, ready, np_=P, nh=4, wd=P):
            toks = []
            for b in range(nh // 2):
                PE.at(*ready, *bank_free[6 + b])
                for c in range(2):
                    for t in range(T):
                        last = nc.tensor.transpose(PS[0:wd, 6 + b, c * 256 + t * P:c * 256 + t * P + P],
                                                   src(t, 2 * b + c), ident)
                toks.append(PE.i(last))
            return toks

        def hgrn(l, st):
            free = st["at_free"]
            z = V.i(V.at(*free).memset(AR[:, 12288:13312], 0.0))
            q4 = HQ.rearrange("p (a m) -> p a m", m=P)
            k4 = HK.rearrange("p (a m) -> p a m", m=P)
            ready = st["qk"]
            tot_tok = st["f"]
            tot = TOT
            ntot = 1024
            alt = TT
            for li, m in enumerate(LEVELS):
                pt = []
                for b in range(2):
                    PE.at(*ready, *bank_free[b])
                    for a_ in range(4):
                        last = nc.tensor.matmul(PS[:, b, a_ * P:a_ * P + P], k4[:, 4 * b + a_, :], q4[:, 4 * b + a_, :],
                                                start=True, stop=True)
                    pt.append(PE.i(last))
                yield
                for b in range(2):
                    v = V.i(V.at(pt[b], z, V.last).copy_predicated(
                        ATT[:, 4 * b:4 * b + 4, :], hmask[li].unsqueeze(1).to_broadcast([P, 4, P]),
                        PS[:, b, :].rearrange("p (a m) -> p a m", a=4)))
                    bank_free[b] = [v]
                if m == 0:
                    v = V.i(V.at(*pt, tot_tok).tensor_tensor(HQ, HQ, TOT, ALU.mult))
                    ready = [v]
                else:
                    nb = 1024 // (2 * m)
                    q3 = HQ.rearrange("p (b w m) -> p b w m", w=2, m=m)
                    k3 = HK.rearrange("p (b w m) -> p b w m", w=2, m=m)
                    t3 = tot[:, 0:2 * nb].rearrange("p (b w) -> p b w", w=2)
                    v1 = V.i(V.at(*pt, tot_tok).tensor_tensor(
                        q3[:, :, 1, :], q3[:, :, 1, :], t3[:, :, 0:1].to_broadcast([P, nb, m]), ALU.mult))
                    v2 = V.i(V.at(*pt, tot_tok).tensor_tensor(
                        k3[:, :, 0, :], k3[:, :, 0, :], t3[:, :, 1:2].to_broadcast([P, nb, m]), ALU.mult))
                    nt = alt[:, 0:nb]
                    tot_tok = V.i(V.at(tot_tok, v2).tensor_tensor(nt, t3[:, :, 0], t3[:, :, 1], ALU.mult))
                    tot, alt = alt, (TOT if alt is TT else TT)
                    ready = [v1, v2]
            q3 = HQ.rearrange("p (h t m) -> p h t m", h=4, t=2)
            k3 = HK.rearrange("p (h t m) -> p h t m", h=4, t=2)
            PE.at(*ready, *bank_free[0])
            for h in range(4):
                last = nc.tensor.matmul(PS[:, 0, h * P:h * P + P], k3[:, h, 0, :], q3[:, h, 1, :], start=True, stop=True)
            tk = PE.i(last)
            yield
            ax = V.i(V.at(tk).tensor_copy(AR[:, 13312:13824], PS[:, 0, :]))
            bank_free[0] = [ax]
            yield
            pv = []
            for t in range(T):
                PE.at(ax, V.last, st["v"], *bank_free[2 + t])
                for h in range(4):
                    o = PS[:, 2 + t, h * P:h * P + P]
                    last = nc.tensor.matmul(o, ATT[:, 2 * h + t, :], VH[:, t, h * P:h * P + P],
                                            start=True, stop=(t == 0))
                    if t == 1:
                        last = nc.tensor.matmul(o, ATX[:, h, :], VH[:, 0, h * P:h * P + P], start=False, stop=True)
                pv.append(PE.i(last))
            yield
            for t in range(T):
                sq = SG[:, 0:512]
                a = S.i(S.at(pv[t], V.last).activation(sq, PS[:, 2 + t, :], ACT.Square))
                r4 = sm[:, 40:44]
                v = V.i(V.at(a, V.last).tensor_reduce(r4, sq.rearrange("p (h m) -> p h m", h=4), AX.X, ALU.add))
                v = V.i(V.at(v).tensor_scalar(r4, r4, 1.0 / P, EPS, ALU.mult, ALU.add))
                a = S.i(S.at(v).activation(r4, r4, ACT.Sqrt))
                v = V.i(V.at(a).reciprocal(r4, r4))
                g3 = GG[:, t, :].rearrange("p (h m) -> p h m", h=4)
                v = V.i(V.at(v, st["g"]).tensor_tensor(g3, g3, r4.unsqueeze(2).to_broadcast([P, 4, P]), ALU.mult))
                v = V.i(V.at(v).tensor_tensor(GG[:, t, :], PS[:, 2 + t, :], GG[:, t, :], ALU.mult))
                bank_free[2 + t] = [v, a]
                yield
            st["done"] = [v, a, pv[1]]

        def softmax_tasks(tasks):
            n = len(tasks)
            st = [dict() for _ in tasks]

            def sA(i):
                q = tasks[i]
                PE.at(*q["ready"], *bank_free[0], *bank_free[1])
                for o, lh, rh in q["scores"]:
                    last = nc.tensor.matmul(o, lh, rh, start=True, stop=True)
                st[i]["s"] = PE.i(last)

            def sB(i):
                q, b = tasks[i], i % 2
                prev = st[i - 2]["tr"] if i >= 2 else None
                s2 = SC[:, b, 0:q["n"]]
                V.at(st[i]["s"], prev, st[i - 2]["e"] if i >= 2 else None, *q["scfree"])
                for dst, ps, mk in q["mask"](s2):
                    v = V.i(nc.vector.scalar_tensor_tensor(out=dst, in0=ps, scalar=q["scale"], in1=mk,
                                                           op0=ALU.mult, op1=ALU.add))
                bank_free[0] = bank_free[1] = [v]
                ns = q["nsub"]
                mx = sm[:, 48 + 4 * b:48 + 4 * b + ns]
                v = V.i(V.at(v).tensor_reduce(mx, s2.rearrange("p (a k) -> p a k", a=ns), AX.X, ALU.max))
                v = V.i(V.at(v).tensor_scalar(mx, mx, -1.0, None, ALU.mult))
                w = q["n"] // ns
                for a_ in range(ns):
                    e = S.i(S.at(v, q["denfree"]).activation(s2[:, a_ * w:a_ * w + w], s2[:, a_ * w:a_ * w + w], ACT.Exp,
                                               bias=mx[:, a_:a_ + 1], accum_out=q["den"][:, a_:a_ + 1]))
                st[i]["e"] = e

            def sC(i):
                q, b = tasks[i], i % 2
                nch = q["n"] // P
                PE.at(st[i]["e"])
                st[i]["ev"] = []
                for bb in range(-(-nch // 4)):
                    PE.at(*bank_free[6 + bb])
                    m = min(4, nch - 4 * bb)
                    for c in range(m):
                        last = nc.tensor.transpose(PS[:, 6 + bb, c * P:c * P + P],
                                                   SC[:, b, (4 * bb + c) * P:(4 * bb + c) * P + P], ident)
                    tp = PE.i(last)
                    old = st[i - 2]["pv"] if i >= 2 else None
                    dst = PT[:, b, bb * 512:bb * 512 + m * P]
                    if bb == 0:
                        ev = S.i(S.at(tp, old, *q["scfree"]).copy(dst, PS[:, 6, 0:m * P]))
                    else:
                        ev = V.i(V.at(tp, old, *q["scfree"]).tensor_copy(dst, PS[:, 7, 0:m * P]))
                    bank_free[6 + bb] = [ev]
                    st[i]["ev"].append(ev)
                st[i]["tr"] = PE.last

            def sE(i):
                q, b = tasks[i], i % 2
                PE.at(*st[i]["ev"], *bank_free[q["obank"]] if q["ofirst"] else [])
                PE.at(*st[i]["ev"])
                for o, chunks in q["pv"]:
                    for j, (c, v) in enumerate(chunks):
                        last = nc.tensor.matmul(o, PT[:, b, c * P:c * P + P], v, start=(j == 0), stop=(j == len(chunks) - 1))
                st[i]["pv"] = PE.i(last)
                if q["after"] is not None:
                    q["after"](st[i]["pv"], st[i]["e"])

            for k in range(n + 2):
                if 0 <= k - 2 < n:
                    sE(k - 2)
                if 0 <= k - 1 < n:
                    sC(k - 1)
                if k < n:
                    sA(k)
                    sB(k)
                yield

        xr = [ld_x]
        xn_free = []
        ar_free = [ci_tok]
        for l in range(2):
            xt = norm_t(("n1", l), xr, xn_free)
            st = {}
            ztr = [None]
            hg_tmp = []

            def qk1(which, g, tk):
                cp = []
                for t in range(T):
                    a = S.i(S.at(tk[t], ztr[0], V.last if which == 0 and g == 0 else None).copy(ZT[:, t, :], PS[:, 4 + t, :]))
                    bank_free[4 + t] = [a]
                cp.append(a)
                r4 = ZT[:, :, :].rearrange("p t (h d) -> p t h d", h=4)
                p1 = RP[:, :, 0:128].rearrange("p t (h d) -> p t h d", h=4)
                p2 = RP[:, :, 128:256].rearrange("p t (h d) -> p t h d", h=4)
                V.at(a, V.last)
                v = None
                for t in range(T):
                    A = ropeA[:, t, :].unsqueeze(1).to_broadcast([P, 4, 32])
                    B = ropeB[:, t, :].unsqueeze(1).to_broadcast([P, 4, 32])
                    V.i(nc.vector.tensor_tensor(p1[:, t], r4[:, t, :, 0:32], A, ALU.mult))
                    V.i(nc.vector.tensor_tensor(p2[:, t, :, 0:16], r4[:, t, :, 16:32], B[:, :, 0:16], ALU.mult))
                    v = V.i(nc.vector.tensor_tensor(p2[:, t, :, 16:32], r4[:, t, :, 0:16], B[:, :, 16:32], ALU.mult))
                for t in range(T):
                    v = V.i(V.at(v).tensor_tensor(r4[:, t, :, 0:32], p1[:, t], p2[:, t], ALU.add))
                yield
                dst = QT if which == 0 else KT
                tt = turn_heads(lambda t, h: ZT[:, t, h * P:h * P + P], [v, a])
                ztr[0] = tt[-1]
                a = S.i(S.at(tt[0]).copy(dst[:, g, 0:2, :], PS[:, 6, :].rearrange("p (h m) -> p h m", h=2)))
                v = V.i(V.at(tt[1]).tensor_copy(dst[:, g, 2:4, :], PS[:, 7, :].rearrange("p (h m) -> p h m", h=2)))
                bank_free[6], bank_free[7] = [a], [v]
                st[("qk", which, g)] = [a, v]
                yield

            def hq(which, tk):
                for t in range(T):
                    a = S.i(S.at(tk[t], ztr[0], *ar_free).copy(ZT[:, t, :], PS[:, 4 + t, :]))
                    bank_free[4 + t] = [a]
                yield
                tt = turn_heads(lambda t, h: ZT[:, t, h * P:h * P + P], [a])
                ztr[0] = tt[-1]
                for b in range(2):
                    sl = slice(b * 512, b * 512 + 512)
                    if which == 0:
                        a = S.i(S.at(tt[b], V.last).activation(SG[:, sl], PS[:, 6 + b, :], ACT.Sigmoid))
                        v = V.i(V.at(a).tensor_tensor(HQ[:, sl], PS[:, 6 + b, :], SG[:, sl], ALU.mult))
                        st["q"] = v
                    else:
                        a = S.i(S.at(tt[b]).activation(TOT[:, sl], PS[:, 6 + b, :], ACT.Sigmoid))
                        a = S.i(S.at(tt[b]).activation(HK[:, sl], PS[:, 6 + b, :], ACT.Sigmoid, scale=-1.0))
                        v = a
                        if l == 1:
                            for h in range(2 * b, 2 * b + 2):
                                hs = slice(h * 256, h * 256 + 256)
                                V.i(V.at(a, lb_tok).tensor_scalar(TOT[:, hs], TOT[:, hs], OMB[:, h:h + 1], LB[:, h:h + 1],
                                                                  ALU.mult, ALU.add))
                                v = V.i(V.at(a, lb_tok).tensor_scalar(HK[:, hs], HK[:, hs], OMB[:, h:h + 1], None, ALU.mult))
                        st["f"] = v
                    bank_free[6 + b] = [a, v if which == 0 else a]
                st["qk"] = [st["q"], st.get("f")]
                if which == 1:
                    st["at_free"] = ar_free
                    bg.append(hgrn(l, st))
                yield

            def plain(dst, tk, fn, wait=()):
                for t in range(T):
                    if fn is None:
                        a = S.i(S.at(tk[t], *wait).copy(dst(t), PS[:, 4 + t, :]))
                    else:
                        a = S.i(S.at(tk[t], *wait).activation(dst(t), PS[:, 4 + t, :], fn))
                    bank_free[4 + t] = [a]
                return a

            for g in range(17):
                if g == 10:
                    while "done" not in st:
                        tick()
                tk = up(("in1", l, g), 512, xt)
                if g < 2:
                    bg.append(hq(g, tk))
                elif g == 2:
                    st["v"] = plain(lambda t: VH[:, t, :], tk, None, ar_free)
                elif g == 3:
                    st["g"] = plain(lambda t: GG[:, t, :], tk, ACT.Sigmoid, ar_free)
                elif g < 10:
                    bg.append(qk1((g - 4) // 3, (g - 4) % 3, tk))
                elif g < 13:
                    st["vv"] = plain(lambda t: VV[:, t, g - 10, :], tk, None, st["done"])
                else:
                    if g == 13:
                        while bg:
                            tick()
                    dst = XN if g < 15 else ZB
                    o = (g - 13) % 2 * 512
                    st[("z", g)] = plain(lambda t: dst[:, t, o:o + 512], tk, None, st["done"] + [xt[2], ztr[0]])
                if g == 12:
                    while bg:
                        tick()
                    tasks = []
                    rd = [st["vv"]] + [x for w in range(2) for gg in range(3) for x in st[("qk", w, gg)]]
                    for t in range(T):
                        nk = (t + 1) * P
                        for h in range(4):
                            den = sm[:, 64 + 4 * t + h:65 + 4 * t + h]
                            sc, mk = [], []
                            for gg in range(3):
                                if t == 0:
                                    o = PS[:, 0, gg * P:gg * P + P]
                                else:
                                    o = PS[:, gg // 2, (gg % 2) * 256:(gg % 2) * 256 + 256]
                                sc.append((o, QT[:, gg, h, t * P:t * P + P], KT[:, gg, h, 0:nk]))

                            def mask(s2, t=t, nk=nk):
                                if t == 0:
                                    return [(s2, PS[:, 0, 0:384], CB[:, 0:384])]
                                return [(s2[:, 0:512], PS[:, 0, :], CB[:, 384:896]),
                                        (s2[:, 512:768], PS[:, 1, 0:256], CB[:, 896:1152])]

                            chunks = [(gg * (t + 1) + kc, VV[:, kc, gg, h * P:h * P + P])
                                      for gg in range(3) for kc in range(t + 1)]

                            def after(pv, e, t=t, h=h):
                                if h < 3:
                                    return
                                rden = sm[:, 72 + 4 * t:76 + 4 * t]
                                v = V.i(V.at(e, V.last).reciprocal(rden, sm[:, 64 + 4 * t:68 + 4 * t]))
                                v = V.i(V.at(v, pv, *st["done"]).tensor_tensor(
                                    OA[:, t, :].rearrange("p (h m) -> p h m", h=4),
                                    PS[:, 2 + t, :].rearrange("p (h m) -> p h m", h=4),
                                    rden.unsqueeze(2).to_broadcast([P, 4, P]), ALU.mult))
                                bank_free[2 + t] = [v]
                                st["oa"] = v

                            tasks.append(dict(ready=rd, scores=sc, n=3 * nk, nsub=1, scale=float(P) ** -0.5, mask=mask,
                                              scfree=st["done"] + [ztr[0]], den=den, denfree=V.last, obank=2 + t, ofirst=h == 0,
                                              pv=[(PS[:, 2 + t, h * P:h * P + P], chunks)], after=after))
                    bg.append(softmax_tasks(tasks))
                else:
                    tick()
            drain()
            xg = to_xt(GG, st["done"], [gc(("hn", l), c) for c in range(4)], 0, 4)
            xo = to_xt(OA, [st["oa"]], [None] * 4, 4, 4)
            sa = sb_ = None
            for t in range(T):
                sa = S.i(S.at(*[st[("z", g)] for g in range(13, 17)]).activation(XN[:, t, :], XN[:, t, :], ACT.Sigmoid))
                sb_ = S.i(S.at().activation(ZB[:, t, :], ZB[:, t, :], ACT.Sigmoid))
            for n in range(2):
                tk = up(("bra", l, n), 512, xg, K=512, k0=0)
                for t in range(T):
                    o = XN[:, t, n * 512:n * 512 + 512]
                    v = V.i(V.at(tk[t], sa, sb_).tensor_tensor(o, PS[:, 4 + t, :], o, ALU.mult))
                    bank_free[4 + t] = [v]
            for n in range(2):
                tk = up(("brb", l, n), 512, xo, K=512, k0=4)
                for t in range(T):
                    o = XN[:, t, n * 512:n * 512 + 512]
                    z = ZB[:, t, n * 512:n * 512 + 512]
                    v = V.i(V.at(tk[t]).tensor_tensor(z, PS[:, 4 + t, :], z, ALU.mult))
                    bank_free[4 + t] = [v]
                    v = V.i(V.at(v).tensor_tensor(o, o, z, ALU.add))
            xy = to_xt(XN, [v], [None] * 8)
            v = out_proj(("out1", l), xy)
            xt = norm_t(("n2", l), [v], [xy[2]])
            d = mlp(("m1", l), False, 4096, xt)
            v = add_x(d)
            xr = [v]
            xn_free = [xt[2]]
            ar_free = [PE.last, v, S.last]

        v = block_norm(dr["final_norm_g"], "ld_f1", X, xr, xn_free)
        xr = [v]

        s_m = sem("ld_m")
        SP.at(PE.last, V.last, S.last)
        nld = 0
        for l in range(2):
            for j, nm in enumerate(("lambda_q1_2", "lambda_k1_2", "lambda_q2_2", "lambda_k2_2")):
                nc.sync.dma_start(LQ[:, l, j, :], dr[nm][l].partition_broadcast(P)).then_inc(s_m, 16)
                nld += 16
            nc.sync.dma_start(BF[:, l, :], dr["b_forget_2"][l].partition_broadcast(P)).then_inc(s_m, 16)
            nld += 16
        nc.sync.dma_start(RT[:, :].rearrange("p (c e) -> p c e", c=8),
                          dr["router_2"][0].rearrange("(c p) e -> p c e", p=P)).then_inc(s_m, 16)
        ld_m = ("ld_m", s_m, nld + 16)
        NLAM = sm[:, 80:82]
        lp = sm[:, 84:88]
        for l in range(2):
            for j in range(2):
                v = V.i(V.at(ld_m).tensor_tensor(LQ[:, l, 2 * j, :], LQ[:, l, 2 * j, :], LQ[:, l, 2 * j + 1, :], ALU.mult))
                v = V.i(V.at(v).tensor_reduce(lp[:, 2 * l + j:2 * l + j + 1], LQ[:, l, 2 * j, :], AX.X, ALU.add))
        a = S.i(S.at(v).activation(lp, lp, ACT.Exp))
        for l in range(2):
            v = V.i(V.at(a).tensor_scalar(NLAM[:, l:l + 1], lp[:, 2 * l + 1:2 * l + 2], lp[:, 2 * l:2 * l + 1], -LAM_INIT[l],
                                          ALU.subtract, ALU.add))
            v = V.i(V.at(g_all, PE.last).tensor_scalar(gc(("sub", l)), gc(("sub", l)), 1.0 - LAM_INIT[l], None, ALU.mult))
        lam_tok = v
        ra = S.i(S.at(ld_m).copy(RTH[:, :, :], RT[:, :].rearrange("p (c e) -> p c e", c=8)))
        rt_tok = V.i(V.at(ra).tensor_tensor(RTL[:, :, :], RT[:, :].rearrange("p (c e) -> p c e", c=8),
                                            RTH[:, :, :].bitcast(F32), ALU.subtract))
        ar_free = [v, S.last, PE.last]

        def a2(o, n, **k):
            return AR[:, o:o + n]

        QAT = a2(0, 1024).rearrange("p (c m) -> p c m", c=4)
        KAT = a2(1024, 1024).rearrange("p (c m) -> p c m", c=4)
        VA = a2(2048, 1024).rearrange("p (t n) -> p t n", t=2)
        QB = a2(3072, 528).rearrange("p (t h d) -> p t h d", t=2, h=4)
        KB = a2(3600, 528).rearrange("p (t h d) -> p t h d", t=2, h=4)
        QBT = a2(4128, 1024).rearrange("p (h m) -> p h m", h=4)
        KBT = a2(5152, 1024).rearrange("p (h m) -> p h m", h=4)
        VB = a2(6176, 512).rearrange("p (t n) -> p t n", t=2)
        QKC = a2(6688, 1024).rearrange("p (c m) -> p c m", c=4)
        VC = a2(7712, 512).rearrange("p (t n) -> p t n", t=2)
        GC = a2(8224, 512).rearrange("p (t n) -> p t n", t=2)
        RA = a2(8736, 1536).rearrange("p (h n) -> p h n", h=4)
        SQ = a2(10272, 512)
        LF = sm[:, 88:136]
        MIX = XN

        for l in range(2):
            xt = norm_t(("nm", l), xr, [PE.last])
            xtp = xt[2]
            st = {}
            ztr = [None]

            def qk_a(dst, tk, name, rot=False):
                for t in range(T):
                    a = S.i(S.at(tk[t], ztr[0], *ar_free).copy(ZT[:, t, :], PS[:, 4 + t, :]))
                    bank_free[4 + t] = [a]
                v = None
                if rot:
                    for t in range(T):
                        r4 = ZT[:, t, :].rearrange("p (h d) -> p h d", h=8)
                        p1 = OA[:, 0, :].rearrange("p (h d) -> p h d", h=8)
                        p2 = OA[:, 1, :].rearrange("p (h d) -> p h d", h=8)
                        A = rotA[:, t, :].unsqueeze(1).to_broadcast([P, 8, 64])
                        B = rotB[:, t, :].unsqueeze(1).to_broadcast([P, 8, 64])
                        V.i(V.at(a, V.last).tensor_tensor(p1, r4, A, ALU.mult))
                        V.i(nc.vector.tensor_tensor(p2[:, :, 0:32], r4[:, :, 32:64], B[:, :, 0:32], ALU.mult))
                        v = V.i(nc.vector.tensor_tensor(p2[:, :, 32:64], r4[:, :, 0:32], B[:, :, 32:64], ALU.mult))
                        v = V.i(V.at(v).tensor_tensor(r4, p1, p2, ALU.add))
                yield
                tt = turn_heads(lambda t, h: ZT[:, t, h * P:h * P + P], [v, a])
                ztr[0] = tt[-1]
                a = S.i(S.at(tt[0]).copy(dst[:, 0:2, :], PS[:, 6, :].rearrange("p (h m) -> p h m", h=2)))
                v = V.i(V.at(tt[1], *ar_free).tensor_copy(dst[:, 2:4, :], PS[:, 7, :].rearrange("p (h m) -> p h m", h=2)))
                bank_free[6], bank_free[7] = [a], [v]
                st[name] = [a, v]
                yield

            def fox_gate(tk):
                a = None
                for t in range(T):
                    a = S.i(S.at(tk[t], *ar_free).copy(VB[:, t, :], PS[:, 4 + t, 0:256]))
                    v = V.i(V.at(a, ld_m, V.last).tensor_tensor(LF[:, 4 * t:4 * t + 4], PS[:, 4 + t, 256:260], BF[:, l, :], ALU.add))
                    bank_free[4 + t] = [a, v]
                st["vb"] = a
                x, y, z = LF[:, 0:8], LF[:, 8:16], LF[:, 16:24]
                v = V.i(V.at(v).tensor_scalar(y, x, -1.0, None, ALU.mult))
                v = V.i(V.at(v).tensor_tensor(z, x, y, ALU.max))
                v = V.i(V.at(v).tensor_scalar(y, y, 0.0, None, ALU.max))
                a = S.i(S.at(v).activation(z, z, ACT.Exp, scale=-1.0))
                a = S.i(S.at(a).activation(z, z, ACT.Ln, bias=1.0))
                v = V.i(V.at(a).tensor_tensor(y, y, z, ALU.add))
                v = V.i(V.at(v).tensor_scalar(y, y, -1.0, None, ALU.mult))
                st["lf"] = v
                yield
                PE.at(v, *bank_free[7])
                nc.tensor.matmul(PS[:, 7, 0:4], tri, y[:, 0:4], start=True, stop=True)
                nc.tensor.matmul(PS[:, 7, 8:12], ones, y[:, 0:4], start=True, stop=False)
                c = PE.i(nc.tensor.matmul(PS[:, 7, 8:12], tri, y[:, 4:8], start=False, stop=True))
                for t in range(T):
                    cu = PS[:, 7, 8 * t:8 * t + 4].unsqueeze(2)
                    V.i(V.at(c, *ar_free).tensor_scalar(QB[:, t, :, 64:65], cu, 8.0, None, ALU.mult))
                    V.i(nc.vector.tensor_scalar(KB[:, t, :, 65:66], cu, -8.0, None, ALU.mult))
                    V.i(nc.vector.memset(QB[:, t, :, 65:66], 1.0))
                    v = V.i(nc.vector.memset(KB[:, t, :, 64:65], 1.0))
                bank_free[7] = [v]
                st["cum"] = v
                yield

            def qk_b(tk):
                for t in range(T):
                    a = S.i(S.at(tk[t], *ar_free).copy(QB[:, t, :, 0:64], PS[:, 4 + t, 0:256].rearrange("p (h d) -> p h d", h=4)))
                    a = S.i(nc.scalar.copy(KB[:, t, :, 0:64], PS[:, 4 + t, 256:512].rearrange("p (h d) -> p h d", h=4)))
                    bank_free[4 + t] = [a]
                yield
                r = []
                for src, dst in ((QB, QBT), (KB, KBT)):
                    tt = turn_heads(lambda t, h: src[:, t, h, :], [a, st["cum"]], wd=66)
                    a2_ = S.i(S.at(tt[0], *ar_free).copy(dst[0:66, 0:2, :], PS[0:66, 6, :].rearrange("p (h m) -> p h m", h=2)))
                    v2_ = V.i(V.at(tt[1], *ar_free).tensor_copy(dst[0:66, 2:4, :], PS[0:66, 7, :].rearrange("p (h m) -> p h m", h=2)))
                    bank_free[6], bank_free[7] = [a2_], [v2_]
                    r += [a2_, v2_]
                    yield
                st["qkb"] = r

            def soft2(kind, start_free):
                tasks = []
                for t in range(T):
                    nk = (t + 1) * P
                    for pr in range(4 if kind == "diff" else 2):
                        b = len(tasks) % 2
                        den = sm[:, 140 + 2 * b:142 + 2 * b]
                        rd2 = sm[:, 144 + 2 * b:146 + 2 * b]
                        sc, pv = [], []
                        ob = 2 + b
                        for j in range(2):
                            o = PS[:, j, 0:nk] if kind == "diff" else PS[:, 0, j * nk:j * nk + nk]
                            if kind == "diff":
                                r = slice(64 * j, 64 * j + 64)
                                sc.append((o, QAT[r, pr, t * P:t * P + P], KAT[r, pr, 0:nk]))
                                ch = [(j * (t + 1) + kc, VA[:, kc, pr * P:pr * P + P]) for kc in range(t + 1)]
                                pv.append((PS[:, ob, j * P:j * P + P], ch))
                            else:
                                h = 2 * pr + j
                                sc.append((o, QBT[0:66, h, t * P:t * P + P], KBT[0:66, h, 0:nk]))
                                ch = [(j * (t + 1) + kc, VB[:, kc, h * 64:h * 64 + 64]) for kc in range(t + 1)]
                                pv.append((PS[:, ob, j * 64:j * 64 + 64], ch))

                        def mask(s2, nk=nk, t=t):
                            if kind == "diff":
                                return [(s2[:, j * nk:j * nk + nk], PS[:, j, 0:nk], mask2[t]) for j in range(2)]
                            m = mask2[t].unsqueeze(1).to_broadcast([P, 2, nk])
                            return [(s2.rearrange("p (a k) -> p a k", a=2),
                                     PS[:, 0, 0:2 * nk].rearrange("p (a k) -> p a k", a=2), m)]

                        def after(pvt, e, t=t, pr=pr, ob=ob, den=den, rd2=rd2):
                            v = V.i(V.at(e, V.last).reciprocal(rd2, den))
                            if kind == "diff":
                                v = V.i(V.at(v, lam_tok).tensor_tensor(rd2[:, 1:2], rd2[:, 1:2], NLAM[:, l:l + 1], ALU.mult))
                                dst = MIX[:, t, pr * P:pr * P + P]
                                v = V.i(V.at(v, pvt, xtp).tensor_scalar(dst, PS[:, ob, 0:P], rd2[:, 0:1], None, ALU.mult))
                                v = V.i(V.at(v).scalar_tensor_tensor(out=dst, in0=PS[:, ob, P:2 * P], scalar=rd2[:, 1:2],
                                                                     in1=dst, op0=ALU.mult, op1=ALU.add))
                            else:
                                dst = MIX[:, t, 512 + pr * P:512 + pr * P + P].rearrange("p (a d) -> p a d", a=2)
                                v = V.i(V.at(v, pvt, xtp).tensor_tensor(
                                    dst, PS[:, ob, 0:P].rearrange("p (a d) -> p a d", a=2),
                                    rd2.unsqueeze(2).to_broadcast([P, 2, 64]), ALU.mult))
                            bank_free[ob] = [v]
                            st[kind] = v

                        rdy = st["qa"] + st["ka"] + [st["va"]] if kind == "diff" else st["qkb"] + [st["vb"]]
                        tasks.append(dict(ready=rdy, scores=sc, n=2 * nk, nsub=2, scale=0.125, mask=mask,
                                          scfree=start_free, den=den, denfree=V.last, obank=ob, ofirst=True, pv=pv, after=after))
                return softmax_tasks(tasks)

            def diff_norm():
                for t in range(T):
                    m = MIX[:, t, 0:512]
                    a = S.i(S.at(st["diff"], V.last).activation(SQ, m, ACT.Square))
                    r4 = sm[:, 40:44]
                    v = V.i(V.at(a).tensor_reduce(r4, SQ.rearrange("p (h m) -> p h m", h=4), AX.X, ALU.add))
                    v = V.i(V.at(v).tensor_scalar(r4, r4, 1.0 / P, EPS, ALU.mult, ALU.add))
                    a = S.i(S.at(v).activation(r4, r4, ACT.Sqrt))
                    v = V.i(V.at(a).reciprocal(r4, r4))
                    m3 = m.rearrange("p (h m) -> p h m", h=4)
                    v = V.i(V.at(v).tensor_tensor(m3, m3, r4.unsqueeze(2).to_broadcast([P, 4, P]), ALU.mult))
                    yield
                st["dn"] = v

            def retention():
                for h in range(4):
                    b = h % 2
                    r = slice(64 * (h % 2), 64 * (h % 2) + 64)
                    c = h // 2
                    PE.at(*st["qkc"], *bank_free[b])
                    nc.tensor.matmul(PS[:, b, 0:256], QKC[r, 2 + c, 0:128], QKC[r, c, 0:256], start=True, stop=True)
                    tk = PE.i(nc.tensor.matmul(PS[:, b, 256:384], QKC[r, 2 + c, 128:256], QKC[r, c, 128:256], start=True, stop=True))
                    V.i(V.at(tk, *ar_free).tensor_tensor(RA[:, h, 0:256], PS[:, b, 0:256], RD[:, h, :], ALU.mult))
                    v = V.i(nc.vector.tensor_tensor(RA[:, h, 256:384], PS[:, b, 256:384], RD[:, h, 0:128], ALU.mult))
                    bank_free[b] = [v]
                yield
                pv = []
                for t in range(T):
                    PE.at(v, st["vgc"], *bank_free[2 + t])
                    for h in range(4):
                        o = PS[:, 2 + t, h * 64:h * 64 + 64]
                        last = nc.tensor.matmul(o, RA[:, h, t * P:t * P + P], VC[:, 0, h * 64:h * 64 + 64], start=True, stop=t == 0)
                        if t:
                            last = nc.tensor.matmul(o, RA[:, h, 256:384], VC[:, 1, h * 64:h * 64 + 64], start=False, stop=True)
                    pv.append(PE.i(last))
                yield
                for t in range(T):
                    o3 = PS[:, 2 + t, 0:256].rearrange("p (h d) -> p h d", h=4)
                    m3 = MIX[:, t, 768:1024].rearrange("p (h d) -> p h d", h=4)
                    r4 = sm[:, 148:152]
                    v = V.i(V.at(pv[t], V.last).tensor_reduce(r4, o3, AX.X, ALU.add))
                    v = V.i(V.at(v).tensor_scalar(r4, r4, 1.0 / 64, None, ALU.mult))
                    v = V.i(V.at(v, xtp).tensor_tensor(m3, o3, r4.unsqueeze(2).to_broadcast([P, 4, 64]), ALU.subtract))
                    bank_free[2 + t] = [v]
                    q3 = SQ[:, 0:256].rearrange("p (h d) -> p h d", h=4)
                    a = S.i(S.at(v).activation(q3, m3, ACT.Square))
                    v = V.i(V.at(a, V.last).tensor_reduce(r4, q3, AX.X, ALU.add))
                    v = V.i(V.at(v).tensor_scalar(r4, r4, 1.0 / 64, EPS, ALU.mult, ALU.add))
                    a = S.i(S.at(v).activation(r4, r4, ACT.Sqrt))
                    v = V.i(V.at(a).reciprocal(r4, r4))
                    v = V.i(V.at(v).tensor_tensor(m3, m3, r4.unsqueeze(2).to_broadcast([P, 4, 64]), ALU.mult))
                    v = V.i(V.at(v, st["vgc"]).tensor_tensor(MIX[:, t, 768:1024], MIX[:, t, 768:1024], GC[:, t, :], ALU.mult))
                    yield
                st["ret"] = v

            def chain(*gens):
                for g in gens:
                    yield from g()

            tk = up(("in2", l, "qa"), 512, xt)
            bg.append(qk_a(QAT, tk, "qa"))
            tick()
            tk = up(("in2", l, "ka"), 512, xt)
            bg.append(qk_a(KAT, tk, "ka"))
            tick()
            tk = up(("in2", l, "va"), 512, xt)
            for t in range(T):
                a = S.i(S.at(tk[t], *ar_free).copy(VA[:, t, :], PS[:, 4 + t, :]))
                bank_free[4 + t] = [a]
            st["va"] = a
            drain()
            tk = up(("in2", l, "vf"), 260, xt)
            bg.append(fox_gate(tk))
            drain()
            tk = up(("in2", l, "qkb"), 512, xt)
            bg.append(qk_b(tk))
            drain()
            tk = up(("in2", l, "qkc"), 512, xt)
            bg.append(qk_a(QKC, tk, "qkc", rot=True))
            drain()

            def seq():
                yield from soft2("diff", [ztr[0], V.last, S.last])
                yield from soft2("fox", [PE.last, V.last, S.last])
                yield from diff_norm()

            bg.append(seq())
            tick()
            tk = up(("in2", l, "vgc"), 512, xt)
            for t in range(T):
                a = S.i(S.at(tk[t], *ar_free).copy(VC[:, t, :], PS[:, 4 + t, 0:256]))
                a = S.i(nc.scalar.activation(GC[:, t, :], PS[:, 4 + t, 256:512], ACT.Silu))
                bank_free[4 + t] = [a]
            st["vgc"] = a
            drain()
            bg.append(retention())
            drain()
            gains = [gc(("sub", l))] * 4 + [None] * 2 + [gc(("rg", l), 0), gc(("rg", l), 1)]
            xy = to_xt(MIX, [st["dn"], st["fox"], st["ret"]], gains)
            v = out_proj(("out2", l), xy)
            xt = norm_t(("nf", l), [v], [xy[2]])
            if l == 0:
                d = mlp(("m2", 0), True, FF2, xt)
            else:
                v = moe(xt)
            if l == 0:
                v = add_x(d)
            xt = norm_t(("pn", l), [v], [xt[2], PE.last])
            PP = AR[:, 0:512].rearrange("p (t n) -> p t n", t=2)
            SGT = AR[:, 2048:4096].rearrange("p (t n) -> p t n", t=2)
            s_p = sem(f"ld_p{l}")
            SP.at(PE.last, V.last, S.last)
            nc.sync.dma_start(PP, dr["p_2"][l, 0].rearrange("(t p) n -> p t n", p=P)).then_inc(s_p, 16)
            pt = to_xt(PP, [(f"ld_p{l}", s_p, 16)], [None] * 2, 0, 2, dst=(HTH, HTL))
            d = down(("pp", l), 256, HTH, HTL, pt, True, True)
            for n in range(2):
                tk = up(("pg", l, n), 512, xt)
                for t in range(T):
                    sg = SGT[:, t, n * 512:n * 512 + 512]
                    xo = X[:, t, n * 512:n * 512 + 512]
                    a = S.i(S.at(tk[t], pt[0], V.last).activation(sg, PS[:, 4 + t, :], ACT.Sigmoid))
                    bank_free[4 + t] = [a]
                    v = V.i(V.at(a, d).tensor_tensor(sg, PS[:, 2 * t + n, :], sg, ALU.mult))
                    bank_free[2 * t + n] = [v]
                    v = V.i(V.at(v).tensor_tensor(xo, xo, sg, ALU.add))
            xr = [v]
            ar_free = [PE.last, v, S.last]

        v = block_norm(dr["final_norm_2"], "ld_f2", XN, xr, [PE.last])
        s_o = sem("s_out")
        SP.at(v)
        nc.sync.dma_start(out[0].rearrange("(t p) d -> p t d", p=P), XN[:, :, :]).then_inc(s_o, 16)
        nc.sync.wait_ge(s_o, 16)


def constants():
    i = np.arange(128)
    cf = np.zeros((128, 1928), np.float32)
    cf[:, 0:128] = np.eye(128)
    cf[:, 128:256] = i[:, None] <= i[None, :]
    cf[:, 256:384] = 1.0
    pos = np.arange(256, dtype=np.float32)
    f1 = (np.float32(500000.0) ** (-np.arange(0, 32, 2, dtype=np.float32) / np.float32(32))).astype(np.float32)
    a1 = (pos[:, None] * f1[None, :]).astype(np.float32).astype(np.float64)
    f2 = (np.float32(10000.0) ** (-np.arange(32, dtype=np.float32) / np.float32(32))).astype(np.float32)
    a2 = (pos[:, None] * f2[None, :]).astype(np.float32).astype(np.float64)
    for o, w, ang in ((384, 32, a1), (512, 64, a2)):
        A = np.concatenate([np.cos(ang), np.cos(ang)], 1).astype(np.float32).reshape(2, 128, w)
        B = np.concatenate([-np.sin(ang), np.sin(ang)], 1).astype(np.float32).reshape(2, 128, w)
        cf[:, o:o + 2 * w] = A.transpose(1, 0, 2).reshape(128, 2 * w)
        cf[:, o + 2 * w:o + 4 * w] = B.transpose(1, 0, 2).reshape(128, 2 * w)
    cf[:, 1800:1928] = np.arange(128)
    lg = np.log1p(-np.exp2(-5.0 - np.arange(4)))
    d = np.arange(256)[None, :] - i[:, None]
    for h in range(4):
        cf[:, 776 + 256 * h:776 + 256 * h + 256] = np.where(d >= 0, np.exp(np.maximum(d, 0) * lg[h]), 0.0) * 0.125
    neg = -1e30
    cb = np.zeros((128, 1408), np.float32)
    for t in range(2):
        q = t * 128 + i[:, None]
        k = np.arange((t + 1) * 128)[None, :]
        for g, (w, dil) in enumerate(((128, 1), (512, 4), (2048, 16))):
            ok = (k <= q) & (q - k <= w) & ((q - k) % dil == 0)
            o = g * 128 if t == 0 else 384 + g * 256
            cb[:, o:o + (t + 1) * 128] = np.where(ok, 0.0, neg)
    cb[:, 1152:1408] = np.where(np.arange(256)[None, :] <= 128 + i[:, None], 0.0, neg)
    ci = np.zeros((128, 1024), np.float32)
    s, t = i[:, None], i[None, :]
    for li, m in enumerate(LEVELS):
        if m == 0:
            ok = s == t
        else:
            ok = (s // (2 * m) == t // (2 * m)) & ((s // m) % 2 == 0) & ((t // m) % 2 == 1)
        ci[:, li * 128:li * 128 + 128] = ok
    return cf, cb, ci


_INS = ["x", "norm1_g", "w_in", "hg_lower_bounds", "hg_norm_g", "w_branch_a", "w_branch_b", "w_out", "norm2_g", "w_up",
        "w_down", "final_norm_g", "p_2", "norm_mix_2", "w_in_2", "b_forget_2", "lambda_q1_2", "lambda_k1_2",
        "lambda_q2_2", "lambda_k2_2", "diff_subln_2", "ret_gn_2", "w_out_2", "norm_ffn_2", "dense_w_gate_2",
        "dense_w_up_2", "dense_w_down_2", "router_2", "moe_w_gate_2", "moe_w_up_2", "moe_w_down_2", "ple_norm_2",
        "ple_gate_2", "ple_proj_2", "final_norm_2"]


def kernel(**inputs):
    from concourse import bacc as _bacc
    from concourse.bass_utils import run_bass_kernel_spmd as _run

    nc = _bacc.Bacc("TRN2", target_bir_lowering=False, num_devices=1)
    arrays, dr = {}, {}
    for name in _INS:
        a = np.ascontiguousarray(inputs[name])
        arrays[f"in_{name}"] = a
        dr[name] = nc.dram_tensor(f"in_{name}", a.shape, mybir.dt.from_np(a.dtype), kind="ExternalInput").ap()
    cs = []
    for name, a in zip(("cf", "cb", "ci"), constants()):
        arrays[f"const_{name}"] = a
        cs.append(nc.dram_tensor(f"const_{name}", a.shape, mybir.dt.from_np(a.dtype), kind="ExternalInput").ap())
    o = nc.dram_tensor("out_0", (1, 256, 1024), F32, kind="ExternalOutput").ap()
    program(nc, dr, cs[0], cs[1], cs[2], o)
    r = _run(nc, [arrays], core_ids=[0])
    return r.results[0]["out_0"]
```

```python
import numpy as np
import concourse.bass as bass
from concourse import mybir
from contextlib import ExitStack

F32 = mybir.dt.float32
F32R = mybir.dt.float32r
BF16 = mybir.dt.bfloat16
I8 = mybir.dt.int8
U32 = mybir.dt.uint32
ALU = mybir.AluOpType
ACT = mybir.ActivationFunctionType
AX = mybir.AxisListType

P = 128
T = 2
D = 1024
EPS = 1e-6
RAW = 5
WR = 3
LAM_INIT = [0.8 - 0.6 * float(np.exp(-0.3 * i)) for i in range(2)]
FF2, FE, NE = 2816, 3584, 8
LEVELS = [0, 1, 2, 4, 8, 16, 32, 64]


class Eng:

    def __init__(self, e, sem):
        self.e, self.sem, self.n, self.seen = e, sem, 0, {}

    def at(self, *toks):
        for tok in toks:
            if tok is None:
                continue
            key, sem, val = tok
            if self.seen.get(key, 0) < val:
                self.seen[key] = val
                self.e.wait_ge(sem, val)
        return self.e

    def i(self, ins):
        ins.then_inc(self.sem, 1)
        self.n += 1
        return (self.sem.name, self.sem, self.n)

    @property
    def last(self):
        return (self.sem.name, self.sem, self.n) if self.n else None


def plan(dr):
    out = []

    def rows(w, kp, c0, n):
        return w[kp * 512:kp * 512 + 512, c0:c0 + n].rearrange("(k p) n -> p k n", p=P)

    def up(key, w, c0, n, K=D):
        for kp in range(K // 512):
            out.append(((key, kp), rows(w, kp, c0, n), 4, n))

    def down(key, w, r0, K):
        for kp in range(K // 256):
            out.append(((key, kp), w[r0 + kp * 256:r0 + kp * 256 + 256, :].rearrange("(k p) n -> p k n", p=P), 2, D))

    def mlp(key, gate, upw, dn, F):
        ng = -(-F // 512)
        for n in range(ng + 1):
            w = min(512, F - n * 512)
            if n < ng:
                if gate is not None:
                    up((key, "g", n), gate, n * 512, w)
                up((key, "u", n), upw, n * 512, w)
            if n:
                down((key, "d", n - 1), dn, (n - 1) * 512, min(512, F - (n - 1) * 512))

    for l in range(2):
        for g in range(17):
            up(("in1", l, g), dr["w_in"][l], g * 512, 512)
        for br in ("a", "b"):
            for n in range(2):
                up(("br" + br, l, n), dr["w_branch_" + br][l], n * 512, 512, 512)
        for n in range(2):
            up(("out1", l, n), dr["w_out"][l], n * 512, 512)
        mlp(("m1", l), None, dr["w_up"][l], dr["w_down"][l], 4096)
    for l in range(2):
        for name, c0, n in (("qa", 0, 512), ("vf", 2048, 260), ("ka", 512, 512), ("va", 1024, 512),
                            ("qkb", 1536, 512), ("qkc", 2308, 512), ("vgc", 2820, 512)):
            up(("in2", l, name), dr["w_in_2"][l], c0, n)
        for kp in range(2):
            for n in range(2):
                out.append(((("out2", l, n), kp), rows(dr["w_out_2"][l], kp, n * 512, 512), 4, 512))
        if l == 0:
            mlp(("m2", 0), dr["dense_w_gate_2"][0], dr["dense_w_up_2"][0], dr["dense_w_down_2"][0], FF2)
        else:
            gr = [(e, n) for e in range(NE) for n in range(FE // 512)]
            for i in range(len(gr) + 1):
                if i < len(gr):
                    e, n = gr[i]
                    up(("moe", "g", e, n), dr["moe_w_gate_2"][0, e], n * 512, 512)
                    up(("moe", "u", e, n), dr["moe_w_up_2"][0, e], n * 512, 512)
                if i:
                    e, n = gr[i - 1]
                    down(("moe", "d", e, n), dr["moe_w_down_2"][0, e], n * 512, 512)
        down(("pp", l), dr["ple_proj_2"][l], 0, 256)
        for n in range(2):
            up(("pg", l, n), dr["ple_gate_2"][l], n * 512, 512)
    return out


def program(nc, dr, cf, cb, ci, out):
    ctx = ExitStack()
    with ctx:
        def sb(name, shape, dt=F32):
            return ctx.enter_context(nc.sbuf_tensor(name, shape, dt))

        def sem(name):
            return ctx.enter_context(nc.semaphore(name))

        PS = ctx.enter_context(nc.psum_tensor("PS", [P, 8, 512], F32))
        raw = sb("raw", [P, RAW, 2048])
        WH = sb("WH", [P, WR, 2048], F32R)
        WL = sb("WL", [P, WR, 2048], F32R)
        XTH = sb("XTH", [P, 8, 256], F32R)
        XTL = sb("XTL", [P, 8, 256], F32R)
        HTH = sb("HTH", [P, 4, 256], F32R)
        HTL = sb("HTL", [P, 4, 256], F32R)
        RTH = sb("RTH", [P, 8, 8], F32R)
        RTL = sb("RTL", [P, 8, 8], F32R)
        X = sb("X", [P, T, D])
        XN = sb("XN", [P, T, D])
        AR = sb("AR", [P, 16384])
        CF = sb("CF", [P, 896])
        PTH = sb("PTH", [P, 2, 256], F32R)
        PTL = sb("PTL", [P, 2, 256], F32R)
        CB = sb("CB", [P, cb.shape[1]], BF16)
        CI = sb("CI", [P, ci.shape[1]], I8)
        G = sb("G", [P, 128])
        GR = sb("GR", [P, 128])
        sm = sb("sm", [P, 256])
        RT = sb("RT", [P, 64])
        LQ = AR[:, 8192:8704].rearrange("p (l j d) -> p l j d", l=2, j=4)
        BF = sb("BF", [P, 2, 4])
        sm2 = sb("sm2", [P, 64])
        CNT = sb("CNT", [P, 1], mybir.dt.int32)
        idx = sb("idx", [P, 2, 8], U32)

        PE = Eng(nc.tensor, sem("s_pe"))
        V = Eng(nc.vector, sem("s_v"))
        S = Eng(nc.scalar, sem("s_s"))
        SP = Eng(nc.sync, sem("s_sp"))

        ident = CF[:, 0:128]
        tri = CF[:, 128:256]
        ones = CF[:, 256:384]
        ropeA = CF[:, 384:448].rearrange("p (t d) -> p t d", t=2)
        ropeB = CF[:, 448:512].rearrange("p (t d) -> p t d", t=2)
        rotA = CF[:, 512:640].rearrange("p (t d) -> p t d", t=2)
        rotB = CF[:, 640:768].rearrange("p (t d) -> p t d", t=2)
        iota = CF[:, 768:896]
        RDA = AR[:, 11264:12288]
        RD = RDA.rearrange("p (h t) -> p h t", h=4)
        mask1 = [CB[:, 0:384].rearrange("p (g k) -> p g k", g=3), CB[:, 384:1152].rearrange("p (g k) -> p g k", g=3)]
        mask2 = [CB[:, 0:128], CB[:, 1152:1408]]
        hmask = [CI[:, i * 128:(i + 1) * 128] for i in range(8)]

        def small(name, pairs, eng=None):
            s = sem(name)
            for a, b in pairs:
                (eng or nc.sync).dma_start(a, b).then_inc(s, 16)
            return (name, s, 16 * len(pairs))

        G0 = AR[0:8, 16256:16384]
        ld_g0 = small("ld_g0", [(G0, dr["norm1_g"][0].rearrange("(c p) -> c p", p=P))], nc.scalar)
        xv = dr["x"][0].rearrange("(t p) d -> p t d", p=P)
        ld_i = small("ld_i", [(CF[:, 0:128], cf[:, 0:128])])
        ld_x = small("ld_x", [(X[:, :, 0:512], xv[:, :, 0:512])])
        ld_y = small("ld_y", [(X[:, :, 512:1024], xv[:, :, 512:1024])])
        rows, pairs = {}, []

        def grow(key, ap, n):
            k = sum(v[1] for v in rows.values())
            rows[key] = (k, n)
            pairs.append((GR[k:k + n, :], ap.rearrange("(c p) -> c p", p=P)))

        for l in range(2):
            if l:
                grow(("n1", l), dr["norm1_g"][l], 8)
            grow(("n2", l), dr["norm2_g"][l], 8)
            grow(("nm", l), dr["norm_mix_2"][l], 8)
            grow(("nf", l), dr["norm_ffn_2"][l], 8)
            grow(("pn", l), dr["ple_norm_2"][l], 8)
            grow(("hb", l), dr["hg_lower_bounds"][l], 4)
            grow(("hn", l), dr["hg_norm_g"][l], 4)
            grow(("sub", l), dr["diff_subln_2"][l], 1)
            grow(("rg", l), dr["ret_gn_2"][l], 2)
        NG = sum(v[1] for v in rows.values())
        rows[("n1", 0)] = (NG, 8)

        PIECES = plan(dr)
        more_raw = [AR[:, 4608 + 2048 * i:4608 + 2048 * (i + 1)] for i in range(5)]
        slots = [raw[:, i, :] for i in range(RAW)] + more_raw
        dsem = [sem(f"ld_w{i}") for i in range(len(slots))]
        raw_free = [[] for _ in slots]
        nfill = [0] * len(slots)
        ready_slots, where = list(range(RAW)), []
        moe_end = max(i for i, x in enumerate(PIECES) if x[0][0][0] == "moe") + 1
        loaded, split_tok, pe_done = [], [], []

        def load():
            i = len(loaded)
            if i >= len(PIECES):
                return
            _, src, nb, n = PIECES[i]
            s = ready_slots.pop(0)
            SP.at(*raw_free[s])
            nc.sync.dma_start(slots[s][:, 0:nb * n].rearrange("p (k n) -> p k n", k=nb), src).then_inc(dsem[s], 16)
            nfill[s] += 1
            where.append(s)
            loaded.append((f"ld_w{s}", dsem[s], 16 * nfill[s]))

        def lend(free):
            for s in range(RAW, len(slots)):
                raw_free[s] = free
                ready_slots.append(s)
                load()

        def split():
            i = len(split_tok)
            if i >= len(PIECES):
                return
            _, _, nb, n = PIECES[i]
            s, w, m = where[i], i % WR, nb * n
            free = pe_done[i - WR] if i >= WR else None
            toks = []
            for o in (0, m // 2):
                c = slice(o, o + m // 2)
                a = S.i(S.at(loaded[i], free).copy(WH[:, w, c], slots[s][:, c]))
                b = V.i(V.at(loaded[i], a, free).tensor_tensor(WL[:, w, c], slots[s][:, c],
                                                               WH[:, w, c].bitcast(F32), ALU.subtract))
                toks.append(b)
            split_tok.append(toks)
            raw_free[s] = [a, b]
            if s < RAW or len(loaded) < moe_end:
                ready_slots.append(s)
                load()

        for _ in range(RAW):
            load()
        ld_c = small("ld_c", [(CF[:, 128:768], cf[:, 128:768]), (CF[:, 768:896], cf[:, 1800:1928]),
                              (AR[:, 1024:2432], cb), (AR[:, 0:1024], ci)])
        ld_g = small("ld_g", pairs)

        bg = []

        def tick():
            for g in list(bg):
                try:
                    next(g)
                except StopIteration:
                    bg.remove(g)

        def drain():
            while bg:
                tick()

        box_tok = [None]

        def second():
            PE.at(box_tok[0])

        def take(key):
            i = len(pe_done)
            assert PIECES[i][0] == key, (PIECES[i][0], key)
            while len(split_tok) < min(i + WR, len(PIECES)):
                split()
            PE.at(split_tok[i][0])
            _, _, nb, n = PIECES[i]
            w = i % WR
            box_tok[0] = split_tok[i][1]
            return [f[:, w, 0:nb * n].rearrange("p (k n) -> p k n", k=nb) for f in (WH, WL)]

        bank_free = [[] for _ in range(8)]

        def mm3(o, lh, ll, rh, rl, start, stop):
            nc.tensor.matmul(o, lh, rh, start=start, stop=False, skip_group_check=True)
            nc.tensor.matmul(o, lh, rl, start=False, stop=False, skip_group_check=True)
            return nc.tensor.matmul(o, ll, rh, start=False, stop=stop, skip_group_check=True)

        fine = [False]

        def up(key, n, N, K=D, k0=0, banks=(4, 5), mid=None, hook=None):
            nk = K // 512
            toks = [None, None]
            for kp in range(nk):
                wh, wl = take((key, kp))
                for t in range(T):
                    if kp == 0:
                        PE.at(*bank_free[banks[t]])
                    for k in range(4):
                        if k == 2:
                            second()
                        PE.at(*N["r"][kp][2 * (k // 2):2 * (k // 2) + 2])
                        kk = k0 + kp * 4 + k
                        last = mm3(PS[:, banks[t], 0:n], XTH[:, kk, t * P:t * P + P], XTL[:, kk, t * P:t * P + P],
                                   wh[:, k, :], wl[:, k, :], kp == 0 and k == 0, kp == nk - 1 and k == 3)
                    if kp == nk - 1 or t == 1:
                        toks[t] = PE.i(last)
                    if t == 0 and kp < nk - 1 and N["r"][kp + 1] is None:
                        N["more"]()
                    if t == 0 and kp == nk - 1 and hook is not None:
                        hook(toks)
                    if t == 0 and fine[0]:
                        tick()
                pe_done.append(toks[1])
                if kp < nk - 1:
                    if mid is not None:
                        mid()
                    tick()
            return toks

        def down(key, K, lh, ll, ready, first, final, mid=None):
            PE.at(*ready)
            nk = K // 256
            toks = [None, None]
            for kp in range(nk):
                wh, wl = take((key, kp))
                for j in range(2):
                    for t in range(T):
                        if first and kp == 0:
                            PE.at(*bank_free[2 * t + j])
                        for k in range(2):
                            if k:
                                second()
                            kk = kp * 2 + k
                            last = mm3(PS[:, 2 * t + j, :], lh[:, kk, t * P:t * P + P], ll[:, kk, t * P:t * P + P],
                                       wh[:, k, j * 512:j * 512 + 512], wl[:, k, j * 512:j * 512 + 512],
                                       first and kk == 0, final and kk == 2 * nk - 1)
                        if mid is not None and (kp, j, t) == (nk - 1, 1, 0):
                            PE.i(last)
                            mid(toks)
                    if j == 1 or kp == nk - 1:
                        toks[j] = PE.i(last)
                pe_done.append(toks[1])
                tick()
            return toks

        PE.at(ld_i, ld_g0)
        t0 = PE.i(nc.tensor.transpose(PS[:, 7, 0:8], G0, ident[0:8, 0:8]))
        gains = {"tok": V.i(V.at(t0).tensor_copy(G[:, NG:NG + 8], PS[:, 7, 0:8]))}
        bank_free[7] = [gains["tok"]]

        def gc(key, c=0, n=1):
            return G[:, rows[key][0] + c:rows[key][0] + c + n]

        LB = sm[:, 0:4]
        OMB = sm[:, 4:8]
        lt = sm[:, 8:32]

        def params():
            S.at(ld_c)
            PE.at(ld_c)
            V.i(V.at(ld_c).tensor_copy(CB[:, :], AR[:, 1024:2432]))
            gains["ci"] = V.i(V.at(ld_c).tensor_copy(CI[:, :], AR[:, 0:1024]))

        def params2():
            PE.at(ld_g, *bank_free[7])
            t0 = PE.i(nc.tensor.transpose(PS[:, 7, 0:NG], GR[0:NG, :], ident[0:NG, 0:NG]))
            g = V.i(V.at(t0).tensor_copy(G[:, 0:NG], PS[:, 7, 0:NG]))
            gains["tok"] = g
            bank_free[7] = [g]
            yield
            a = V.i(V.at(g).tensor_tensor(lt[:, 0:4], gc(("hb", 0), 0, 4), gc(("hb", 1), 0, 4), ALU.max))
            a = V.i(V.at(a).tensor_tensor(lt[:, 4:8], gc(("hb", 0), 0, 4), lt[:, 0:4], ALU.subtract))
            a = V.i(V.at(a).tensor_tensor(lt[:, 8:12], gc(("hb", 1), 0, 4), lt[:, 0:4], ALU.subtract))
            a = S.i(S.at(a).activation(lt[:, 12:20], lt[:, 4:12], ACT.Exp))
            a = V.i(V.at(a).tensor_tensor(lt[:, 20:24], lt[:, 12:16], lt[:, 16:20], ALU.add))
            a = V.i(V.at(a).reciprocal(lt[:, 20:24], lt[:, 20:24]))
            a = V.i(V.at(a).tensor_tensor(LB, lt[:, 16:20], lt[:, 20:24], ALU.mult))
            gains["lb"] = V.i(V.at(a).tensor_scalar(OMB, LB, -1.0, 1.0, ALU.mult, ALU.add))

        ss = sm[:, 32:34]
        rs = sm[:, 34:36]

        def rstd(ready, junk_free):
            for t in range(T):
                a = S.i(S.at(*(ready[t] if isinstance(ready, tuple) else ready), *junk_free).activation(XN[:, t, :], X[:, t, :], ACT.Square,
                                                            accum_out=ss[:, t:t + 1]))
            a = V.i(V.at(a).tensor_scalar(rs, ss, 1.0 / D, EPS, ALU.mult, ALU.add))
            a = S.i(S.at(a).activation(rs, rs, ACT.Sqrt))
            return V.i(V.at(a).reciprocal(rs, rs))

        def half(src, h, ready, gn, dst=None, nch=4, s0=None):
            dh, dl = dst if dst is not None else (XTH, XTL)
            s0 = 4 * h if s0 is None else s0
            free = PE.last
            wr = []
            for r in range(nch // 2):
                b = 6 + r
                PE.at(*(ready[r] if isinstance(ready, tuple) else ready), *bank_free[b])
                for c in range(2):
                    for t in range(T):
                        cc = s0 + 2 * r + c
                        last = nc.tensor.transpose(PS[:, b, c * 256 + t * P:c * 256 + t * P + P],
                                                   src[:, t, cc * P:cc * P + P], ident)
                tp = PE.i(last)
                S.at(tp, free, gains["tok"])
                V.at(free)
                g2 = gn[2 * r:2 * r + 2]
                d0 = 4 * h + 2 * r
                if g2 == [None, None]:
                    pv = PS[:, b, :].rearrange("p (c m) -> p c m", c=2)
                    a = S.i(nc.scalar.copy(dh[:, d0:d0 + 2, :], pv))
                    v = V.i(V.at(a).tensor_tensor(dl[:, d0:d0 + 2, :], pv, dh[:, d0:d0 + 2, :].bitcast(F32), ALU.subtract))
                else:
                    for c in range(2):
                        a = S.i(nc.scalar.activation(dh[:, d0 + c, :], PS[:, b, c * 256:c * 256 + 256], ACT.Copy, scale=g2[c]))
                    for c in range(2):
                        v = V.i(V.at(a).scalar_tensor_tensor(
                            out=dl[:, d0 + c, :], in0=PS[:, b, c * 256:c * 256 + 256], scalar=g2[c],
                            in1=dh[:, d0 + c, :].bitcast(F32), op0=ALU.mult, op1=ALU.subtract))
                wr += [a, v]
                bank_free[b] = [a, v]
            return wr

        def norm_start(key, x0, x1=None):
            N = {"r": [half(X, 0, x0, [gc(key, c) for c in range(4)]), None], "x1": x1}

            def more():
                N["r"][1] = half(X, 1, N["x1"], [gc(key, 4 + c) for c in range(4)])
                N["rs"] = rstd([*x0, *N["x1"]], [PE.last, V.last])

            N["more"] = more
            return N

        def whole(src, r0, r1, gn):
            N = {"r": [half(src, 0, r0, gn[0:4]), None]}

            def more():
                N["r"][1] = half(src, 1, r1() if callable(r1) else r1, gn[4:8])

            N["more"] = more
            return N

        def load_gain(gain_dram, name, gb):
            s = sem(name)
            SP.at(PE.last, V.last, S.last)
            nc.sync.dma_start(gb, gain_dram.partition_broadcast(P)).then_inc(s, 16)
            return gb, (name, s, 16)

        def last_norm(gain, dst, xready):
            gb, ld = gain
            r = rstd(xready, [v_free])
            return [V.i(V.at(r, ld).scalar_tensor_tensor(out=dst[:, t, :], in0=X[:, t, :], scalar=rs[:, t:t + 1], in1=gb,
                                                         op0=ALU.mult, op1=ALU.mult)) for t in range(T)]

        def two_norms(gain, key, x0):
            gb, ld = gain

            def times_gain(j, ready):
                js = slice(j * 512, j * 512 + 512)
                for t in range(T):
                    v = V.i(V.at(ready, ld, PE.last).tensor_tensor(XN[:, t, js], X[:, t, js], gb[:, js], ALU.mult))
                return v

            N = {"r": [half(XN, 0, [times_gain(0, x0)], [gc(key, c) for c in range(4)]), None]}

            def more():
                xr = N["x1"][0]
                g = times_gain(1, xr)
                N["r"][1] = half(XN, 1, [g], [gc(key, 4 + c) for c in range(4)])
                q2, r2, r1 = sm[:, 208:210], sm[:, 210:212], sm[:, 212:214]
                junk = [AR[:, 2048 + 1024 * i:3072 + 1024 * i] for i in range(4)]
                for t in range(T):
                    a = S.i(S.at(xr, V.last).activation(junk[2 * t], X[:, t, :], ACT.Square, accum_out=ss[:, t:t + 1]))
                    a = S.i(S.at(g, a).activation(junk[2 * t + 1], XN[:, t, :], ACT.Square, accum_out=q2[:, t:t + 1]))
                v = V.i(V.at(a).tensor_scalar(r1, ss, 1.0 / D, EPS, ALU.mult, ALU.add))
                a = S.i(S.at(v).activation(r1, r1, ACT.Sqrt))
                v = V.i(V.at(a).reciprocal(r1, r1))
                v = V.i(V.at(v).tensor_tensor(q2, q2, r1, ALU.mult))
                v = V.i(V.at(v).tensor_tensor(q2, q2, r1, ALU.mult))
                v = V.i(V.at(v).tensor_scalar(r2, q2, 1.0 / D, EPS, ALU.mult, ALU.add))
                a = S.i(S.at(v).activation(r2, r2, ACT.Sqrt))
                r = V.i(V.at(a).reciprocal(r2, r2))
                N["rs"] = V.i(V.at(r).tensor_tensor(rs, r1, r2, ALU.mult))
                for t in range(T):
                    V.i(V.at(r).tensor_scalar(X[:, t, :], XN[:, t, :], r1[:, t:t + 1], None, ALU.mult))

            N["more"] = more
            return N

        HM = AR[:, 15360:16384].rearrange("p (t n) -> p t n", t=2)

        def mlp(key, gated, F, ready, mid=None):
            ng = -(-F // 512)
            hm_tok = None
            tr_last, v_free = [None], V.last
            for n in range(ng + 1):
                w = min(512, F - n * 512)
                state = {}

                def turn(n=n):
                    wp = min(512, F - (n - 1) * 512)
                    toks = []
                    pd = PE.last
                    for r in range(wp // 256):
                        b = 6 + r
                        PE.at(*hm_tok, *bank_free[b])
                        for c in range(2):
                            for t in range(T):
                                last = nc.tensor.transpose(PS[:, b, c * 256 + t * P:c * 256 + t * P + P],
                                                           HM[:, t, (2 * r + c) * P:(2 * r + c) * P + P], ident)
                        tp = PE.i(last)
                        pv = PS[:, b, :].rearrange("p (c m) -> p c m", c=2)
                        a = S.i(S.at(tp, pd).copy(HTH[:, 2 * r:2 * r + 2, :], pv))
                        v = V.i(V.at(a, tp, pd).tensor_tensor(HTL[:, 2 * r:2 * r + 2, :], pv,
                                                              HTH[:, 2 * r:2 * r + 2, :].bitcast(F32), ALU.subtract))
                        bank_free[b] = [a, v]
                        toks += [a, v]
                    state["ht"] = toks
                    tr_last[0] = PE.last

                if n < ng:
                    if gated:
                        tg = up((key, "g", n), w, ready, mid=turn if n else None)
                        sil = []
                        for t in range(T):
                            a = S.i(S.at(tg[t], tr_last[0], v_free, ready["rs"]).activation(
                                HM[:, t, 0:w], PS[:, 4 + t, 0:w], ACT.Silu, scale=rs[:, t:t + 1]))
                            bank_free[4 + t] = [a]
                            sil.append(a)
                        tick()
                        tu = up((key, "u", n), w, ready)
                        new = []
                        for t in range(T):
                            v = V.i(V.at(tu[t], sil[t]).scalar_tensor_tensor(
                                out=HM[:, t, 0:w], in0=PS[:, 4 + t, 0:w], scalar=rs[:, t:t + 1], in1=HM[:, t, 0:w],
                                op0=ALU.mult, op1=ALU.mult))
                            bank_free[4 + t] = [v]
                            new.append(v)
                    else:
                        tu = up((key, "u", n), w, ready, mid=turn if n else None)
                        new = []
                        for t in range(T):
                            a = S.i(S.at(tu[t], tr_last[0], v_free, ready["rs"]).activation(
                                HM[:, t, 0:w], PS[:, 4 + t, 0:w], ACT.Relu, scale=rs[:, t:t + 1]))
                            v = V.i(V.at(a).scalar_tensor_tensor(
                                out=HM[:, t, 0:w], in0=PS[:, 4 + t, 0:w], scalar=rs[:, t:t + 1],
                                in1=HM[:, t, 0:w], op0=ALU.mult, op1=ALU.mult))
                            bank_free[4 + t] = [v]
                            new.append(v)
                    hm_next = new
                    tick()
                else:
                    turn()
                if n:
                    d = down((key, "d", n - 1), min(512, F - (n - 1) * 512), HTH, HTL, state["ht"],
                             n == 1, n == ng, mid if n == ng else None)
                hm_tok = hm_next
            return d

        def add_x(tok, j):
            for t in range(T):
                v = V.i(V.at(tok).tensor_tensor(X[:, t, j * 512:j * 512 + 512], PS[:, 2 * t + j, :],
                                                X[:, t, j * 512:j * 512 + 512], ALU.add))
                bank_free[2 * t + j] = [v]
            return v

        def mlp_x(key, gated, F, ready, start):
            box = {}

            def mid(toks):
                box["v"] = add_x(toks[0], 0)
                if start is not None:
                    box["n"] = start(box["v"])

            d = mlp(key, gated, F, ready, mid)
            v = add_x(d[1], 1)
            if start is not None:
                box["n"]["x1"] = [v]
            return box.get("n"), [box["v"], v]

        def out_proj(key, N, nkey):
            box = {}

            def early():
                box["n"] = norm_start(nkey, [box["v"]])

            for n in range(2):
                tk = up((key[0], key[1], n), 512, N, mid=early if n else None)
                for t in range(T):
                    v = V.i(V.at(tk[t]).tensor_tensor(X[:, t, n * 512:n * 512 + 512], PS[:, 4 + t, :],
                                                      X[:, t, n * 512:n * 512 + 512], ALU.add))
                    bank_free[4 + t] = [v]
                box["v"] = v
                tick()
            box["n"]["x1"] = [v]
            return box["n"]

        SEL = sm2[:, 0:16]
        SLOT = sm2[:, 16:32]
        SLOT2 = sm2[:, 32:48]
        COMB = sm2[:, 48:64]

        def moe(xt):
            xt["more"]()
            PE.at(par["rt"], *xt["r"][0], *xt["r"][1], *bank_free[7])
            for k in range(8):
                last = mm3(PS[0:8, 7, 0:256], RTH[:, k, :], RTL[:, k, :], XTH[:, k, :], XTL[:, k, :], k == 0, k == 7)
            tk = PE.i(last)
            LT = AR[0:8, 1536:1792]
            PE.at(V.i(V.at(tk, *ar_free).tensor_copy(LT, PS[0:8, 7, 0:256])))
            for t in range(T):
                last = nc.tensor.transpose(PS[:, 7, 256 + 8 * t:264 + 8 * t], LT[:, t * P:t * P + P], ident[0:8, 0:8])
            tk = PE.i(last)
            for t in range(T):
                xn_tok = S.i(S.at(xt["rs"]).mul(XN[:, t, :], X[:, t, :], rs[:, t:t + 1]))

            def te(ap):
                return ap.rearrange("p (t e) -> p t e", t=2)

            lg, mx, f8, oh, o1 = (te(sm[:, o:o + 16]) for o in (212, 152, 168, 184, 228))
            d1, e1, w1, w2 = (sm[:, o:o + 2] for o in (246, 248, 250, 252))
            shape = [P, 2, 8]
            io = iota[:, 0:8].unsqueeze(1).to_broadcast(shape)
            v = V.i(V.at(tk, xt["rs"]).tensor_tensor(lg, te(PS[:, 7, 256:272]), rs.unsqueeze(2).to_broadcast(shape), ALU.mult))
            bank_free[7] = [v]
            for t in range(T):
                m = V.i(V.at(v).max(mx[:, t, :], lg[:, t, :]))
                x = V.i(V.at(m).max_index(idx[:, t, :], mx[:, t, :], lg[:, t, :]))
            v = V.i(V.at(x).tensor_copy(f8, idx[:, :, :]))
            V.i(V.at(v).tensor_tensor(o1, io, f8[:, :, 0:1].to_broadcast(shape), ALU.is_equal))
            v = V.i(nc.vector.tensor_tensor(oh, io, f8[:, :, 1:2].to_broadcast(shape), ALU.is_equal))
            sel_tok = V.i(V.at(v).tensor_tensor(te(SEL), o1, oh, ALU.add))
            PE.at(sel_tok, *bank_free[7])
            nc.tensor.matmul(PS[:, 7, 0:8], tri, SEL[:, 0:8], start=True, stop=True)
            nc.tensor.matmul(PS[:, 7, 8:16], ones, SEL[:, 0:8], start=True, stop=False)
            nc.tensor.matmul(PS[:, 7, 8:16], tri, SEL[:, 8:16], start=False, stop=True)
            nc.tensor.matmul(PS[:, 7, 16:24], ones, SEL[:, 0:8], start=True, stop=False)
            tk = PE.i(nc.tensor.matmul(PS[:, 7, 16:24], ones, SEL[:, 8:16], start=False, stop=True))
            v = V.i(V.at(sel_tok).tensor_tensor(d1, mx[:, :, 1], mx[:, :, 0], ALU.subtract))
            a = S.i(S.at(v).activation(e1, d1, ACT.Exp))
            v = V.i(V.at(a).tensor_scalar(w1, e1, 1.0, None, ALU.add))
            v = V.i(V.at(v).reciprocal(w1, w1))
            v = V.i(V.at(v).tensor_tensor(w2, e1, w1, ALU.mult))
            V.i(V.at(v).tensor_tensor(o1, o1, w1.unsqueeze(2).to_broadcast(shape), ALU.mult))
            v = V.i(nc.vector.tensor_tensor(oh, oh, w2.unsqueeze(2).to_broadcast(shape), ALU.mult))
            V.i(V.at(v).tensor_tensor(te(COMB), o1, oh, ALU.add))
            v = V.i(V.at(tk).tensor_tensor(SLOT, PS[:, 7, 0:16], SEL, ALU.mult))
            v = V.i(V.at(v).tensor_scalar(SLOT, SLOT, -1.0, None, ALU.add))
            V.i(V.at(v).tensor_scalar(SLOT2, SLOT, -128.0, None, ALU.add))
            v = V.i(V.at(v).tensor_reduce(sm[:, 244:245], PS[:, 7, 16:24], AX.X, ALU.max))
            bank_free[7] = [v]
            cnt_tok = slot_tok = V.i(V.at(v).tensor_copy(CNT[:, :], sm[:, 244:245]))
            nfg = [gc(("nf", 1), c) for c in range(8)]

            GPM = AR[:, 0:512].rearrange("p (b t j) -> p b t j", b=2, t=2)
            PCM = AR[:, 512:1024].rearrange("p (b t j) -> p b t j", b=2, t=2)
            PTM = AR[:, 1024:1536].rearrange("p (b m) -> p b m", b=2)
            YE = AR[:, 1536:2560]
            HX = AR[:, 15360:16384].rearrange("p (b n) -> p b n", b=2)
            xg, ptm, up_last, sc_last = {}, {}, {}, {}

            def select(g, pc, slot, e, wait):
                for t in range(T):
                    k = 8 * t + e
                    V.i(V.at(*wait).tensor_scalar(g[:, t, :], iota, slot[:, k:k + 1], None, ALU.is_equal))
                    v = V.i(nc.vector.tensor_scalar(pc[:, t, :], iota, slot[:, k:k + 1], COMB[:, k:k + 1],
                                                    ALU.is_equal, ALU.mult))
                return v

            def prep(e):
                b = e % 2
                sl = slice(b * P, b * P + P)
                v = select(GPM[:, b], PCM[:, b], SLOT, e, [slot_tok, *ar_free, up_last.get(e - 2)])
                yield
                wr = xg[e] = []
                for half, bank in enumerate((7, 3)):
                    PE.at(v, xn_tok, *bank_free[bank])
                    for c in range(4):
                        cc = 4 * half + c
                        for t in range(T):
                            last = nc.tensor.matmul(PS[:, bank, c * P:c * P + P], XN[:, t, cc * P:cc * P + P],
                                                    GPM[:, b, t, :], start=t == 0, stop=t == 1)
                    tk = PE.i(last)
                    for c in range(4):
                        cc = 4 * half + c
                        a = S.i(S.at(tk, up_last.get(e - 2)).activation(XTH[:, cc, sl], PS[:, bank, c * P:c * P + P], ACT.Copy,
                                                     scale=nfg[cc]))
                    for c in range(4):
                        cc = 4 * half + c
                        w = V.i(V.at(a, tk, up_last.get(e - 2)).scalar_tensor_tensor(
                            out=XTL[:, cc, sl], in0=PS[:, bank, c * P:c * P + P], scalar=nfg[cc],
                            in1=XTH[:, cc, sl].bitcast(F32), op0=ALU.mult, op1=ALU.subtract))
                    bank_free[bank] = [w]
                    wr += [a, w]
                    yield
                PE.at(v, *bank_free[7])
                for t in range(T):
                    last = nc.tensor.transpose(PS[:, 7, t * P:t * P + P], PCM[:, b, t, :], ident)
                tk = PE.i(last)
                w = V.i(V.at(tk, sc_last.get(e - 2)).tensor_copy(PTM[:, b, :], PS[:, 7, 0:256]))
                bank_free[7] = [w]
                ptm[e] = w
                yield

            def up1(key, e, bank, mid=None):
                sl = slice((e % 2) * P, (e % 2) * P + P)
                for kp in range(2):
                    PE.at(*xg[e][2 * kp:2 * kp + 2])
                    wh, wl = take((key, kp))
                    if kp == 0:
                        PE.at(*bank_free[bank])
                    for k in range(4):
                        if k == 2:
                            second()
                        last = mm3(PS[:, bank, :], XTH[:, 4 * kp + k, sl], XTL[:, 4 * kp + k, sl], wh[:, k, :], wl[:, k, :],
                                   kp + k == 0, kp == 1 and k == 3)
                    pe_done.append(PE.i(last))
                    if kp == 0 and mid is not None:
                        mid()
                    tick()
                return PE.last

            def put_back(e, d):
                a = S.i(S.at(d, sc_last.get(e - 1)).copy(YE[:, 0:512], PS[:, 0, :]))
                v = V.i(V.at(d, sc_last.get(e - 1)).tensor_copy(YE[:, 512:1024], PS[:, 1, :]))
                bank_free[0], bank_free[1] = [a], [v]
                yield
                yield
                for t in range(T):
                    for j in range(2):
                        PE.at(a, v, ptm[e], *bank_free[2 + j])
                        tk = PE.i(nc.tensor.matmul(PS[:, 2 + j, :], PTM[:, e % 2, t * P:t * P + P],
                                                   YE[:, j * 512:j * 512 + 512], start=True, stop=True))
                        xo = X[:, t, j * 512:j * 512 + 512]
                        w = V.i(V.at(tk).tensor_tensor(xo, PS[:, 2 + j, :], xo, ALU.add))
                        bank_free[2 + j] = [w]
                        yield
                sc_last[e] = tk

            first = prep(0)
            while len(xg.get(0, [])) < 4:
                next(first)
            bg.append(first)
            gr = [(e, n) for e in range(NE) for n in range(FE // 512)]
            hm = {}
            ht = {}

            def turn(i):
                pd = PE.last
                PE.at(hm[i], *bank_free[6])
                for c in range(4):
                    last = nc.tensor.transpose(PS[:, 6, c * P:c * P + P], HX[:, i % 2, c * P:c * P + P], ident)
                tp = PE.i(last)
                pv = PS[:, 6, :].rearrange("p (c m) -> p c m", c=4)
                a = S.i(S.at(tp, pd).copy(HTH[:, :, 0:P], pv))
                w = V.i(V.at(a, tp, pd).tensor_tensor(HTL[:, :, 0:P], pv, HTH[:, :, 0:P].bitcast(F32), ALU.subtract))
                bank_free[6] = [a, w]
                ht[i] = [a, w, tp]

            for i in range(len(gr) + 1):
                if i < len(gr):
                    e, n = gr[i]
                    if n == 0 and len(xg.get(e, [])) < 4:
                        drain()
                    tg = up1(("moe", "g", e, n), e, 4, mid=(lambda i=i: turn(i - 1)) if i else None)
                    hx = HX[:, i % 2, :]
                    old = ht[i - 2][2] if i >= 2 else None
                    a = S.i(S.at(tg, old, *ar_free).activation(hx, PS[:, 4, :], ACT.Silu))
                    bank_free[4] = [a]
                    tu = up1(("moe", "u", e, n), e, 5)
                    w = V.i(V.at(tu, a).tensor_tensor(hx, PS[:, 5, :], hx, ALU.mult))
                    bank_free[5] = [w]
                    hm[i] = w
                    if n == FE // 512 - 1:
                        up_last[e] = PE.last
                    if n == 2 and e + 1 < NE:
                        bg.append(prep(e + 1))
                else:
                    turn(i - 1)
                if i:
                    e, n = gr[i - 1]
                    PE.at(*ht[i - 1])
                    if n == 0:
                        PE.at(*bank_free[0], *bank_free[1])
                    for kp in range(2):
                        wh, wl = take((("moe", "d", e, n), kp))
                        for j in range(2):
                            for k in range(2):
                                if k:
                                    second()
                                kk = kp * 2 + k
                                js = slice(j * 512, j * 512 + 512)
                                last = mm3(PS[:, j, :], HTH[:, kk, 0:P], HTL[:, kk, 0:P], wh[:, k, js], wl[:, k, js],
                                           n == 0 and kk == 0, n == FE // 512 - 1 and kk == 3)
                        pe_done.append(PE.i(last))
                        tick()
                    if n == FE // 512 - 1:
                        bg.append(put_back(e, PE.last))
            drain()

            engs = (PE, V, S, SP)
            for E in (PE, S, SP):
                E.at(cnt_tok)
            V.at(cnt_tok)
            over = nc.values_load(CNT[0:1, 0:1], engines=[mybir.EngineType.PE, mybir.EngineType.DVE,
                                                          mybir.EngineType.Activation, mybir.EngineType.SP],
                                  min_val=0, max_val=256)
            before = [(E, E.n, dict(E.seen)) for E in engs]
            WB = AR[:, 2560:6656].rearrange("p (b n) -> p b n", b=2)
            XG2 = AR[:, 12288:13312].rearrange("p (c j) -> p c j", c=8)
            H2 = AR[:, 13312:13824]
            HT2 = AR[:, 14336:14848].rearrange("p (c j) -> p c j", c=4)
            G2 = AR[:, 7168:7424].rearrange("p (t j) -> p t j", t=2)
            PC2 = AR[:, 7424:7680].rearrange("p (t j) -> p t j", t=2)
            PT2 = AR[:, 7680:7936]
            osem = [sem("ld_o0"), sem("ld_o1")]
            with nc.If(over > 128):
                nload = [0]
                buf_free = [PE.last, PE.last]

                def fetch(src, kb, n):
                    i = nload[0]
                    nload[0] += 1
                    b = i % 2
                    SP.at(buf_free[b], V.last if i < 2 else None)
                    nc.sync.dma_start(WB[:, b, 0:kb * n].rearrange("p (k n) -> p k n", k=kb),
                                      src.rearrange("(k p) n -> p k n", p=P)).then_inc(osem[b], 16)
                    PE.at((f"ld_o{b}", osem[b], 16 * (i // 2 + 1)))
                    return WB[:, b, 0:kb * n].rearrange("p (k n) -> p k n", k=kb), b

                for e in range(NE):
                    v = select(G2, PC2, SLOT2, e, [slot_tok, PE.last])
                    for half in range(2):
                        PE.at(v, V.last)
                        for c in range(4):
                            cc = 4 * half + c
                            for t in range(T):
                                last = nc.tensor.matmul(PS[:, half, c * P:c * P + P], XN[:, t, cc * P:cc * P + P],
                                                        G2[:, t, :], start=t == 0, stop=t == 1)
                        tk = PE.i(last)
                        for c in range(4):
                            cc = 4 * half + c
                            w = V.i(V.at(tk).tensor_scalar(XG2[:, cc, :], PS[:, half, c * P:c * P + P], nfg[cc], None,
                                                           ALU.mult))
                    PE.at(w)
                    for t in range(T):
                        last = nc.tensor.transpose(PS[:, 2, t * P:t * P + P], PC2[:, t, :], ident)
                    tk = PE.i(last)
                    v = V.i(V.at(tk).tensor_copy(PT2, PS[:, 2, 0:256]))
                    for n in range(FE // 512):
                        cs = slice(n * 512, n * 512 + 512)
                        for which, w_ in enumerate((dr["moe_w_gate_2"], dr["moe_w_up_2"])):
                            PE.at(V.last, S.last)
                            for kp in range(2):
                                wb, b = fetch(w_[0, e, kp * 512:kp * 512 + 512, cs], 4, 512)
                                for k in range(4):
                                    last = nc.tensor.matmul(PS[:, 4 + which, :], XG2[:, 4 * kp + k, :], wb[:, k, :],
                                                            start=kp + k == 0, stop=kp == 1 and k == 3)
                                buf_free[b] = PE.i(last)
                        tk = PE.last
                        a = S.i(S.at(tk).activation(H2, PS[:, 4, :], ACT.Silu))
                        v = V.i(V.at(tk, a).tensor_tensor(H2, PS[:, 5, :], H2, ALU.mult))
                        PE.at(v)
                        for c in range(4):
                            last = nc.tensor.transpose(PS[:, 6, c * P:c * P + P], H2[:, c * P:c * P + P], ident)
                        tk = PE.i(last)
                        v = V.i(V.at(tk).tensor_copy(HT2, PS[:, 6, :].rearrange("p (c j) -> p c j", c=4)))
                        PE.at(v)
                        for kp in range(2):
                            wb, b = fetch(dr["moe_w_down_2"][0, e, n * 512 + kp * 256:n * 512 + kp * 256 + 256, :], 2, D)
                            for j in range(2):
                                for k in range(2):
                                    last = nc.tensor.matmul(PS[:, j, :], HT2[:, 2 * kp + k, :], wb[:, k, j * 512:j * 512 + 512],
                                                            start=n == 0 and kp + k == 0,
                                                            stop=n == FE // 512 - 1 and kp + k == 2,
                                                            skip_group_check=True)
                            buf_free[b] = PE.i(last)
                    for j in range(2):
                        v = V.i(V.at(PE.last).tensor_copy(YE[:, j * 512:j * 512 + 512], PS[:, j, :]))
                    for t in range(T):
                        for j in range(2):
                            PE.at(V.last)
                            tk = PE.i(nc.tensor.matmul(PS[:, 2 + j, :], PT2[:, t * P:t * P + P], YE[:, j * 512:j * 512 + 512],
                                                       start=True, stop=True))
                            xo = X[:, t, j * 512:j * 512 + 512]
                            V.i(V.at(tk).tensor_tensor(xo, PS[:, 2 + j, :], xo, ALU.add))
            with nc.Else():
                for E, n0, _ in before:
                    if E.n > n0:
                        E.e.wait_ge(E.sem, n0)
                        E.e.sem_inc(E.sem, E.n - n0)
            nc.end_ifs()
            for E, _, seen in before:
                E.seen = seen
            for b in range(8):
                bank_free[b] = [V.last, PE.last, S.last]
            return [V.last]

        QT = AR[:, 0:3072].rearrange("p (g h m) -> p g h m", g=3, h=4)
        KT = AR[:, 3072:6144].rearrange("p (g h m) -> p g h m", g=3, h=4)
        VV = AR[:, 6144:9216].rearrange("p (t g n) -> p t g n", t=2, g=3)
        GG = AR[:, 9216:10240].rearrange("p (t n) -> p t n", t=2)
        VH = AR[:, 6144:7168].rearrange("p (t n) -> p t n", t=2)
        SG = AR[:, 7168:8192]
        TOT = AR[:, 8192:9216]
        HQ = AR[:, 10240:11264]
        HK = AR[:, 11264:12288]
        ATT = AR[:, 12288:13312].rearrange("p (a m) -> p a m", a=8)
        ATX = AR[:, 13312:13824].rearrange("p (h m) -> p h m", h=4)
        TT = AR[:, 13824:14336]
        ZT = AR[:, 14336:15360].rearrange("p (t n) -> p t n", t=2)
        RP = AR[:, 15360:15872].rearrange("p (t x) -> p t x", t=2)
        ZB = AR[:, 10240:12288].rearrange("p (t n) -> p t n", t=2)
        SC = AR[:, 12288:13824].rearrange("p (b n) -> p b n", b=2)
        PT = AR[:, 13824:15360].rearrange("p (b n) -> p b n", b=2)
        OA = AR[:, 15360:16384].rearrange("p (t n) -> p t n", t=2)

        def turn_heads(src, ready, np_=P, nh=4, wd=P):
            toks = []
            for b in range(nh // 2):
                PE.at(*ready, *bank_free[6 + b])
                for c in range(2):
                    for t in range(T):
                        last = nc.tensor.transpose(PS[0:wd, 6 + b, c * 256 + t * P:c * 256 + t * P + P],
                                                   src(t, 2 * b + c), ident)
                toks.append(PE.i(last))
            return toks

        def hgrn(l, st):
            free = st["at_free"]
            z = V.i(V.at(*free).memset(AR[:, 12288:13312], 0.0))
            q4 = HQ.rearrange("p (a m) -> p a m", m=P)
            k4 = HK.rearrange("p (a m) -> p a m", m=P)
            ready = st["qk"]
            tot_tok = st["f"]
            tot = TOT
            alt = TT
            for li, m in enumerate(LEVELS):
                pt = []
                if m == 0:
                    for b in range(2):
                        PE.at(*ready, *bank_free[b])
                        for a_ in range(4):
                            last = nc.tensor.matmul(PS[:, b, a_ * P:a_ * P + P], k4[:, 4 * b + a_, :], q4[:, 4 * b + a_, :],
                                                    start=True, stop=True)
                        pt.append(PE.i(last))
                    yield
                    for b in range(2):
                        v = V.i(V.at(pt[b], z, V.last).copy_predicated(
                            ATT[:, 4 * b:4 * b + 4, :], hmask[li].unsqueeze(1).to_broadcast([P, 4, P]),
                            PS[:, b, :].rearrange("p (a m) -> p a m", a=4)))
                        bank_free[b] = [v]
                else:
                    b, nbk = li % 2, 64 // m
                    PE.at(*ready, *bank_free[b])
                    for a_ in range(8):
                        last = nc.tensor.matmul(
                            PS[:, b, a_ * 64:a_ * 64 + 64].rearrange("p (b m) -> p b m", m=m), k4[:, a_, :],
                            q4[:, a_, :].rearrange("p (b w m) -> p b w m", w=2, m=m)[:, :, 1, :], start=True, stop=True)
                    pt.append(PE.i(last))
                    yield
                    mk = hmask[li].rearrange("p (b w m) -> p b w m", w=2, m=m)[:, :, 1, :]
                    dst = ATT.rearrange("p a (b w m) -> p a b w m", w=2, m=m)[:, :, :, 1, :]
                    pv_ = PS[:, b, :].rearrange("p (a b m) -> p a b m", a=8, m=m)
                    if m == 1:
                        v = V.i(V.at(pt[0], V.last).copy_predicated(
                            dst[:, :, :, 0], mk[:, :, 0].unsqueeze(1).to_broadcast([P, 8, nbk]), pv_[:, :, :, 0]))
                    elif m == 64:
                        v = V.i(V.at(pt[0], V.last).copy_predicated(
                            dst[:, :, 0, :], mk[:, 0, :].unsqueeze(1).to_broadcast([P, 8, m]), pv_[:, :, 0, :]))
                    else:
                        v = V.i(V.at(pt[0], V.last).copy_predicated(
                            dst, mk.unsqueeze(1).to_broadcast([P, 8, nbk, m]), pv_))
                    bank_free[b] = [v]
                if m == 0:
                    v = V.i(V.at(*pt, tot_tok).tensor_tensor(HQ, HQ, TOT, ALU.mult))
                    ready = [v]
                else:
                    nb = 1024 // (2 * m)
                    q3 = HQ.rearrange("p (b w m) -> p b w m", w=2, m=m)
                    k3 = HK.rearrange("p (b w m) -> p b w m", w=2, m=m)
                    t3 = tot[:, 0:2 * nb].rearrange("p (b w) -> p b w", w=2)
                    v1 = V.i(V.at(*pt, tot_tok).tensor_tensor(
                        q3[:, :, 1, :], q3[:, :, 1, :], t3[:, :, 0:1].to_broadcast([P, nb, m]), ALU.mult))
                    v2 = V.i(V.at(*pt, tot_tok).tensor_tensor(
                        k3[:, :, 0, :], k3[:, :, 0, :], t3[:, :, 1:2].to_broadcast([P, nb, m]), ALU.mult))
                    nt = alt[:, 0:nb]
                    tot_tok = V.i(V.at(tot_tok, v2).tensor_tensor(nt, t3[:, :, 0], t3[:, :, 1], ALU.mult))
                    tot, alt = alt, (TOT if alt is TT else TT)
                    ready = [v1, v2]
            q3 = HQ.rearrange("p (h t m) -> p h t m", h=4, t=2)
            k3 = HK.rearrange("p (h t m) -> p h t m", h=4, t=2)
            PE.at(*ready, *bank_free[0])
            for h in range(4):
                last = nc.tensor.matmul(PS[:, 0, h * P:h * P + P], k3[:, h, 0, :], q3[:, h, 1, :], start=True, stop=True)
            tk = PE.i(last)
            yield
            ax = V.i(V.at(tk).tensor_copy(AR[:, 13312:13824], PS[:, 0, :]))
            bank_free[0] = [ax]
            yield
            pv = []
            for t in range(T):
                PE.at(ax, V.last, st["v"], *bank_free[2 + t])
                for h in range(4):
                    o = PS[:, 2 + t, h * P:h * P + P]
                    last = nc.tensor.matmul(o, ATT[:, 2 * h + t, :], VH[:, t, h * P:h * P + P],
                                            start=True, stop=(t == 0))
                    if t == 1:
                        last = nc.tensor.matmul(o, ATX[:, h, :], VH[:, 0, h * P:h * P + P], start=False, stop=True)
                pv.append(PE.i(last))
            yield
            for t in range(T):
                sq = SG[:, 0:512]
                a = S.i(S.at(pv[t], V.last).activation(sq, PS[:, 2 + t, :], ACT.Square))
                r4 = sm[:, 40:44]
                v = V.i(V.at(a, V.last).tensor_reduce(r4, sq.rearrange("p (h m) -> p h m", h=4), AX.X, ALU.add))
                v = V.i(V.at(v).tensor_scalar(r4, r4, 1.0 / P, EPS, ALU.mult, ALU.add))
                a = S.i(S.at(v).activation(r4, r4, ACT.Sqrt))
                v = V.i(V.at(a).reciprocal(r4, r4))
                g3 = GG[:, t, :].rearrange("p (h m) -> p h m", h=4)
                v = V.i(V.at(v, st["g"]).tensor_tensor(g3, g3, r4.unsqueeze(2).to_broadcast([P, 4, P]), ALU.mult))
                v = V.i(V.at(v).tensor_tensor(GG[:, t, :], PS[:, 2 + t, :], GG[:, t, :], ALU.mult))
                bank_free[2 + t] = [v, a]
                yield
            st["done"] = [v, a, pv[1]]

        def softmax_tasks(tasks, SC=SC, PT=PT, nb=2, lc=1, beat=False):
            n = len(tasks)
            st = [dict() for _ in tasks]

            def sA(i):
                q = tasks[i]
                PE.at(*q["ready"](), *bank_free[0], *bank_free[1])
                for o, lh, rh in q["scores"]:
                    last = nc.tensor.matmul(o, lh, rh, start=True, stop=True)
                st[i]["s"] = PE.i(last)

            def sB(i):
                q, b = tasks[i], i % nb
                prev = st[i - nb]["tr"] if i >= nb else None
                s2 = SC[:, b, 0:q["n"]]
                V.at(st[i]["s"], prev, st[i - nb]["e"] if i >= nb else None, *q["scfree"])
                for dst, ps, mk in q["mask"](s2):
                    v = V.i(nc.vector.scalar_tensor_tensor(out=dst, in0=ps, scalar=q["scale"], in1=mk,
                                                           op0=ALU.mult, op1=ALU.add))
                bank_free[0] = bank_free[1] = [v]
                ns = q["nsub"]
                mx = sm[:, 48 + 4 * b:48 + 4 * b + ns]
                v = V.i(V.at(v).tensor_reduce(mx, s2.rearrange("p (a k) -> p a k", a=ns), AX.X, ALU.max))
                v = V.i(V.at(v).tensor_scalar(mx, mx, -1.0, None, ALU.mult))
                w = q["n"] // ns
                for a_ in range(ns):
                    e = S.i(S.at(v, q["denfree"]).activation(s2[:, a_ * w:a_ * w + w], s2[:, a_ * w:a_ * w + w], ACT.Exp,
                                               bias=mx[:, a_:a_ + 1], accum_out=q["den"][:, a_:a_ + 1]))
                st[i]["e"] = e

            def sC(i):
                q, b = tasks[i], i % nb
                nch = q["n"] // P
                PE.at(st[i]["e"])
                st[i]["ev"] = []
                for bb in range(-(-nch // 4)):
                    PE.at(*bank_free[6 + bb])
                    m = min(4, nch - 4 * bb)
                    for c in range(m):
                        last = nc.tensor.transpose(PS[:, 6 + bb, c * P:c * P + P],
                                                   SC[:, b, (4 * bb + c) * P:(4 * bb + c) * P + P], ident)
                    tp = PE.i(last)
                    old = st[i - nb]["pv"] if i >= nb else None
                    dst = PT[:, b, bb * 512:bb * 512 + m * P]
                    if bb == 0:
                        ev = S.i(S.at(tp, old, *q["scfree"]).copy(dst, PS[:, 6, 0:m * P]))
                    else:
                        ev = V.i(V.at(tp, old, *q["scfree"]).tensor_copy(dst, PS[:, 7, 0:m * P]))
                    bank_free[6 + bb] = [ev]
                    st[i]["ev"].append(ev)
                st[i]["tr"] = PE.last

            def sE(i):
                q, b = tasks[i], i % nb
                PE.at(*st[i]["ev"], *bank_free[q["obank"]] if q["ofirst"] else [])
                PE.at(*st[i]["ev"], *q["vready"]())
                for o, chunks in q["pv"]:
                    for j, (c, v) in enumerate(chunks):
                        last = nc.tensor.matmul(o, PT[:, b, c * P:c * P + P], v, start=(j == 0), stop=(j == len(chunks) - 1))
                st[i]["pv"] = PE.i(last)
                if q["after"] is not None:
                    q["after"](st[i]["pv"], st[i]["e"])

            started = 0
            line = [None] * (lc + 1)
            while started < n or any(x is not None for x in line):
                done, turned = line[lc], line[lc - 1]
                line = [None] + line[:lc]
                if done is not None:
                    sE(done)
                if turned is not None and not beat:
                    sC(turned)
                if started < n and tasks[started]["ready"]() is not None:
                    sA(started)
                    sB(started)
                    line[0] = started
                    started += 1
                yield
                if turned is not None and beat:
                    sC(turned)
                    yield
                elif beat:
                    yield

        NLAM = sm[:, 80:82]
        lp = sm[:, 84:88]
        par = {}

        def second_params():
            s_m = sem("ld_m")
            SP.at(PE.last, V.last, S.last)
            nld = 0
            for l in range(2):
                for j, nm in enumerate(("lambda_q1_2", "lambda_k1_2", "lambda_q2_2", "lambda_k2_2")):
                    nc.sync.dma_start(LQ[:, l, j, :], dr[nm][l].partition_broadcast(P)).then_inc(s_m, 16)
                    nld += 16
                nc.sync.dma_start(BF[:, l, :], dr["b_forget_2"][l].partition_broadcast(P)).then_inc(s_m, 16)
                nld += 16
            nc.sync.dma_start(RT[:, :].rearrange("p (c e) -> p c e", c=8),
                              dr["router_2"][0].rearrange("(c p) e -> p c e", p=P)).then_inc(s_m, 16)
            ld_m = par["ld_m"] = ("ld_m", s_m, nld + 16)
            s_rd = sem("ld_rd")
            nc.sync.dma_start(RDA, cf[:, 776:1800]).then_inc(s_rd, 16)
            par["rd"] = ("ld_rd", s_rd, 16)
            for _ in range(8):
                yield
            for l in range(2):
                for j in range(2):
                    v = V.i(V.at(ld_m).tensor_tensor(LQ[:, l, 2 * j, :], LQ[:, l, 2 * j, :], LQ[:, l, 2 * j + 1, :], ALU.mult))
                    v = V.i(V.at(v).tensor_reduce(lp[:, 2 * l + j:2 * l + j + 1], LQ[:, l, 2 * j, :], AX.X, ALU.add))
            a = S.i(S.at(v).activation(lp, lp, ACT.Exp))
            yield
            for l in range(2):
                v = V.i(V.at(a).tensor_scalar(NLAM[:, l:l + 1], lp[:, 2 * l + 1:2 * l + 2], lp[:, 2 * l:2 * l + 1], -LAM_INIT[l],
                                              ALU.subtract, ALU.add))
                v = V.i(V.at(gains["tok"], PE.last).tensor_scalar(gc(("sub", l)), gc(("sub", l)), 1.0 - LAM_INIT[l], None,
                                                                  ALU.mult))
            par["lam"] = v
            ra = S.i(S.at(ld_m).copy(RTH[:, :, :], RT[:, :].rearrange("p (c e) -> p c e", c=8)))
            par["rt"] = V.i(V.at(ra).tensor_tensor(RTL[:, :, :], RT[:, :].rearrange("p (c e) -> p c e", c=8),
                                                   RTH[:, :, :].bitcast(F32), ALU.subtract))

        N = norm_start(("n1", 0), [ld_x], [ld_y])
        ar_free = []
        for l in range(2):
            xt = N
            st = {}
            ztr = [None]
            hg_tmp = []

            def qk1(which, g, tk):
                cp = []
                for t in range(T):
                    a = S.i(S.at(tk[t], ztr[0], V.last if which == 0 and g == 0 else None).mul(
                        ZT[:, t, :], PS[:, 4 + t, :], rs[:, t:t + 1]))
                    bank_free[4 + t] = [a]
                cp.append(a)
                r4 = ZT[:, :, :].rearrange("p t (h d) -> p t h d", h=4)
                p1 = RP[:, :, 0:128].rearrange("p t (h d) -> p t h d", h=4)
                p2 = RP[:, :, 128:256].rearrange("p t (h d) -> p t h d", h=4)
                V.at(a, V.last)
                v = None
                for t in range(T):
                    A = ropeA[:, t, :].unsqueeze(1).to_broadcast([P, 4, 32])
                    B = ropeB[:, t, :].unsqueeze(1).to_broadcast([P, 4, 32])
                    V.i(nc.vector.tensor_tensor(p1[:, t], r4[:, t, :, 0:32], A, ALU.mult))
                    V.i(nc.vector.tensor_tensor(p2[:, t, :, 0:16], r4[:, t, :, 16:32], B[:, :, 0:16], ALU.mult))
                    v = V.i(nc.vector.tensor_tensor(p2[:, t, :, 16:32], r4[:, t, :, 0:16], B[:, :, 16:32], ALU.mult))
                for t in range(T):
                    v = V.i(V.at(v).tensor_tensor(r4[:, t, :, 0:32], p1[:, t], p2[:, t], ALU.add))
                yield
                dst = QT if which == 0 else KT
                tt = turn_heads(lambda t, h: ZT[:, t, h * P:h * P + P], [v, a])
                ztr[0] = tt[-1]
                a = S.i(S.at(tt[0]).copy(dst[:, g, 0:2, :], PS[:, 6, :].rearrange("p (h m) -> p h m", h=2)))
                v = V.i(V.at(tt[1]).tensor_copy(dst[:, g, 2:4, :], PS[:, 7, :].rearrange("p (h m) -> p h m", h=2)))
                bank_free[6], bank_free[7] = [a], [v]
                st[("qk", which, g)] = [a, v]
                yield

            def hq(which, tk):
                for t in range(T):
                    a = S.i(S.at(tk[t], ztr[0], *ar_free, xt["rs"]).mul(ZT[:, t, :], PS[:, 4 + t, :], rs[:, t:t + 1]))
                    bank_free[4 + t] = [a]
                yield
                tt = turn_heads(lambda t, h: ZT[:, t, h * P:h * P + P], [a])
                ztr[0] = tt[-1]
                for b in range(2):
                    sl = slice(b * 512, b * 512 + 512)
                    if which == 0:
                        a = S.i(S.at(tt[b], V.last).activation(SG[:, sl], PS[:, 6 + b, :], ACT.Sigmoid))
                        v = V.i(V.at(a).tensor_tensor(HQ[:, sl], PS[:, 6 + b, :], SG[:, sl], ALU.mult))
                        st["q"] = v
                    else:
                        a = S.i(S.at(tt[b]).activation(TOT[:, sl], PS[:, 6 + b, :], ACT.Sigmoid))
                        a = S.i(S.at(tt[b]).activation(HK[:, sl], PS[:, 6 + b, :], ACT.Sigmoid, scale=-1.0))
                        v = a
                        if l == 1:
                            for h in range(2 * b, 2 * b + 2):
                                hs = slice(h * 256, h * 256 + 256)
                                V.i(V.at(a, gains["lb"]).tensor_scalar(TOT[:, hs], TOT[:, hs], OMB[:, h:h + 1], LB[:, h:h + 1],
                                                                  ALU.mult, ALU.add))
                                v = V.i(V.at(a, gains["lb"]).tensor_scalar(HK[:, hs], HK[:, hs], OMB[:, h:h + 1], None, ALU.mult))
                        st["f"] = v
                    bank_free[6 + b] = [a, v if which == 0 else a]
                st["qk"] = [st["q"], st.get("f")]
                if which == 1:
                    st["at_free"] = ar_free
                    bg.append(hgrn(l, st))
                yield

            def plain(dst, tk, fn, wait=()):
                for t in range(T):
                    a = S.i(S.at(tk[t], *wait).activation(dst(t), PS[:, 4 + t, :], fn, scale=rs[:, t:t + 1]))
                    bank_free[4 + t] = [a]
                return a

            for g in range(17):
                if g == 10:
                    while "done" not in st:
                        tick()
                def early_gg():
                    st["gg"] = half(GG, 0, st["done"], [gc(("hn", l), c) for c in range(4)])

                tk = up(("in1", l, g), 512, xt, mid=early_gg if g == 16 else params if g == 1 and l == 0 else None)
                if g == 1 and l == 0:
                    ar_free = [gains["ci"]]
                if g < 2:
                    bg.append(hq(g, tk))
                elif g == 2:
                    st["v"] = plain(lambda t: VH[:, t, :], tk, ACT.Copy, ar_free)
                elif g == 3:
                    st["g"] = plain(lambda t: GG[:, t, :], tk, ACT.Sigmoid, ar_free)
                elif g < 10:
                    bg.append(qk1((g - 4) // 3, (g - 4) % 3, tk))
                elif g < 13:
                    st["vv"] = plain(lambda t: VV[:, t, g - 10, :], tk, ACT.Copy, st["done"])
                else:
                    dst = XN if g < 15 else ZB
                    o = (g - 13) % 2 * 512
                    st[("z", g)] = plain(lambda t: dst[:, t, o:o + 512], tk, ACT.Copy, st["done"] + [ztr[0]])
                if g == 10 and l == 0:
                    bg.append(params2())
                if g == 12:
                    while bg:
                        tick()
                    fine[0] = True
                    tasks = []
                    rd = [st["vv"]] + [x for w in range(2) for gg in range(3) for x in st[("qk", w, gg)]]
                    for t in range(T):
                        nk = (t + 1) * P
                        for h in range(4):
                            den = sm[:, 64 + 4 * t + h:65 + 4 * t + h]
                            sc, mk = [], []
                            for gg in range(3):
                                if t == 0:
                                    o = PS[:, 0, gg * P:gg * P + P]
                                else:
                                    o = PS[:, gg // 2, (gg % 2) * 256:(gg % 2) * 256 + 256]
                                sc.append((o, QT[:, gg, h, t * P:t * P + P], KT[:, gg, h, 0:nk]))

                            def mask(s2, t=t, nk=nk):
                                if t == 0:
                                    return [(s2, PS[:, 0, 0:384], CB[:, 0:384])]
                                return [(s2[:, 0:512], PS[:, 0, :], CB[:, 384:896]),
                                        (s2[:, 512:768], PS[:, 1, 0:256], CB[:, 896:1152])]

                            chunks = [(gg * (t + 1) + kc, VV[:, kc, gg, h * P:h * P + P])
                                      for gg in range(3) for kc in range(t + 1)]

                            def after(pv, e, t=t, h=h):
                                if h < 3:
                                    return
                                rden = sm[:, 72 + 4 * t:76 + 4 * t]
                                v = V.i(V.at(e, V.last).reciprocal(rden, sm[:, 64 + 4 * t:68 + 4 * t]))
                                v = V.i(V.at(v, pv, *st["done"]).tensor_tensor(
                                    OA[:, t, :].rearrange("p (h m) -> p h m", h=4),
                                    PS[:, 2 + t, :].rearrange("p (h m) -> p h m", h=4),
                                    rden.unsqueeze(2).to_broadcast([P, 4, P]), ALU.mult))
                                bank_free[2 + t] = [v]
                                st["oa"] = v

                            tasks.append(dict(ready=lambda: rd, vready=lambda: [], scores=sc, n=3 * nk, nsub=1, scale=float(P) ** -0.5, mask=mask,
                                              scfree=st["done"] + [ztr[0]], den=den, denfree=V.last, obank=2 + t, ofirst=h == 0,
                                              pv=[(PS[:, 2 + t, h * P:h * P + P], chunks)], after=after))
                    bg.append(softmax_tasks(tasks, beat=True))
                tick()
            drain()
            fine[0] = False
            NG_ = {"r": [st["gg"]]}
            sa = sb_ = None
            for t in range(T):
                sa = S.i(S.at(*[st[("z", g)] for g in range(13, 17)]).activation(XN[:, t, :], XN[:, t, :], ACT.Sigmoid))
            tka = up(("bra", l, 0), 512, NG_, K=512, k0=0)
            tkb = up(("bra", l, 1), 512, NG_, K=512, k0=0, banks=(0, 1))
            NO_ = {"r": [half(OA, 1, [st["oa"]], [None] * 4, s0=0)]}
            for t in range(T):
                sb_ = S.i(S.at().activation(ZB[:, t, :], ZB[:, t, :], ACT.Sigmoid))
            for n, tk, bk in ((0, tka, 4), (1, tkb, 0)):
                for t in range(T):
                    o = XN[:, t, n * 512:n * 512 + 512]
                    v = V.i(V.at(tk[t], sa).tensor_tensor(o, PS[:, bk + t, :], o, ALU.mult))
                    bank_free[bk + t] = [v]
            yh = []
            for n in range(2):
                tk = up(("brb", l, n), 512, NO_, K=512, k0=4, banks=((2, 3), (4, 5))[n])
                for t in range(T):
                    bk = (2, 4)[n] + t
                    o = XN[:, t, n * 512:n * 512 + 512]
                    z = ZB[:, t, n * 512:n * 512 + 512]
                    v = V.i(V.at(tk[t], sb_).tensor_tensor(z, PS[:, bk, :], z, ALU.mult))
                    bank_free[bk] = [v]
                    v = V.i(V.at(v).tensor_tensor(o, o, z, ALU.add))
                yh.append([v])
            NY = whole(XN, yh[0], yh[1], [None] * 8)
            N = out_proj(("out1", l), NY, ("n2", l))
            if l == 0:
                def start(v):
                    return norm_start(("n1", 1), [v])
            else:
                gain1 = load_gain(dr["final_norm_g"], "ld_f1", AR[:, 0:1024])
                bg.append(second_params())

                def start(v):
                    return two_norms(gain1, ("nm", 0), v)

            N, xr = mlp_x(("m1", l), False, 4096, N, start)
            ar_free = [PE.last, xr[1], S.last]

        ar_free = [V.last, S.last, PE.last]

        def a2(o, n):
            return AR[:, o:o + n]

        QAT = a2(0, 1024).rearrange("p (c m) -> p c m", c=4)
        KAT = a2(1024, 1024).rearrange("p (c m) -> p c m", c=4)
        VA = a2(2048, 1024).rearrange("p (t n) -> p t n", t=2)
        QB = a2(3072, 528).rearrange("p (t h d) -> p t h d", t=2, h=4)
        KB = a2(3600, 528).rearrange("p (t h d) -> p t h d", t=2, h=4)
        QBT = a2(4128, 1024).rearrange("p (h m) -> p h m", h=4)
        KBT = a2(5152, 1024).rearrange("p (h m) -> p h m", h=4)
        VB = a2(6176, 512).rearrange("p (t n) -> p t n", t=2)
        QKC = a2(6688, 1024).rearrange("p (c m) -> p c m", c=4)
        VC = a2(7712, 512).rearrange("p (t n) -> p t n", t=2)
        GC = a2(8224, 512).rearrange("p (t n) -> p t n", t=2)
        RA = a2(8736, 1536).rearrange("p (h n) -> p h n", h=4)
        SQ = a2(10272, 512)
        ZT2 = a2(8736, 1024).rearrange("p (t n) -> p t n", t=2)
        R1, R2 = a2(9760, 512), a2(10272, 512)
        SC3 = a2(12288, 2048).rearrange("p (b n) -> p b n", b=4)
        PT3 = a2(14336, 2048).rearrange("p (b n) -> p b n", b=4)
        LF = sm[:, 88:136]
        MIX = XN

        for l in range(2):
            xt = N
            st = {}
            ztr = [None]

            def qk_a(dst, name, tk, rot=False):
                for t in range(T):
                    a = S.i(S.at(tk[t], ztr[0], *ar_free, xt["rs"]).mul(ZT2[:, t, :], PS[:, 4 + t, :], rs[:, t:t + 1]))
                    bank_free[4 + t] = [a]
                    if t == 0:
                        yield
                v = None
                if rot:
                    for t in range(T):
                        r4 = ZT2[:, t, :].rearrange("p (h d) -> p h d", h=8)
                        p1 = R1.rearrange("p (h d) -> p h d", h=8)
                        p2 = R2.rearrange("p (h d) -> p h d", h=8)
                        A = rotA[:, t, :].unsqueeze(1).to_broadcast([P, 8, 64])
                        B = rotB[:, t, :].unsqueeze(1).to_broadcast([P, 8, 64])
                        V.i(V.at(a, V.last).tensor_tensor(p1, r4, A, ALU.mult))
                        V.i(nc.vector.tensor_tensor(p2[:, :, 0:32], r4[:, :, 32:64], B[:, :, 0:32], ALU.mult))
                        v = V.i(nc.vector.tensor_tensor(p2[:, :, 32:64], r4[:, :, 0:32], B[:, :, 32:64], ALU.mult))
                        v = V.i(V.at(v).tensor_tensor(r4, p1, p2, ALU.add))
                yield
                tt = turn_heads(lambda t, h: ZT2[:, t, h * P:h * P + P], [v, a])
                ztr[0] = tt[-1]
                a = S.i(S.at(tt[0]).copy(dst[:, 0:2, :], PS[:, 6, :].rearrange("p (h m) -> p h m", h=2)))
                v = V.i(V.at(tt[1], *ar_free).tensor_copy(dst[:, 2:4, :], PS[:, 7, :].rearrange("p (h m) -> p h m", h=2)))
                bank_free[6], bank_free[7] = [a], [v]
                st[name] = [a, v]
                yield

            def fox_gate(tk):
                a = None
                for t in range(T):
                    a = S.i(S.at(tk[t], *ar_free, xt["rs"]).mul(VB[:, t, :], PS[:, 4 + t, 0:256], rs[:, t:t + 1]))
                    v = V.i(V.at(a, par["ld_m"], xt["rs"], V.last).scalar_tensor_tensor(
                        out=LF[:, 4 * t:4 * t + 4], in0=PS[:, 4 + t, 256:260], scalar=rs[:, t:t + 1], in1=BF[:, l, :],
                        op0=ALU.mult, op1=ALU.add))
                    bank_free[4 + t] = [a, v]
                st["vb"] = a
                x, y, z = LF[:, 0:8], LF[:, 8:16], LF[:, 16:24]
                v = V.i(V.at(v).tensor_scalar(y, x, -1.0, None, ALU.mult))
                v = V.i(V.at(v).tensor_tensor(z, x, y, ALU.max))
                v = V.i(V.at(v).tensor_scalar(y, y, 0.0, None, ALU.max))
                a = S.i(S.at(v).activation(z, z, ACT.Exp, scale=-1.0))
                a = S.i(S.at(a).activation(z, z, ACT.Ln, bias=1.0))
                v = V.i(V.at(a).tensor_tensor(y, y, z, ALU.add))
                v = V.i(V.at(v).tensor_scalar(y, y, -1.0, None, ALU.mult))
                st["lf"] = v
                yield
                PE.at(v, *bank_free[7])
                nc.tensor.matmul(PS[:, 7, 0:4], tri, y[:, 0:4], start=True, stop=True)
                nc.tensor.matmul(PS[:, 7, 8:12], ones, y[:, 0:4], start=True, stop=False)
                c = PE.i(nc.tensor.matmul(PS[:, 7, 8:12], tri, y[:, 4:8], start=False, stop=True))
                for t in range(T):
                    cu = PS[:, 7, 8 * t:8 * t + 4].unsqueeze(2)
                    V.i(V.at(c, *ar_free).tensor_scalar(QB[:, t, :, 64:65], cu, 8.0, None, ALU.mult))
                    V.i(nc.vector.tensor_scalar(KB[:, t, :, 65:66], cu, -8.0, None, ALU.mult))
                    V.i(nc.vector.memset(QB[:, t, :, 65:66], 1.0))
                    v = V.i(nc.vector.memset(KB[:, t, :, 64:65], 1.0))
                bank_free[7] = [v]
                st["cum"] = v
                yield

            def qk_b(tk):
                for t in range(T):
                    a = S.i(S.at(tk[t], *ar_free).mul(QB[:, t, :, 0:64], PS[:, 4 + t, 0:256].rearrange("p (h d) -> p h d", h=4),
                                                      rs[:, t:t + 1]))
                    a = S.i(nc.scalar.mul(KB[:, t, :, 0:64], PS[:, 4 + t, 256:512].rearrange("p (h d) -> p h d", h=4),
                                          rs[:, t:t + 1]))
                    bank_free[4 + t] = [a]
                    yield
                r = []
                for src, dst in ((QB, QBT), (KB, KBT)):
                    tt = turn_heads(lambda t, h: src[:, t, h, :], [a, st["cum"]], wd=66)
                    a2_ = S.i(S.at(tt[0], *ar_free).copy(dst[0:66, 0:2, :], PS[0:66, 6, :].rearrange("p (h m) -> p h m", h=2)))
                    v2_ = V.i(V.at(tt[1], *ar_free).tensor_copy(dst[0:66, 2:4, :], PS[0:66, 7, :].rearrange("p (h m) -> p h m", h=2)))
                    bank_free[6], bank_free[7] = [a2_], [v2_]
                    r += [a2_, v2_]
                    yield
                st["qkb"] = r

            def scored(st):
                return st.get("nscore", 0) == 12

            def soft2(start_free):
                tasks = []

                def rdy_diff():
                    return st["qa"] + st["ka"] if "ka" in st else None

                def rdy_fox():
                    return st["qkb"] if "qkb" in st else None

                for kind, t in (("diff", 0), ("diff", 1), ("fox", 0), ("fox", 1)):
                    nk = (t + 1) * P
                    npr = 4 if kind == "diff" else 2
                    for pr in range(npr):
                        b = len(tasks) % 2
                        dn = len(tasks) % 4
                        den = sm2[:, 2 * dn:2 * dn + 2]
                        rd2 = sm2[:, 8 + 2 * dn:10 + 2 * dn]
                        sc, pv = [], []
                        ob = 2 + b
                        for j in range(2):
                            o = PS[:, j, 0:nk] if kind == "diff" else PS[:, 0, j * nk:j * nk + nk]
                            if kind == "diff":
                                r = slice(64 * j, 64 * j + 64)
                                sc.append((o, QAT[r, pr, t * P:t * P + P], KAT[r, pr, 0:nk]))
                                ch = [(j * (t + 1) + kc, VA[:, kc, pr * P:pr * P + P]) for kc in range(t + 1)]
                                pv.append((PS[:, ob, j * P:j * P + P], ch))
                            else:
                                h = 2 * pr + j
                                sc.append((o, QBT[0:66, h, t * P:t * P + P], KBT[0:66, h, 0:nk]))
                                ch = [(j * (t + 1) + kc, VB[:, kc, h * 64:h * 64 + 64]) for kc in range(t + 1)]
                                pv.append((PS[:, ob, j * 64:j * 64 + 64], ch))

                        def mask(s2, nk=nk, t=t, kind=kind):
                            st["nscore"] = st.get("nscore", 0) + 1
                            if kind == "diff":
                                return [(s2[:, j * nk:j * nk + nk], PS[:, j, 0:nk], mask2[t]) for j in range(2)]
                            m = mask2[t].unsqueeze(1).to_broadcast([P, 2, nk])
                            return [(s2.rearrange("p (a k) -> p a k", a=2),
                                     PS[:, 0, 0:2 * nk].rearrange("p (a k) -> p a k", a=2), m)]

                        def after(pvt, e, t=t, pr=pr, ob=ob, den=den, rd2=rd2, kind=kind, end=pr == npr - 1):
                            v = V.i(V.at(e, V.last).reciprocal(rd2, den))
                            if kind == "diff":
                                v = V.i(V.at(v, par["lam"]).tensor_tensor(rd2[:, 1:2], rd2[:, 1:2], NLAM[:, l:l + 1], ALU.mult))
                                dst = MIX[:, t, pr * P:pr * P + P]
                                v = V.i(V.at(v, pvt).tensor_scalar(dst, PS[:, ob, 0:P], rd2[:, 0:1], None, ALU.mult))
                                v = V.i(V.at(v).scalar_tensor_tensor(out=dst, in0=PS[:, ob, P:2 * P], scalar=rd2[:, 1:2],
                                                                     in1=dst, op0=ALU.mult, op1=ALU.add))
                            else:
                                dst = MIX[:, t, 512 + pr * P:512 + pr * P + P].rearrange("p (a d) -> p a d", a=2)
                                v = V.i(V.at(v, pvt).tensor_tensor(
                                    dst, PS[:, ob, 0:P].rearrange("p (a d) -> p a d", a=2),
                                    rd2.unsqueeze(2).to_broadcast([P, 2, 64]), ALU.mult))
                            bank_free[ob] = [v]
                            if end:
                                st[(kind, t)] = v
                                if kind == "diff":
                                    bg.append(diff_norm(t))

                        tasks.append(dict(ready=rdy_diff if kind == "diff" else rdy_fox,
                                          vready=(lambda: [st["va"]]) if kind == "diff" else (lambda: [st["vb"]]), scores=sc, n=2 * nk, nsub=2, scale=0.125, mask=mask,
                                          scfree=start_free, den=den, denfree=V.last, obank=ob, ofirst=True, pv=pv, after=after))
                return softmax_tasks(tasks, SC3, PT3, 4, 3)

            def diff_norm(t):
                m = MIX[:, t, 0:512]
                a = S.i(S.at(st[("diff", t)], V.last).activation(SQ, m, ACT.Square))
                r4 = sm[:, 40:44]
                v = V.i(V.at(a).tensor_reduce(r4, SQ.rearrange("p (h m) -> p h m", h=4), AX.X, ALU.add))
                v = V.i(V.at(v).tensor_scalar(r4, r4, 1.0 / P, EPS, ALU.mult, ALU.add))
                a = S.i(S.at(v).activation(r4, r4, ACT.Sqrt))
                v = V.i(V.at(a).reciprocal(r4, r4))
                m3 = m.rearrange("p (h m) -> p h m", h=4)
                v = V.i(V.at(v).tensor_tensor(m3, m3, r4.unsqueeze(2).to_broadcast([P, 4, P]), ALU.mult))
                st[("dn", t)] = v
                yield

            def retention():
                for h in range(4):
                    b = h % 2
                    r = slice(64 * (h % 2), 64 * (h % 2) + 64)
                    c = h // 2
                    PE.at(*st["qkc"], *bank_free[b])
                    nc.tensor.matmul(PS[:, b, 0:256], QKC[r, 2 + c, 0:128], QKC[r, c, 0:256], start=True, stop=True)
                    tk = PE.i(nc.tensor.matmul(PS[:, b, 256:384], QKC[r, 2 + c, 128:256], QKC[r, c, 128:256], start=True, stop=True))
                    V.i(V.at(tk, par["rd"], *ar_free).tensor_tensor(RA[:, h, 0:256], PS[:, b, 0:256], RD[:, h, :], ALU.mult))
                    v = V.i(nc.vector.tensor_tensor(RA[:, h, 256:384], PS[:, b, 256:384], RD[:, h, 0:128], ALU.mult))
                    bank_free[b] = [v]
                yield
                pv = []
                for t in range(T):
                    PE.at(v, st["vgc"], *bank_free[t])
                    for h in range(4):
                        o = PS[:, t, h * 64:h * 64 + 64]
                        last = nc.tensor.matmul(o, RA[:, h, t * P:t * P + P], VC[:, 0, h * 64:h * 64 + 64], start=True, stop=t == 0)
                        if t:
                            last = nc.tensor.matmul(o, RA[:, h, 256:384], VC[:, 1, h * 64:h * 64 + 64], start=False, stop=True)
                    pv.append(PE.i(last))
                yield
                o3 = PS[:, 0:2, 0:256].rearrange("p t (h d) -> p t h d", h=4)
                m3 = MIX[:, :, 768:1024].rearrange("p t (h d) -> p t h d", h=4)
                q3 = SQ.rearrange("p (t h d) -> p t h d", t=2, h=4)
                r8 = sm[:, 200:208].rearrange("p (t h) -> p t h", t=2)
                rb = r8.unsqueeze(3).to_broadcast([P, T, 4, 64])
                v = V.i(V.at(*pv, V.last).tensor_reduce(r8, o3, AX.X, ALU.add))
                v = V.i(V.at(v).tensor_scalar(r8, r8, 1.0 / 64, None, ALU.mult))
                v = V.i(V.at(v).tensor_tensor(m3, o3, rb, ALU.subtract))
                bank_free[0] = bank_free[1] = [v]
                a = S.i(S.at(v).activation(q3, m3, ACT.Square))
                v = V.i(V.at(a, V.last).tensor_reduce(r8, q3, AX.X, ALU.add))
                v = V.i(V.at(v).tensor_scalar(r8, r8, 1.0 / 64, EPS, ALU.mult, ALU.add))
                a = S.i(S.at(v).activation(r8, r8, ACT.Sqrt))
                v = V.i(V.at(a).reciprocal(r8, r8))
                yield
                v = V.i(V.at(v).tensor_tensor(m3, m3, rb, ALU.mult))
                v = V.i(V.at(v, st["vgc"]).tensor_tensor(MIX[:, :, 768:1024], MIX[:, :, 768:1024], GC[:, :, :], ALU.mult))
                st["ret"] = v

            early = []

            def begin(fn, *args, **kw):
                def hook(toks):
                    early.append(fn(*args, toks, **kw))
                    next(early[-1])
                return hook

            up(("in2", l, "qa"), 512, xt, hook=begin(qk_a, QAT, "qa"))
            bg.insert(0, early.pop())
            tick()
            tk = up(("in2", l, "vf"), 260, xt)
            bg.insert(0, fox_gate(tk))
            tick()
            up(("in2", l, "ka"), 512, xt, hook=begin(qk_a, KAT, "ka"))
            bg.append(soft2(ar_free))
            bg.insert(0, early.pop())
            tick()
            fine[0] = True
            def put_va(t, tok):
                st["va"] = a = S.i(S.at(tok, *ar_free).mul(VA[:, t, :], PS[:, 4 + t, :], rs[:, t:t + 1]))
                bank_free[4 + t] = [a]

            tk = up(("in2", l, "va"), 512, xt, hook=lambda toks: put_va(0, toks[0]))
            put_va(1, tk[1])
            tick()
            up(("in2", l, "qkb"), 512, xt, hook=begin(qk_b))
            bg.insert(0, early.pop())
            tick()
            up(("in2", l, "qkc"), 512, xt, hook=begin(qk_a, QKC, "qkc", rot=True))
            bg.insert(0, early.pop())
            tick()
            def put_vgc(t, tok):
                S.i(S.at(tok, *ar_free).mul(VC[:, t, :], PS[:, 4 + t, 0:256], rs[:, t:t + 1]))
                a = S.i(nc.scalar.activation(GC[:, t, :], PS[:, 4 + t, 256:512], ACT.Silu, scale=rs[:, t:t + 1]))
                bank_free[4 + t] = [a]
                st["vgc" if t else "vgc0"] = a

            tk = up(("in2", l, "vgc"), 512, xt, hook=lambda toks: put_vgc(0, toks[0]))
            put_vgc(1, tk[1])
            tick()
            while ("dn", 1) not in st or not scored(st):
                tick()
            fine[0] = False
            bg.append(retention())
            h0 = half(MIX, 0, [st[("dn", 0)], st[("dn", 1)]], [gc(("sub", l))] * 4)
            for n in range(2):
                bk = (4, 2)[n]
                PE.at(*h0)
                while n and ("fox", 1) not in st:
                    tick()
                wh, wl = take((("out2", l, n), 0))
                for t in range(T):
                    PE.at(*bank_free[bk + t])
                    for k in range(4):
                        if k == 2:
                            second()
                        last = mm3(PS[:, bk + t, :], XTH[:, k, t * P:t * P + P], XTL[:, k, t * P:t * P + P],
                                   wh[:, k, :], wl[:, k, :], k == 0, False)
                    if t == 0:
                        tick()
                pe_done.append(PE.i(last))
                tick()
            drain()
            if l == 1:
                lend([PE.last, V.last, S.last])
            h1 = half(MIX, 1, ([st[("fox", 1)]], [st["ret"]]), [None, None, gc(("rg", l), 0), gc(("rg", l), 1)])
            xr = []
            for n in range(2):
                bk = (4, 2)[n]
                wh, wl = take((("out2", l, n), 1))
                for t in range(T):
                    for k in range(4):
                        if k == 2:
                            second()
                        PE.at(*h1[2 * (k // 2):2 * (k // 2) + 2])
                        last = mm3(PS[:, bk + t, :], XTH[:, 4 + k, t * P:t * P + P], XTL[:, 4 + k, t * P:t * P + P],
                                   wh[:, k, :], wl[:, k, :], False, k == 3)
                    tk = PE.i(last)
                    if (n, t) == (1, 0):
                        N = norm_start(("nf", l), [xr[0]])
                    v = V.i(V.at(tk).tensor_tensor(X[:, t, n * 512:n * 512 + 512], PS[:, bk + t, :],
                                                   X[:, t, n * 512:n * 512 + 512], ALU.add))
                    bank_free[bk + t] = [v]
                pe_done.append(tk)
                xr.append(v)
            N["x1"] = [xr[1]]
            PP = AR[:, 14848:15360].rearrange("p (t n) -> p t n", t=2)
            SGT = AR[:, 2560:4608].rearrange("p (t n) -> p t n", t=2)
            s_p = sem(f"ld_p{l}")
            SP.at(PE.last, V.last, S.last)
            nc.sync.dma_start(PP, dr["p_2"][l, 0].rearrange("(t p) n -> p t n", p=P)).then_inc(s_p, 16)
            box = {}

            def ple_turn():
                for _ in range(6):
                    yield
                box["pt"] = half(PP, 0, [(f"ld_p{l}", s_p, 16)], [None] * 2, dst=(PTH, PTL), nch=2)

            bg.append(ple_turn())
            if l == 0:
                _, xr = mlp_x(("m2", 0), True, FF2, N, None)
            else:
                xr = moe(N) * 2
            if l == 1:
                gain2 = load_gain(dr["final_norm_2"], "ld_f2", AR[:, 8192:9216])
            N = norm_start(("pn", l), [xr[0]], [xr[1]])
            d = down(("pp", l), 256, PTH, PTL, box["pt"], True, True)
            v_free, xt_ready = V.last, [None, None]
            for n in range(2):
                tk = up(("pg", l, n), 512, N, mid=(lambda: box.update(n=norm_start(("nm", 1), [box["v"]]))) if n and l == 0 else None)
                for t in range(T):
                    sg = SGT[:, t, n * 512:n * 512 + 512]
                    xo = X[:, t, n * 512:n * 512 + 512]
                    a = S.i(S.at(tk[t], N["rs"], v_free).activation(sg, PS[:, 4 + t, :], ACT.Sigmoid, scale=rs[:, t:t + 1]))
                    bank_free[4 + t] = [a]
                    v = V.i(V.at(a, d[1]).tensor_tensor(sg, PS[:, 2 * t + n, :], sg, ALU.mult))
                    bank_free[2 * t + n] = [v]
                    v = V.i(V.at(v).tensor_tensor(xo, xo, sg, ALU.add))
                    xt_ready[t] = v
                box = {"v": v} if n == 0 else box
            if l == 0:
                N = box["n"]
                N["x1"] = [v]
            xr = [v]
            ar_free = [PE.last, v, S.last]

        v = last_norm(gain2, XN, ([xt_ready[0]], [xt_ready[1]]))
        s_o = sem("s_out")
        for t in range(T):
            SP.at(v[t])
            nc.sync.dma_start(out[0, t * P:t * P + P, :], XN[:, t, :]).then_inc(s_o, 16)
        nc.sync.wait_ge(s_o, 32)


def constants():
    i = np.arange(128)
    cf = np.zeros((128, 1928), np.float32)
    cf[:, 0:128] = np.eye(128)
    cf[:, 128:256] = i[:, None] <= i[None, :]
    cf[:, 256:384] = 1.0
    pos = np.arange(256, dtype=np.float32)
    f1 = (np.float32(500000.0) ** (-np.arange(0, 32, 2, dtype=np.float32) / np.float32(32))).astype(np.float32)
    a1 = (pos[:, None] * f1[None, :]).astype(np.float32).astype(np.float64)
    f2 = (np.float32(10000.0) ** (-np.arange(32, dtype=np.float32) / np.float32(32))).astype(np.float32)
    a2 = (pos[:, None] * f2[None, :]).astype(np.float32).astype(np.float64)
    for o, w, ang in ((384, 32, a1), (512, 64, a2)):
        A = np.concatenate([np.cos(ang), np.cos(ang)], 1).astype(np.float32).reshape(2, 128, w)
        B = np.concatenate([-np.sin(ang), np.sin(ang)], 1).astype(np.float32).reshape(2, 128, w)
        cf[:, o:o + 2 * w] = A.transpose(1, 0, 2).reshape(128, 2 * w)
        cf[:, o + 2 * w:o + 4 * w] = B.transpose(1, 0, 2).reshape(128, 2 * w)
    cf[:, 1800:1928] = np.arange(128)
    lg = np.log1p(-np.exp2(-5.0 - np.arange(4)))
    d = np.arange(256)[None, :] - i[:, None]
    for h in range(4):
        cf[:, 776 + 256 * h:776 + 256 * h + 256] = np.where(d >= 0, np.exp(np.maximum(d, 0) * lg[h]), 0.0) * 0.125
    neg = -1e30
    cb = np.zeros((128, 1408), np.float32)
    for t in range(2):
        q = t * 128 + i[:, None]
        k = np.arange((t + 1) * 128)[None, :]
        for g, (w, dil) in enumerate(((128, 1), (512, 4), (2048, 16))):
            ok = (k <= q) & (q - k <= w) & ((q - k) % dil == 0)
            o = g * 128 if t == 0 else 384 + g * 256
            cb[:, o:o + (t + 1) * 128] = np.where(ok, 0.0, neg)
    cb[:, 1152:1408] = np.where(np.arange(256)[None, :] <= 128 + i[:, None], 0.0, neg)
    ci = np.zeros((128, 1024), np.float32)
    s, t = i[:, None], i[None, :]
    for li, m in enumerate(LEVELS):
        if m == 0:
            ok = s == t
        else:
            ok = (s // (2 * m) == t // (2 * m)) & ((s // m) % 2 == 0) & ((t // m) % 2 == 1)
        ci[:, li * 128:li * 128 + 128] = ok
    return cf, cb, ci


_INS = ["x", "norm1_g", "w_in", "hg_lower_bounds", "hg_norm_g", "w_branch_a", "w_branch_b", "w_out", "norm2_g", "w_up",
        "w_down", "final_norm_g", "p_2", "norm_mix_2", "w_in_2", "b_forget_2", "lambda_q1_2", "lambda_k1_2",
        "lambda_q2_2", "lambda_k2_2", "diff_subln_2", "ret_gn_2", "w_out_2", "norm_ffn_2", "dense_w_gate_2",
        "dense_w_up_2", "dense_w_down_2", "router_2", "moe_w_gate_2", "moe_w_up_2", "moe_w_down_2", "ple_norm_2",
        "ple_gate_2", "ple_proj_2", "final_norm_2"]


def kernel(**inputs):
    from concourse import bacc as _bacc
    from concourse.bass_utils import run_bass_kernel_spmd as _run

    nc = _bacc.Bacc("TRN2", target_bir_lowering=False, num_devices=1)
    arrays, dr = {}, {}
    for name in _INS:
        a = np.ascontiguousarray(inputs[name])
        arrays[f"in_{name}"] = a
        dr[name] = nc.dram_tensor(f"in_{name}", a.shape, mybir.dt.from_np(a.dtype), kind="ExternalInput").ap()
    cs = []
    for name, a in zip(("cf", "cb", "ci"), constants()):
        arrays[f"const_{name}"] = a
        cs.append(nc.dram_tensor(f"const_{name}", a.shape, mybir.dt.from_np(a.dtype), kind="ExternalInput").ap())
    o = nc.dram_tensor("out_0", (1, 256, 1024), F32, kind="ExternalOutput").ap()
    program(nc, dr, cs[0], cs[1], cs[2], o)
    r = _run(nc, [arrays], core_ids=[0])
    return r.results[0]["out_0"]
```
